# Optimizing a Trainium2 kernel written in Bass

```python
import math
import jax
import jax.numpy as jnp
from jax import lax
import numpy as np

D_MODEL = 1024
BATCH = 1
SEQ = 512
DEPTH = 2

NORM_EPS = 1e-6
N_BUCKETS = 32
MAX_DISTANCE = 128
N_ATTN_HEADS = 8

SSM_HEADS = 8
SSM_HEAD_DIM = 64
SSM_D_INNER = SSM_HEADS * SSM_HEAD_DIM
SSM_GROUPS = 2
SSM_STATE = 128
SSM_CONV = 4
SSM_CHUNK = 128
SSM_CONV_CH = SSM_D_INNER + 2 * SSM_GROUPS * SSM_STATE

DSA_HEADS = N_ATTN_HEADS
DSA_HEAD_DIM = 64
IDX_HEADS = 4
IDX_DIM = 64
DSA_TOPK = 256
DSA_Q_BLOCK = 128

EVEN_SPLITS = (SSM_D_INNER, SSM_CONV_CH, SSM_HEADS, DSA_HEADS * DSA_HEAD_DIM, DSA_HEAD_DIM, DSA_HEAD_DIM, IDX_HEADS * IDX_DIM, IDX_DIM, IDX_HEADS)
EVEN_COLS = sum(EVEN_SPLITS)
EVEN_MIX = SSM_D_INNER + DSA_HEADS * DSA_HEAD_DIM

NSA_HEADS = N_ATTN_HEADS
NSA_KV_GROUPS = 2
NSA_HEAD_DIM = 128
NSA_KV_DIM = NSA_KV_GROUPS * NSA_HEAD_DIM
CMP_BLOCK = 32
CMP_STRIDE = 16
SEL_BLOCK = 64
SEL_TOPN = 16
WINDOW = 512
NSA_Q_BLOCK = 32
ODD_SPLITS = (NSA_HEADS * NSA_HEAD_DIM,) + (NSA_KV_DIM,) * 6 + (3 * NSA_HEADS,)
ODD_COLS = sum(ODD_SPLITS)
ODD_MIX = NSA_HEADS * NSA_HEAD_DIM

MOE_GROUPS = 4
EXPERTS_PER_GROUP = 8
N_EXPERTS = MOE_GROUPS * EXPERTS_PER_GROUP
EXPERT_FF = 512
TOP_K_INNER = 2
MOE_BLOCK = 256

N_EVEN = (DEPTH + 1) // 2
N_ODD = DEPTH // 2

kernel_name = 'hybrid_ssd_dsa_nsa_hmoe'

def rms_norm(x, gain):
    xf = x.astype(jnp.float32)
    y = xf * lax.rsqrt(jnp.mean(xf * xf, axis=-1, keepdims=True) + NORM_EPS)
    return (y * gain.astype(jnp.float32)).astype(x.dtype)

def split_cols(u, sizes):
    out, start = [], 0
    for s in sizes:
        out.append(u[..., start:start + s])
        start += s
    return out

def t5_bucket(dist):
    dist = jnp.maximum(dist, 0)
    max_exact = N_BUCKETS // 2
    large = max_exact + (jnp.log(jnp.maximum(dist, 1).astype(jnp.float32) / max_exact)
                         / math.log(MAX_DISTANCE / max_exact) * (N_BUCKETS - max_exact)).astype(jnp.int32)
    large = jnp.minimum(large, N_BUCKETS - 1)
    return jnp.where(dist < max_exact, dist, large)

def masked_softmax(logits, mask):
    l = jnp.where(mask, logits.astype(jnp.float32), -jnp.inf)
    m = jnp.max(l, axis=-1, keepdims=True)
    m = jnp.where(jnp.isfinite(m), m, 0.0)
    e = jnp.where(mask, jnp.exp(l - m), 0.0)
    return e / jnp.maximum(jnp.sum(e, axis=-1, keepdims=True), 1e-30)

def causal_dwconv(x, w, b):
    ch = x.shape[-1]
    y = lax.conv_general_dilated(x, w[:, None, :].astype(x.dtype), window_strides=(1,),
                                 padding=[(SSM_CONV - 1, 0)], dimension_numbers=('NWC', 'WIO', 'NWC'),
                                 feature_group_count=ch)
    return y + b.astype(x.dtype)

def ssd_chunked(xh, dt, a, bm, cm):
    bsz, seq, n_heads, hd = xh.shape
    g, n = bm.shape[2], bm.shape[3]
    hpg = n_heads // g
    l = SSM_CHUNK
    nc = seq // l
    x = (xh * dt[..., None]).reshape(bsz, nc, l, g, hpg, hd)
    acum = jnp.cumsum((dt * a).reshape(bsz, nc, l, g, hpg), axis=2)
    bm = bm.reshape(bsz, nc, l, g, n)
    cm = cm.reshape(bsz, nc, l, g, n)
    causal = jnp.tril(jnp.ones((l, l), dtype=bool))[:, :, None, None]
    seg = acum[:, :, :, None] - acum[:, :, None]
    decay = jnp.exp(jnp.where(causal, seg, -jnp.inf))
    cb = jnp.einsum('bctgn,bcsgn->bctsg', cm, bm)
    y_diag = jnp.einsum('bctsgh,bcsghp->bctghp', cb[..., None] * decay, x)
    to_end = jnp.exp(acum[:, :, -1:] - acum)
    chunk_states = jnp.einsum('bclgn,bclghp->bcghpn', bm, x * to_end[..., None])
    chunk_decay = jnp.exp(acum[:, :, -1])

    def step(state, inp):
        st, dc, c_c, a_c = inp
        y_off = jnp.einsum('blgn,bghpn->blghp', c_c, state) * jnp.exp(a_c)[..., None]
        return state * dc[..., None, None] + st, y_off

    init = jnp.zeros((bsz, g, hpg, hd, n), jnp.float32)
    mv = lambda t: jnp.moveaxis(t, 1, 0)
    _, y_off = lax.scan(step, init, (mv(chunk_states), mv(chunk_decay), mv(cm), mv(acum)))
    return (y_diag + jnp.moveaxis(y_off, 0, 1)).reshape(bsz, seq, n_heads, hd)

def mamba2_mixer(z, xbc, dt_raw, conv_w, conv_b, dt_bias, a_log, d_skip, norm_g):
    f32 = jnp.float32
    bsz, seq, _ = z.shape
    xbc = jax.nn.silu(causal_dwconv(xbc, conv_w, conv_b))
    xs, bm, cm = split_cols(xbc, (SSM_D_INNER, SSM_GROUPS * SSM_STATE, SSM_GROUPS * SSM_STATE))
    xh = xs.reshape(bsz, seq, SSM_HEADS, SSM_HEAD_DIM).astype(f32)
    dt = jax.nn.softplus(dt_raw.astype(f32) + dt_bias.astype(f32))
    a = -jnp.exp(a_log.astype(f32))
    y = ssd_chunked(xh, dt, a, bm.reshape(bsz, seq, SSM_GROUPS, SSM_STATE).astype(f32),
                    cm.reshape(bsz, seq, SSM_GROUPS, SSM_STATE).astype(f32))
    y = y + d_skip.astype(f32)[:, None] * xh
    y = y.reshape(bsz, seq, SSM_GROUPS, -1) * jax.nn.silu(z.astype(f32)).reshape(bsz, seq, SSM_GROUPS, -1)
    y = y * lax.rsqrt(jnp.mean(y * y, axis=-1, keepdims=True) + NORM_EPS)
    return (y.reshape(bsz, seq, SSM_D_INNER) * norm_g.astype(f32)).astype(z.dtype)

def dsa_attention(q, k, v, iq, ik, iw, rel_bias):
    f32 = jnp.float32
    bsz, seq, n_heads, hd = q.shape
    top_k = min(DSA_TOPK, seq // 4)
    scale = hd ** -0.5
    idx_scale = (IDX_DIM * IDX_HEADS) ** -0.5
    key_pos = jnp.arange(seq)
    gather = jax.vmap(lambda kk, ii: kk[ii])

    def block(q0):
        t = q0 + jnp.arange(DSA_Q_BLOCK)
        qb = lax.dynamic_slice_in_dim(q, q0, DSA_Q_BLOCK, axis=1)
        iqb = lax.dynamic_slice_in_dim(iq, q0, DSA_Q_BLOCK, axis=1)
        iwb = lax.dynamic_slice_in_dim(iw, q0, DSA_Q_BLOCK, axis=1)
        rel = jax.nn.relu(jnp.einsum('bqhd,bsd->bqhs', iqb, ik).astype(f32))
        score = jnp.einsum('bqhs,bqh->bqs', rel, iwb.astype(f32)) * idx_scale
        score = jnp.where((key_pos[None, :] <= t[:, None])[None], score, -jnp.inf)
        _, sel = lax.top_k(score, top_k)
        k_sel = gather(k, sel)
        v_sel = gather(v, sel)
        dist = t[None, :, None] - sel
        logits = jnp.einsum('bqhd,bqkd->bqhk', qb, k_sel).astype(f32) * scale
        logits = logits + jnp.moveaxis(rel_bias[t5_bucket(dist)], -1, 2).astype(f32)
        p = masked_softmax(logits, (dist >= 0)[:, :, None, :])
        return jnp.einsum('bqhk,bqkd->bqhd', p.astype(v.dtype), v_sel)

    out = lax.map(block, jnp.arange(seq // DSA_Q_BLOCK) * DSA_Q_BLOCK)
    return jnp.moveaxis(out, 0, 1).reshape(bsz, seq, n_heads * hd)

def compress_blocks(kv, pos_emb, w1, w2):
    bsz, seq, g, hd = kv.shape
    nc = (seq - CMP_BLOCK) // CMP_STRIDE + 1
    idx = np.arange(nc)[:, None] * CMP_STRIDE + np.arange(CMP_BLOCK)[None, :]
    blk = kv[:, idx] + pos_emb[:, None, :].astype(kv.dtype)
    blk = jnp.moveaxis(blk, 2, 3).reshape(bsz, nc, g, CMP_BLOCK * hd)
    return jax.nn.silu(blk @ w1) @ w2

def nsa_attention(q, kc, vc, ks, vs, kw, vw, gates, rel_bias):
    f32 = jnp.float32
    bsz, seq, n_heads, hd = q.shape
    g = NSA_KV_GROUPS
    hpg = n_heads // g
    nc = kc.shape[1]
    nsel = seq // SEL_BLOCK
    n_top = min(SEL_TOPN, nsel)
    scale = hd ** -0.5
    cmp_start = jnp.arange(nc) * CMP_STRIDE
    cmp_end = cmp_start + CMP_BLOCK - 1
    sel_start = jnp.arange(nsel) * SEL_BLOCK
    overlap = ((cmp_start[:, None] < sel_start[None, :] + SEL_BLOCK)
               & (cmp_end[:, None] >= sel_start[None, :])).astype(f32)
    ks_blk = jnp.moveaxis(ks.reshape(bsz, nsel, SEL_BLOCK, g, hd), 3, 1)
    vs_blk = jnp.moveaxis(vs.reshape(bsz, nsel, SEL_BLOCK, g, hd), 3, 1)
    kw_pad = jnp.concatenate([jnp.zeros((bsz, WINDOW, g, hd), kw.dtype), kw], axis=1)
    vw_pad = jnp.concatenate([jnp.zeros((bsz, WINDOW, g, hd), vw.dtype), vw], axis=1)
    bias_g = rel_bias.reshape(N_BUCKETS, g, hpg)
    qg = q.reshape(bsz, seq, g, hpg, hd)
    gg = gates.reshape(bsz, seq, 3, g, hpg)
    gather = jax.vmap(jax.vmap(lambda kk, ii: kk[ii]))
    bias_per_group = jax.vmap(lambda bk, tb: tb[bk], in_axes=(1, 1), out_axes=1)
    j = jnp.arange(nsel)

    def block(q0):
        t = q0 + jnp.arange(NSA_Q_BLOCK)
        qb = lax.dynamic_slice_in_dim(qg, q0, NSA_Q_BLOCK, axis=1)
        gb = lax.dynamic_slice_in_dim(gg, q0, NSA_Q_BLOCK, axis=1)[..., None]
        dist_c = t[:, None] - cmp_end[None, :]
        lc = jnp.einsum('bqghd,bcgd->bqghc', qb, kc).astype(f32) * scale
        lc = lc + bias_g[t5_bucket(dist_c)].transpose(0, 2, 3, 1).astype(f32)
        p_c = masked_softmax(lc, (dist_c >= 0)[:, None, None, :])
        o_c = jnp.einsum('bqghc,bcgd->bqghd', p_c.astype(vc.dtype), vc)
        imp = jnp.einsum('bqghc,cn->bqgn', p_c, overlap)
        cur = t // SEL_BLOCK
        forced = (j[None] == 0) | (j[None] == cur[:, None]) | (j[None] == cur[:, None] - 1)
        imp = jnp.where(forced[:, None, :], jnp.inf, imp)
        imp = jnp.where((sel_start[None, :] <= t[:, None])[:, None, :], imp, -jnp.inf)
        _, top_blk = lax.top_k(imp, n_top)
        sel_idx = jnp.moveaxis(top_blk, 2, 1)
        n_keys = n_top * SEL_BLOCK
        k_sel = gather(ks_blk, sel_idx).reshape(bsz, g, NSA_Q_BLOCK, n_keys, hd)
        v_sel = gather(vs_blk, sel_idx).reshape(bsz, g, NSA_Q_BLOCK, n_keys, hd)
        s_pos = (sel_idx[..., None] * SEL_BLOCK + jnp.arange(SEL_BLOCK)).reshape(bsz, g, NSA_Q_BLOCK, n_keys)
        dist_s = t[None, None, :, None] - s_pos
        bias_s = bias_per_group(t5_bucket(dist_s), bias_g)
        ls = jnp.einsum('bqghd,bgqkd->bgqhk', qb, k_sel).astype(f32) * scale
        ls = ls + jnp.moveaxis(bias_s, -1, 3).astype(f32)
        p_s = masked_softmax(ls, (dist_s >= 0)[:, :, :, None, :])
        o_s = jnp.einsum('bgqhk,bgqkd->bqghd', p_s.astype(v_sel.dtype), v_sel)
        kwb = lax.dynamic_slice_in_dim(kw_pad, q0, WINDOW + NSA_Q_BLOCK, axis=1)
        vwb = lax.dynamic_slice_in_dim(vw_pad, q0, WINDOW + NSA_Q_BLOCK, axis=1)
        w_pos = q0 - WINDOW + jnp.arange(WINDOW + NSA_Q_BLOCK)
        dist_w = t[:, None] - w_pos[None, :]
        mask_w = (dist_w >= 0) & (dist_w < WINDOW) & (w_pos[None, :] >= 0)
        lw = jnp.einsum('bqghd,bkgd->bqghk', qb, kwb).astype(f32) * scale
        lw = lw + bias_g[t5_bucket(dist_w)].transpose(0, 2, 3, 1).astype(f32)
        p_w = masked_softmax(lw, mask_w[:, None, None, :])
        o_w = jnp.einsum('bqghk,bkgd->bqghd', p_w.astype(vwb.dtype), vwb)
        return gb[:, :, 0] * o_c + gb[:, :, 1] * o_s + gb[:, :, 2] * o_w

    out = lax.map(block, jnp.arange(seq // NSA_Q_BLOCK) * NSA_Q_BLOCK)
    return jnp.moveaxis(out, 0, 1).reshape(bsz, seq, n_heads * hd)

def even_mixer(h, rel_bias, w_in, conv_w, conv_b, dt_bias, a_log, d_skip, ssm_norm, q_norm, k_norm, w_out):
    bsz, seq, _ = h.shape
    u = h @ w_in
    z, xbc, dt_raw, q, k, v, iq, ik, iw = split_cols(u, EVEN_SPLITS)
    y_ssm = mamba2_mixer(z, xbc, dt_raw, conv_w, conv_b, dt_bias, a_log, d_skip, ssm_norm)
    q = rms_norm(q.reshape(bsz, seq, DSA_HEADS, DSA_HEAD_DIM), q_norm)
    k = rms_norm(k, k_norm)
    y_att = dsa_attention(q, k, v, iq.reshape(bsz, seq, IDX_HEADS, IDX_DIM), ik, iw, rel_bias)
    return jnp.concatenate([y_ssm.astype(h.dtype), y_att.astype(h.dtype)], axis=-1) @ w_out

def odd_mixer(h, rel_bias, w_in, q_norm, kc_norm, ks_norm, kw_norm, pos_k, pos_v, ck_w1, ck_w2, cv_w1, cv_w2, w_out):
    bsz, seq, _ = h.shape
    u = h @ w_in
    q, kc, vc, ks, vs, kw, vw, gl = split_cols(u, ODD_SPLITS)
    grp = lambda a: a.reshape(bsz, seq, NSA_KV_GROUPS, NSA_HEAD_DIM)
    q = rms_norm(q.reshape(bsz, seq, NSA_HEADS, NSA_HEAD_DIM), q_norm)
    kc = rms_norm(compress_blocks(grp(kc), pos_k, ck_w1, ck_w2), kc_norm)
    vc = compress_blocks(grp(vc), pos_v, cv_w1, cv_w2)
    ks = rms_norm(grp(ks), ks_norm)
    kw = rms_norm(grp(kw), kw_norm)
    gates = jax.nn.sigmoid(gl.reshape(bsz, seq, 3, NSA_HEADS))
    o = nsa_attention(q, kc, vc, ks, grp(vs), kw, grp(vw), gates, rel_bias)
    return o.astype(h.dtype) @ w_out

def hier_moe(x, w_group, w_router, w_gate, w_up, w_down):
    f32 = jnp.float32
    bsz, seq, dm = x.shape
    xt = x.reshape(-1, dm)
    n_tok = xt.shape[0]
    g_logits = (xt @ w_group).astype(f32)
    g_sel = jnp.argmax(g_logits, axis=-1)
    g_w = jnp.take_along_axis(jax.nn.softmax(g_logits, axis=-1), g_sel[:, None], axis=-1)
    e_logits = jnp.einsum('nd,gde->nge', xt, w_router).astype(f32)
    e_logits = jnp.take_along_axis(e_logits, g_sel[:, None, None], axis=1)[:, 0]
    e_top, e_idx = lax.top_k(e_logits, TOP_K_INNER)
    e_w = jax.nn.softmax(e_top, axis=-1) * g_w
    expert_id = (g_sel[:, None] * EXPERTS_PER_GROUP + e_idx).reshape(-1)
    token_id = jnp.repeat(jnp.arange(n_tok), TOP_K_INNER)
    weight = e_w.reshape(-1)
    n_assign = n_tok * TOP_K_INNER
    order = jnp.argsort(expert_id)
    se = expert_id[order]
    counts = jnp.zeros(N_EXPERTS, jnp.int32).at[expert_id].add(1)
    padded = (counts + MOE_BLOCK - 1) // MOE_BLOCK * MOE_BLOCK
    pad_end = jnp.cumsum(padded)
    pad_start = pad_end - padded
    start = jnp.cumsum(counts) - counts
    dest = pad_start[se] + (jnp.arange(n_assign) - start[se])
    n_rows = (n_assign + MOE_BLOCK - 1) // MOE_BLOCK * MOE_BLOCK + N_EXPERTS * MOE_BLOCK
    n_blocks = n_rows // MOE_BLOCK
    row_token = jnp.zeros(n_rows, jnp.int32).at[dest].set(token_id[order])
    row_weight = jnp.zeros(n_rows, f32).at[dest].set(weight[order])
    blk_expert = jnp.minimum(jnp.searchsorted(pad_end, jnp.arange(n_blocks) * MOE_BLOCK, side='right'), N_EXPERTS - 1)
    xb = xt[row_token].reshape(n_blocks, MOE_BLOCK, dm)

    def expert_block(args):
        xblk, e = args
        hid = jax.nn.silu(xblk @ w_gate[e]) * (xblk @ w_up[e])
        return hid @ w_down[e]

    yb = lax.map(expert_block, (xb, blk_expert)).reshape(n_rows, dm)
    y = jnp.zeros_like(xt).at[row_token].add(yb * row_weight[:, None].astype(yb.dtype))
    return y.reshape(bsz, seq, dm)

def setup_inputs(seed: int = 0) -> dict:
    key = jax.random.key(seed)
    keys = iter(jax.random.split(key, 40))
    f32 = jnp.float32
    nrm = lambda shape, s: jax.random.normal(next(keys), shape, f32) * s
    gain = lambda shape: 1.0 + 0.02 * jax.random.normal(next(keys), shape, f32)
    dt = jnp.exp(jax.random.uniform(next(keys), (N_EVEN, SSM_HEADS), f32, math.log(1e-3), math.log(1e-1)))
    return {
        'x': nrm((BATCH, SEQ, D_MODEL), 1.0),
        'rel_bias': nrm((N_BUCKETS, N_ATTN_HEADS), 0.3),
        'attn_norm': gain((DEPTH, D_MODEL)),
        'ffn_norm': gain((DEPTH, D_MODEL)),
        'even_w_in': nrm((N_EVEN, D_MODEL, EVEN_COLS), D_MODEL ** -0.5),
        'even_conv_w': nrm((N_EVEN, SSM_CONV, SSM_CONV_CH), SSM_CONV ** -0.5),
        'even_conv_b': nrm((N_EVEN, SSM_CONV_CH), 0.02),
        'even_dt_bias': dt + jnp.log(-jnp.expm1(-dt)),
        'even_a_log': jnp.log(jax.random.uniform(next(keys), (N_EVEN, SSM_HEADS), f32, 1.0, 16.0)),
        'even_d_skip': gain((N_EVEN, SSM_HEADS)),
        'even_ssm_norm': gain((N_EVEN, SSM_D_INNER)),
        'even_q_norm': gain((N_EVEN, DSA_HEAD_DIM)),
        'even_k_norm': gain((N_EVEN, DSA_HEAD_DIM)),
        'even_w_out': nrm((N_EVEN, EVEN_MIX, D_MODEL), EVEN_MIX ** -0.5),
        'odd_w_in': nrm((N_ODD, D_MODEL, ODD_COLS), D_MODEL ** -0.5),
        'odd_q_norm': gain((N_ODD, NSA_HEAD_DIM)),
        'odd_kc_norm': gain((N_ODD, NSA_HEAD_DIM)),
        'odd_ks_norm': gain((N_ODD, NSA_HEAD_DIM)),
        'odd_kw_norm': gain((N_ODD, NSA_HEAD_DIM)),
        'odd_cmp_pos_k': nrm((N_ODD, CMP_BLOCK, NSA_HEAD_DIM), 0.1),
        'odd_cmp_pos_v': nrm((N_ODD, CMP_BLOCK, NSA_HEAD_DIM), 0.1),
        'odd_cmp_k_w1': nrm((N_ODD, CMP_BLOCK * NSA_HEAD_DIM, NSA_HEAD_DIM), (CMP_BLOCK * NSA_HEAD_DIM) ** -0.5),
        'odd_cmp_k_w2': nrm((N_ODD, NSA_HEAD_DIM, NSA_HEAD_DIM), NSA_HEAD_DIM ** -0.5),
        'odd_cmp_v_w1': nrm((N_ODD, CMP_BLOCK * NSA_HEAD_DIM, NSA_HEAD_DIM), (CMP_BLOCK * NSA_HEAD_DIM) ** -0.5),
        'odd_cmp_v_w2': nrm((N_ODD, NSA_HEAD_DIM, NSA_HEAD_DIM), NSA_HEAD_DIM ** -0.5),
        'odd_w_out': nrm((N_ODD, ODD_MIX, D_MODEL), ODD_MIX ** -0.5),
        'moe_router_group': nrm((DEPTH, D_MODEL, MOE_GROUPS), D_MODEL ** -0.5),
        'moe_router_expert': nrm((DEPTH, MOE_GROUPS, D_MODEL, EXPERTS_PER_GROUP), D_MODEL ** -0.5),
        'moe_w_gate': nrm((DEPTH, N_EXPERTS, D_MODEL, EXPERT_FF), D_MODEL ** -0.5),
        'moe_w_up': nrm((DEPTH, N_EXPERTS, D_MODEL, EXPERT_FF), D_MODEL ** -0.5),
        'moe_w_down': nrm((DEPTH, N_EXPERTS, EXPERT_FF, D_MODEL), EXPERT_FF ** -0.5),
    }

def reference(x, rel_bias, attn_norm, ffn_norm,
              even_w_in, even_conv_w, even_conv_b, even_dt_bias, even_a_log, even_d_skip,
              even_ssm_norm, even_q_norm, even_k_norm, even_w_out,
              odd_w_in, odd_q_norm, odd_kc_norm, odd_ks_norm, odd_kw_norm, odd_cmp_pos_k, odd_cmp_pos_v,
              odd_cmp_k_w1, odd_cmp_k_w2, odd_cmp_v_w1, odd_cmp_v_w2, odd_w_out,
              moe_router_group, moe_router_expert, moe_w_gate, moe_w_up, moe_w_down):
    for i in range(DEPTH):
        h = rms_norm(x, attn_norm[i])
        if i % 2 == 0:
            e = i // 2
            x = x + even_mixer(h, rel_bias, even_w_in[e], even_conv_w[e], even_conv_b[e], even_dt_bias[e],
                               even_a_log[e], even_d_skip[e], even_ssm_norm[e], even_q_norm[e], even_k_norm[e],
                               even_w_out[e])
        else:
            o = i // 2
            x = x + odd_mixer(h, rel_bias, odd_w_in[o], odd_q_norm[o], odd_kc_norm[o], odd_ks_norm[o], odd_kw_norm[o],
                              odd_cmp_pos_k[o], odd_cmp_pos_v[o], odd_cmp_k_w1[o], odd_cmp_k_w2[o],
                              odd_cmp_v_w1[o], odd_cmp_v_w2[o], odd_w_out[o])
        h = rms_norm(x, ffn_norm[i])
        x = x + hier_moe(h, moe_router_group[i], moe_router_expert[i], moe_w_gate[i], moe_w_up[i], moe_w_down[i])
    return x


_drawn_inputs = setup_inputs


def setup_inputs(seed=0):
    import zlib

    import numpy as np

    out = dict(_drawn_inputs(seed))
    spreads = {}
    factors = {'even_q_norm': 4.977,
     'even_k_norm': 4.574,
     'odd_q_norm': 6.812,
     'odd_kc_norm': 8.0,
     'odd_ks_norm': 8.0,
     'odd_kw_norm': 8.0,
     'odd_cmp_pos_k': 5.98}
    for name, (base, spread) in spreads.items():
        noise = np.random.default_rng([zlib.crc32(name.encode()), seed]).standard_normal(out[name].shape)
        drawn = base * np.exp(spread * noise) if base else spread * noise
        out[name] = jnp.asarray(drawn.astype(out[name].dtype))
    for name, factor in factors.items():
        out[name] = (out[name] * factor).astype(out[name].dtype)
    return out
```

```python
from contextlib import ExitStack, contextmanager

import numpy as np

import concourse.bass as bass
from concourse import mybir

F32 = mybir.dt.float32
BF16 = mybir.dt.bfloat16
I32 = mybir.dt.int32
ALU = mybir.AluOpType
ACT = mybir.ActivationFunctionType
AX = mybir.AxisListType

P = 128
SEQ, DM = 512, 1024
NT = SEQ // P
KD = DM // P
EPS = 1e-6
NEG = -1e30
CLAMP = 1e20
TAKEN = -3e38
NB, HEADS = 32, 8
BIAS_W = 2 * SEQ
TW = SEQ + P * (NT - 1)

SH, SD, SN, SG = 8, 64, 128, 2
DI = SH * SD
XBC = DI + 2 * SG * SN
CT = XBC // P
TAPS = 4
HD = 64
IH, ID = 4, 64
TOPK = min(256, SEQ // 4)
C_Z, C_XBC = 0, DI
C_DT = C_XBC + XBC
C_Q = C_DT + SH
C_K = C_Q + HEADS * HD
C_V = C_K + HD
C_IQ = C_V + HD
C_IK = C_IQ + IH * ID
C_IW = C_IK + ID
EVEN_COLS = C_IW + IH

OG, OD = 2, 128
HPG = HEADS // OG
CB, CS = 32, 16
NC = (SEQ - CB) // CS + 1
OKV = OG * OD
C_OK = HEADS * OD
C_GL = C_OK + 6 * OKV
ODD_COLS = C_GL + 3 * HEADS
assert SEQ // 64 <= 16 and SEQ <= 512

MG, EPG = 4, 8
NE = MG * EPG
FF = 512
NA = 2 * SEQ
CAP = 64
NX = (NA - 1) // (CAP + 1)
NBLK = NE + NX
ROWS = NBLK * CAP
NR = MG + NE
FH = FF // 2
EW = 2 * KD * FF + (FF // P) * DM
RING = 3
TRIPS = NE // RING
MORE = SEQ // CAP - 1

O_RING = 0
O_X = RING * EW
O_HT = O_X + NT * DM
O_ROWS = O_HT + KD * SEQ
ARENA = O_ROWS + NT * DM


def bucket_table():
    dist = np.arange(BIAS_W) - (SEQ - 1)
    d = np.maximum(dist, 1).astype(np.float32)
    large = NB // 2 + (np.log(d / np.float32(NB // 2)) / np.float32(np.log(128 / (NB // 2)))
                       * np.float32(NB // 2)).astype(np.int32)
    bucket = np.where(dist < NB // 2, np.maximum(dist, 0), np.minimum(large, NB - 1))
    table = np.zeros((NB + 1, BIAS_W), np.float32)
    table[:NB] = (np.arange(NB)[:, None] == bucket[None]) & (dist >= 0)[None]
    table[NB] = np.where(dist < 0, NEG, 0.0)
    return table


def wait_apart(eng, *waits):
    waits = [(sem, value if isinstance(value, int) else eng.to_reg(value)) for sem, value in waits]
    if not isinstance(waits[0][1], int):
        eng.wait_ge(waits[0][0], 1)
    for sem, value in waits:
        eng.wait_ge(sem, value)


class Chain:

    def __init__(self, eng, sem):
        self.eng, self.sem, self.n, self.term = eng, sem, 0, None

    def __call__(self, ins):
        self.n += 1
        ins.then_inc(self.sem, 1)
        if self.term is None:
            self.eng.wait_ge(self.sem, self.n)
        else:
            wait_apart(self.eng, (self.sem, self.n + self.term))

    def enter(self, i, per_trip):
        self.term, self.start, self.per = i * per_trip, self.n, per_trip

    def leave(self, trips):
        assert self.n - self.start == self.per, (self.n - self.start, self.per)
        self.n, self.term = self.start + trips * self.per, None


COUNTS_ON = {
    "T_in1": ("T_in0", 16), "opar_in": ("par_in", 192), "op_ev": ("ep_ev", 22), "op_mm": ("ep_mm", 22),
    "op_w0": ("ep_w0", 16), "op_w1": ("ep_w1", 16), "op_w2": ("ep_w2", 16), "op_w3": ("ep_w3", 32),
    "op_w4": ("ep_w4", 16), "op_w5": ("ep_w5", 16), "oo_add": ("eo_add", 8), "oo_mm": ("eo_mm", 8),
    "oo_w0": ("eo_w0", 16), "oo_w1": ("eo_w1", 16), "blk": ("seg", 8), "c_hid": ("cb_mm", 4),
    "c_rows": ("abc_mm", 8), "cw1_in0": ("table_in", 32), "cw1_in1": ("ssm_gain_in", 16), "gl_exp": ("eac", 1),
    "hid_c": ("decay", 8), "kcT": ("z_silu", 1), "kc_ms": ("y_ms", 4), "kc_n": ("dA", 1), "kc_raw": ("a_exp", 1),
    "kc_rstd": ("y_rstd", 4), "kc_ss": ("acum", 1), "kc_turned": ("acum_mm", 1), "ok_n": ("mt", 8),
    "ok_out": ("tok_out", 8), "ok_turned": ("tok_turned", 8), "oq_n": ("qn", 4), "oq_out": ("qk_out", 6),
    "oq_turned": ("qk_turned", 5), "oss": ("ssq", 5), "oss_ms": ("ssq_ms", 1), "oss_rstd": ("ssq_rstd", 1),
    "qscale": ("hgain", 1),
    "m_h": ("x_in", 64), "m_rw": ("bias_out", 16), "m_rmm": ("bias_mm", 2), "m_oh": ("conv", 8),
    "m_cnt": ("ix_mm", 12), "m_dest": ("ix_acc", 12), "m_routed": ("selm", 3), "m_sturn": ("yd_mm", 4),
    "m_sidx": ("xw", 3),
}


def past(name):
    return COUNTS_ON[name][1] if name in COUNTS_ON else 0


class Env:

    def __init__(self, nc, ctx):
        self.nc, self.ctx, self.sems = nc, ctx, {}

    def sb(self, name, shape, dt=F32):
        return self.ctx.enter_context(self.nc.sbuf_tensor(name, shape, dt))

    def s(self, name):
        name = COUNTS_ON[name][0] if name in COUNTS_ON else name
        if name not in self.sems:
            self.sems[name] = self.ctx.enter_context(self.nc.semaphore(name))
        return self.sems[name]


def bcast_rows(ap, n, parts=P):
    return bass.AP(ap.tensor, ap.offset, [[0, parts], [1, n]])


def split(ap, *dims):
    names = "abcd"[:len(dims)]
    return ap.rearrange(f"p ({' '.join(names)}) -> p {' '.join(names)}", **dict(zip(names, dims)))


def build(nc, ins, out):
    ctx = ExitStack()
    with ctx:
        ctx.enter_context(nc.allow_non_contiguous_dma(reason="small parameters, channels onto partitions"))
        env = Env(nc, ctx)
        sb, S = env.sb, env.s
        dram = lambda name, shape: nc.dram_tensor(name, shape, F32, kind="Internal").ap()

        arena = sb("arena", [P, ARENA])
        bank = [ctx.enter_context(nc.psum_tensor(f"bank{n}", [P, 512], F32)) for n in range(8)]

        def at(off, *dims):
            n = int(np.prod(dims))
            return split(arena[:, off:off + n], *dims) if len(dims) > 1 else arena[:, off:off + n]

        bias_row_d = dram("bias_row_d", [HEADS, BIAS_W])
        h_d = [dram(f"h_d{n}", [SEQ, DM]) for n in range(2)]
        slot_d = [dram(f"slot_d{n}", [ROWS, 1]) for n in range(2)]
        y_d = [dram(f"y_d{n}", [ROWS, DM]) for n in range(2)]

        ident = sb("ident", [P, P])
        identb = sb("identb", [P, P], BF16)
        ones = sb("ones", [P, P])
        tri = sb("tri", [P, P])
        tri_strict = sb("tri_strict", [P, P])
        score_base = sb("score_base", [P, SEQ])
        nhalf = sb("nhalf", [P, 36])
        iota32 = sb("iota32", [P, NE])
        row_off = sb("row_off", [P, NE])
        more_at = sb("more_at", [P, MORE])
        half_of = sb("half_of", [P, 1])
        token2 = sb("token2", [P, NT])
        zero_slots = sb("zero_slots", [P, NBLK])
        gain = sb("gain", [P, DM])
        ss = sb("ss", [P, NT])
        rstd = sb("rstd", [P, NT])

        xt = at(O_X, NT, DM)
        hT = at(O_HT, KD, SEQ)
        rows = at(O_ROWS, NT, DM)

        NORM = {"n0": 0, "m0n": 1, "n2": 2, "m1n": 3}
        TURN = {"n0": 0, "eo": 1, "m0n": 2, "n2": 3, "oo": 4, "m1n": 5}

        def rows_ready(eng, tag, tiles):
            eng.wait_ge(S("norm_row"), NT * NORM[tag] + tiles)

        def norm_act(act, tag, x_ready):
            x_ready(act)
            for i in range(NT):
                nc.scalar.activation(rows[:, i, :], xt[:, i, :], ACT.Square,
                                     accum_out=ss[:, i:i + 1]).then_inc(S("norm_sq"), 1)

        def norm_pool(pool, tag):
            pool.wait_ge(S("norm_sq"), NT * (NORM[tag] + 1))
            nc.gpsimd.tensor_scalar(ss[:], ss[:], 1.0 / DM, EPS, ALU.mult, ALU.add).then_inc(S("norm_ms"), 1)
            pool.wait_ge(S("norm_ms"), NORM[tag] + 1)
            nc.gpsimd.tensor_tensor(rstd[:], ss[:], nhalf[:, 0:NT], ALU.pow).then_inc(S("norm_rstd"), 1)

        def norm_dve(dve, tag, gain_n):
            dve.wait_ge(S("norm_rstd"), NORM[tag] + 1)
            dve.wait_ge(S("gain_in"), 16 * gain_n)

            def row(i):
                nc.vector.scalar_tensor_tensor(rows[:, i, :], xt[:, i, :], rstd[:, i:i + 1], gain[:], ALU.mult,
                                               ALU.mult).then_inc(S("norm_row"), 1)
            row(0)
            for i in range(NT):
                if i + 1 < NT:
                    row(i + 1)
                turn_evac(dve, tag, hT, i, 1)

        def turn_pe(pe, tag, src, ready):
            for i in range(NT):
                ready(pe, i)
                for half in range(2):
                    if i >= 2:
                        pe.wait_ge(S(f"turn_out{half}"), NT * TURN[tag] + i - 1)
                    for k in range(4):
                        mm = nc.tensor.transpose(bank[(2 * i + half) % 4][:, k * P:(k + 1) * P],
                                                 src(i, 4 * half + k), ident[:])
                    mm.then_inc(S("turned"), 1)

        def turn_evac(eng, tag, dst, i, half):
            eng.wait_ge(S("turned"), 2 * NT * TURN[tag] + 2 * i + half + 1)
            d = dst[:, 4 * half:4 * half + 4, i * P:(i + 1) * P]
            b = split(bank[(2 * i + half) % 4][:, :], 4, P)
            ins_ = nc.vector.tensor_copy(d, b) if half else nc.scalar.activation(d, b, ACT.Copy)
            ins_.then_inc(S(f"turn_out{half}"), 1)

        def turned(eng, tag):
            eng.wait_ge(S("turn_out0"), NT * (TURN[tag] + 1))
            eng.wait_ge(S("turn_out1"), NT * (TURN[tag] + 1))

        STAGES = 2
        M = STAGES * NT
        O_FIRST = 6

        class Attention:
            def __init__(self, tag, branches, loop, trips, queries, biases, q_of, b_of, work, finish, before=None):
                self.loop, self.queries, self.biases, self.q_of, self.b_of = loop, queries, biases, q_of, b_of
                self.finish, self.first = finish, before is None
                self.NB = len(branches[0])
                self.units = [(s, i, b, branches[i][b]) for s in range(STAGES) for i in range(NT) for b in range(self.NB)]
                self.U = len(self.units)
                self.t0, self.u0, self.m0 = (0, 0, 0) if before is None else before.after
                self.after = self.t0 + trips, self.u0 + trips * self.U, self.m0 + trips * M
                self.lg = at(work, 2, SEQ)
                self.p = at(work + 2 * SEQ, 2, SEQ)
                self.pT = at(work + 4 * SEQ, 2, 4, P)
                self.negm = sb(f"{tag}_negm", [P, 2])
                self.sums = sb(f"{tag}_sums", [P, 2, self.NB])
                self.coef = sb(f"{tag}_coef", [P, 2, self.NB])

            def sem(self, what):
                return S(f"att_{what}")

            def staged(self, it, s):
                return self.sem("staged"), 2 * STAGES * (self.t0 + it) + 2 * s + 2

            def two_macros_ago(self, it, m):
                return self.sem("o"), self.m0 + it * M + m - 1 + O_FIRST

            def pe(self, pe):
                if self.first:
                    pe.sem_inc(self.sem("qk"), 2)
                    pe.sem_inc(self.sem("tr"), 2)
                    pe.sem_inc(self.sem("pv"), 2)
                with self.loop(pe) as (it, v):
                    for t in range(self.U + 2):
                        if t < self.U:
                            s, i, b, br = self.units[t]
                            n = self.u0 + it * self.U + t
                            if i == 0 and b == 0:
                                pe.wait_ge(*self.staged(it, s))
                            pe.wait_ge(self.sem("lg"), n + 1)
                            o = bank[t % 2][:, 0:br["L"]]
                            mm = nc.tensor.matmul(o, self.queries[s][:, i * P:(i + 1) * P], br["k"](v),
                                                  start=True, stop=not br.get("mask"))
                            if br.get("mask"):
                                mm = nc.tensor.matmul(o, identb[:], br["mask"], start=False, stop=True)
                            mm.then_inc(self.sem("qk"), 1)
                        if 1 <= t <= self.U:
                            s, i, b, br = self.units[t - 1]
                            n = self.u0 + it * self.U + t - 1
                            pe.wait_ge(self.sem("ex"), n + 3)
                            pe.wait_ge(self.sem("pt"), n + 1)
                            for kt in range((br["L"] + P - 1) // P):
                                w = min(P, br["L"] - kt * P)
                                mm = nc.tensor.transpose(bank[2 + (t - 1) % 2][0:w, kt * P:(kt + 1) * P],
                                                         self.p[:, (t - 1) % 2, kt * P:kt * P + w], ident[:])
                            mm.then_inc(self.sem("tr"), 1)
                        if t >= 2:
                            s, i, b, br = self.units[t - 2]
                            m = NT * s + i
                            n = self.u0 + it * self.U + t - 2
                            wait_apart(pe, (self.sem("pt"), n + 3), *([self.two_macros_ago(it, m)] if b == 0 else []))
                            D = br["D"]
                            nk = (br["L"] + P - 1) // P
                            for kt in range(nk):
                                w = min(P, br["L"] - kt * P)
                                mm = nc.tensor.matmul(bank[4 + m % 2][:, b * D:(b + 1) * D],
                                                      self.pT[0:w, (t - 2) % 2, kt, :], br["v"](v, kt),
                                                      start=(kt == 0), stop=(kt == nk - 1))
                            mm.then_inc(self.sem("pv"), 1)

            def act(self, act):
                if self.first:
                    act.sem_inc(self.sem("ex"), 2)
                    act.sem_inc(self.sem("pt"), 2)
                with self.loop(act) as (it, v):
                    for t in range(self.U + 1):
                        if t < self.U:
                            s, i, b, br = self.units[t]
                            m = NT * s + i
                            n = self.u0 + it * self.U + t
                            L = br["L"]
                            act.wait_ge(self.sem("lg"), n + 3)
                            act.wait_ge(self.sem("tr"), n + 1)
                            if b == 0:
                                act.wait_ge(*self.two_macros_ago(it, m))
                            nc.scalar.activation(self.p[:, t % 2, 0:L], self.lg[:, t % 2, 0:L], ACT.Exp,
                                                 bias=self.negm[:, t % 2:t % 2 + 1], scale=-1.0,
                                                 accum_out=self.sums[:, m % 2, b:b + 1]).then_inc(self.sem("ex"), 1)
                        if t >= 1:
                            s, i, b, br = self.units[t - 1]
                            n = self.u0 + it * self.U + t - 1
                            L = br["L"]
                            act.wait_ge(self.sem("tr"), n + 3)
                            act.wait_ge(self.sem("pv"), n + 1)
                            w = min(P, L)
                            nk = (L + P - 1) // P
                            nc.scalar.activation(self.pT[0:w, (t - 1) % 2, 0:nk, :],
                                                 split(bank[2 + (t - 1) % 2][0:w, 0:nk * P], nk, P),
                                                 ACT.Copy).then_inc(self.sem("pt"), 1)

            def dve(self, dve, link):
                if self.first:
                    dve.sem_inc(self.sem("lg"), 2)
                    dve.sem_inc(self.sem("o"), O_FIRST)
                with self.loop(dve, link) as (it, v):
                    for t in range(self.U + 2):
                        if t < self.U:
                            s, i, b, br = self.units[t]
                            n = self.u0 + it * self.U + t
                            L = br["L"]
                            first = i == 0 and b == 0
                            wait_apart(dve, (self.sem("qk"), n + 3), (self.sem("ex"), n + 1),
                                       *([self.staged(it, s)] if first else []))
                            ins_ = nc.vector.tensor_tensor_reduce(
                                out=self.lg[:, t % 2, 0:L], in0=bank[t % 2][:, 0:L], in1=br["bias"](self.biases[s]),
                                scale=-1.0, scalar=3e38, op0=ALU.add, op1=ALU.min,
                                accum_out=self.negm[:, t % 2:t % 2 + 1])
                            if br.get("clamp"):
                                link(ins_)
                                ins_ = nc.vector.tensor_scalar(self.negm[:, t % 2:t % 2 + 1],
                                                               self.negm[:, t % 2:t % 2 + 1], CLAMP, None, ALU.min)
                            ins_.then_inc(self.sem("lg"), 1)
                        if t >= 2:
                            s, i, b, br = self.units[t - 2]
                            if b == self.NB - 1:
                                n = self.u0 + it * self.U + t - 2
                                dve.wait_ge(self.sem("pv"), n + 3)
                                self.finish(self, dve, link, v, s, NT * s + i, i).then_inc(self.sem("o"), 1)

            def pool(self, pool):
                with self.loop(pool) as (it, v):
                    for s in range(STAGES):
                        wait_apart(pool, (self.sem("o"), self.m0 + (it - 1) * M + (s + 1) * NT + O_FIRST))
                        nc.gpsimd.tensor_copy(self.queries[s], self.q_of(v, s)).then_inc(self.sem("staged"), 1)
                        nc.gpsimd.tensor_copy(self.biases[s][..., ::-1], self.b_of(v, s)).then_inc(self.sem("staged"), 1)

            def done(self, eng):
                eng.wait_ge(self.sem("o"), self.after[2] + O_FIRST)

        def outproj_pe(pe, tag, mixT, wo, loads):
            turned(pe, tag)
            for half in range(2):
                pe.wait_ge(S(f"{tag}_w{half}"), past(f"{tag}_w{half}") + 16)
                for i in range(NT):
                    n = half * NT + i
                    if n >= 4:
                        pe.wait_ge(S(f"{tag}_add"), past(f"{tag}_add") + n - 3)
                    for k in range(KD):
                        mm = nc.tensor.matmul(bank[4 + n % 4][:, :], mixT[:, k, i * P:(i + 1) * P], wo[half][:, k, :],
                                              start=(k == 0), stop=(k == KD - 1))
                    mm.then_inc(S(f"{tag}_mm"), 1)

        def outproj_dve(dve, tag):
            for half in range(2):
                for i in range(NT):
                    n = half * NT + i
                    dve.wait_ge(S(f"{tag}_mm"), past(f"{tag}_mm") + n + 1)
                    xs = xt[:, i, half * 512:(half + 1) * 512]
                    nc.vector.tensor_tensor(xs, xs, bank[4 + n % 4][:, :], ALU.add).then_inc(S(f"{tag}_add"), 1)

        e0 = O_RING
        T = at(e0, HEADS, TW); e0 += HEADS * TW
        xbcT = at(e0, CT, SEQ + TAPS - 1)
        xtok = at(e0, NT, DI)
        btok = at(e0 + NT * DI, NT, SG * SN)
        state = at(e0 + NT * (DI + SG * SN), DI)
        y_t = at(e0 + NT * (DI + SG * SN) + DI, DI)
        e0 += CT * (SEQ + TAPS - 1)
        O_XBCS = e0
        xbcS = at(e0, CT, SEQ); e0 += CT * SEQ
        z = at(e0, NT, DI); e0 += NT * DI
        O_QROWS = e0
        assert STAGES * (SEQ + 2 * TW) <= CT * SEQ + NT * DI
        qrows = at(e0, NT, HEADS * HD); e0 += NT * HEADS * HD
        eqT = at(e0, 4, SEQ); e0 += 4 * SEQ
        kA = at(e0, SEQ); kB = at(e0 + SEQ, SEQ); e0 += 2 * SEQ
        kvd = at(e0, NT, 2 * HD + SH); e0 += NT * (2 * HD + SH)
        selm = split(arena[:, e0:e0 + NT * SEQ // 2].bitcast(BF16), NT, SEQ); e0 += NT * SEQ // 2
        score = at(e0, NT - 1, SEQ); e0 += (NT - 1) * SEQ
        iqT = at(e0, 2, SEQ); ikA = at(e0 + 2 * SEQ, SEQ); ikB = at(e0 + 3 * SEQ, SEQ); e0 += 4 * SEQ
        O_EW = e0
        ew = [at(e0, KD, 512), at(e0 + KD * 512, KD, 512)]
        assert e0 + 2 * KD * 512 <= RING * EW, e0
        seg = at(O_EW, SG, 4, P)
        cbm = at(O_EW + 1024, SG, P)
        xdt = at(O_EW + 1280, DI)
        xw = at(O_EW + 1792, DI)
        y2 = at(O_EW + 2304, DI)
        ssm_gain = at(O_EW + 2816, DI)
        krn = at(O_EW + 3328, NT, P)
        junk = at(O_ROWS + NT * DI, DI)
        e_wo = [hT, at(O_EW + KD * 512, KD, 512)]
        relu = at(O_ROWS, 2, SEQ)
        rows_m = at(O_ROWS, 2, NT, DI)
        mixT = at(O_RING, KD, SEQ)
        table = at(O_QROWS, BIAS_W)
        brow = at(O_QROWS + BIAS_W, BIAS_W)

        relb = sb("relb", [NB + 1, HEADS])
        conv_w = sb("conv_w", [P, TAPS, CT])
        conv_b = sb("conv_b", [P, CT])
        dt_bias = sb("dt_bias", [P, SH]); a_log = sb("a_log", [P, SH]); d_skip = sb("d_skip", [P, SH])
        head_gain = sb("head_gain", [P, 2])
        iw = sb("iw", [P, NT, IH])
        m8 = sb("m8", [P, 8])
        dt = sb("dt", [P, NT, SH]); dt_e = sb("dt_e", [P, NT, SH]); dA = sb("dA", [P, NT, SH])
        acum = sb("acum", [P, NT, SH]); eac = sb("eac", [P, NT, SH])
        alast = sb("alast", [P, SH]); cdecay = sb("cdecay", [P, SH]); to_end = sb("to_end", [P, SH])
        ssq = sb("ssq", [P, NT, HEADS + 1])
        ssg = sb("ssg", [P, 2])

        w_in = ins["even_w_in"][0]
        EV_CHUNKS = [[(C_IQ, EVEN_COLS - C_IQ)], [(C_XBC, 512)], [(C_XBC + 512, 512)],
                     [(C_K, 2 * HD), (C_DT, SH)], [(C_Z, DI)], [(C_Q, HEADS * HD)]]
        J_IQ, J_IK, J_IW, J_XBC, J_KV, J_Z, J_Q, J_END = 0, 2, 3, 4, 12, 14, 18, 22
        CHUNK_JOBS = [J_XBC, J_XBC + 4, J_KV, J_Z, J_Q, J_END]
        SC = [(i, h) for i in range(1, NT) for h in range(IH)]

        def load_chunk(sp, c, chunks, src, bufs, tag, done_jobs):
            nbuf = len(bufs)
            if c >= nbuf:
                sp.wait_ge(S(f"{tag}_mm"), past(f"{tag}_mm") + done_jobs[c - nbuf])
            off = 0
            for c0, n in chunks[c]:
                sp.dma_start(bufs[c % nbuf][:, :, off:off + n],
                             src[:, c0:c0 + n].rearrange("(k p) c -> p k c", p=P)).then_inc(S(f"{tag}_w{c}"), 16)
                off += n

        def even_sp(sp):
            for i in range(NT):
                sp.dma_start(xt[:, i, :], ins["x"][0, i * P:(i + 1) * P, :]).then_inc(S("x_in"), 16)
            sp.dma_start(gain[:], bcast_rows(ins["attn_norm"][0, :], DM)).then_inc(S("gain_in"), 16)
            load_chunk(sp, 0, EV_CHUNKS, w_in, ew, "ep", CHUNK_JOBS)
            sp.wait_ge(S("relb_ones"), 1)
            sp.dma_start(relb[0:NB, :], ins["rel_bias"]).then_inc(S("table_in"), 16)
            sp.dma_start(table[0:NB + 1, :], ins["bucket_table"]).then_inc(S("table_in"), 16)
            load_chunk(sp, 1, EV_CHUNKS, w_in, ew, "ep", CHUNK_JOBS)
            sp.dma_start(conv_b[:], ins["even_conv_b"][0].rearrange("(c p) -> p c", p=P)).then_inc(S("par_in"), 16)
            for k in range(TAPS):
                sp.dma_start(conv_w[:, k, :],
                             ins["even_conv_w"][0, k].rearrange("(c p) -> p c", p=P)).then_inc(S("par_in"), 16)
            for t_, name in ((dt_bias, "even_dt_bias"), (a_log, "even_a_log"), (d_skip, "even_d_skip")):
                sp.dma_start(t_[:], bcast_rows(ins[name][0], SH)).then_inc(S("par_in"), 16)
            for n, name in enumerate(("even_q_norm", "even_k_norm")):
                for half in range(2):
                    sp.dma_start(head_gain[half * HD:(half + 1) * HD, n:n + 1],
                                 ins[name][0].rearrange("(p c) -> p c", c=1)).then_inc(S("par_in"), 16)
            sp.wait_ge(S("brow"), 2)
            sp.dma_start(bias_row_d, brow[0:HEADS, :]).then_inc(S("bias_out"), 16)
            sp.wait_ge(S("bias_out"), 16)
            load_bias(sp, "T_in0")
            sp.wait_ge(S("zeros"), 1)
            for n in range(2):
                sp.dma_start(slot_d[n].rearrange("(a b) c -> a (b c)", a=CAP),
                             zero_slots[0:CAP, :]).then_inc(S("slots_zero"), 16)
            for c in range(2, 6):
                load_chunk(sp, c, EV_CHUNKS, w_in, ew, "ep", CHUNK_JOBS)
            sp.wait_ge(S("ep_mm"), J_END)
            sp.dma_start(e_wo[0], ins["even_w_out"][0, :, 0:512].rearrange("(k p) c -> p k c", p=P)).then_inc(S("eo_w0"), 16)
            sp.dma_start(ssm_gain, bcast_rows(ins["even_ssm_norm"][0], DI)).then_inc(S("ssm_gain_in"), 16)
            sp.dma_start(e_wo[1], ins["even_w_out"][0, :, 512:1024].rearrange("(k p) c -> p k c", p=P)).then_inc(S("eo_w1"), 16)

        def load_bias(sp, done):
            src = bass.AP(bias_row_d.tensor, 0, [[1, P], [BIAS_W, HEADS], [1, TW]])
            sp.dma_start(T, src).then_inc(S(done), 16)

        def even_pe(pe):
            pe.wait_ge(S("table_in"), 32)
            pe.wait_ge(S("consts"), 1)
            for half in range(2):
                nc.tensor.matmul(bank[4 + half][0:HEADS, :], relb[:], table[0:NB + 1, half * 512:(half + 1) * 512],
                                 start=True, stop=True).then_inc(S("bias_mm"), 1)
            turn_pe(pe, "n0", lambda i, k: rows[:, i, k * P:(k + 1) * P], lambda e, i: rows_ready(e, "n0", i + 1))
            turned(pe, "n0")

            def job(n, mms):
                if n >= 4:
                    pe.wait_ge(S("ep_ev"), n - 3)
                for mm_args in mms:
                    for k in range(KD):
                        o, l, r = mm_args(k)
                        mm = nc.tensor.matmul(o, l, r, start=(k == 0), stop=(k == KD - 1))
                mm.then_inc(S("ep_mm"), 1)

            def channels(n, w, c0, hTk=hT):
                b = bank[n % 4]
                job(n, [lambda k: (b[:, :], w[:, k, c0:c0 + P], hT[:, k, :])])

            def tokens(n, w, tiles, cols):
                b = bank[n % 4]
                job(n, [lambda k, i=i, s=s: (b[:, s * cols:(s + 1) * cols], hT[:, k, i * P:(i + 1) * P], w[:, k, 0:cols])
                        for s, i in enumerate(tiles)])

            pe.wait_ge(S("ep_w0"), 16)
            for j in range(2):
                channels(J_IQ + j, ew[0], j * P)
            b = bank[J_IK % 4]
            c0 = IH * ID
            job(J_IK, [lambda k, q=q: (b[q * HD:(q + 1) * HD, :], ew[0][:, k, c0:c0 + ID], hT[:, k, :]) for q in range(2)])
            b2 = bank[J_IW % 4]
            c1 = c0 + ID
            job(J_IW, [lambda k, i=i: (b2[:, i * IH:(i + 1) * IH], hT[:, k, i * P:(i + 1) * P], ew[0][:, k, c1:c1 + IH])
                       for i in range(NT)])
            pe.wait_ge(S("ep_ev"), J_IK + 1)
            pe.wait_ge(S("brow"), 2)
            for u, (i, h) in enumerate(SC):
                if u >= 2:
                    pe.wait_ge(S("ix_relu"), u - 1)
                L = (i + 1) * P
                nc.tensor.matmul(bank[4 + u % 2][:, 0:L], iqT[:, h // 2, i * P:(i + 1) * P], (ikA, ikB)[h % 2][:, 0:L],
                                 start=True, stop=True).then_inc(S("ix_mm"), 1)
            for c in range(2):
                pe.wait_ge(S(f"ep_w{1 + c}"), 16)
                for j in range(4):
                    channels(J_XBC + 4 * c + j, ew[(1 + c) % 2], j * P)
            pe.wait_ge(S("ep_w3"), 32)
            for j in range(2):
                tokens(J_KV + j, ew[1], (2 * j, 2 * j + 1), 2 * HD + SH)
            pe.wait_ge(S("ep_w4"), 16)
            for i in range(NT):
                tokens(J_Z + i, ew[0], (i,), DI)
            pe.wait_ge(S("ep_w5"), 16)
            for i in range(NT):
                tokens(J_Q + i, ew[1], (i,), HEADS * HD)

            pe.wait_ge(S("ep_ev"), J_END)
            pe.wait_ge(S("kn"), 2)
            for i in range(NT):
                mm = nc.tensor.transpose(bank[0][:, i * P:(i + 1) * P], krn[:, i, :], ident[:])
            mm.then_inc(S("qk_turned"), 1)
            for i in range(NT):
                pe.wait_ge(S("qn"), i + 1)
                if i >= 2:
                    pe.wait_ge(S("qk_out"), i + 1)
                for j in range(4):
                    mm = nc.tensor.transpose(bank[1 + i % 2][:, j * P:(j + 1) * P], qrows[:, i, j * P:(j + 1) * P], ident[:])
                mm.then_inc(S("qk_turned"), 1)

            pe.wait_ge(S("dA"), 1)
            for i in range(NT):
                mm = nc.tensor.matmul(bank[3][:, i * SH:(i + 1) * SH], tri[:], dA[:, i, :], start=True, stop=True)
            mm.then_inc(S("acum_mm"), 1)
            pe.wait_ge(S("silu"), CT)
            pe.wait_ge(S("qk_out"), NT + 2)
            for i in range(NT):
                if i >= 1:
                    pe.wait_ge(S("tok_out"), 2 * i)
                for j in range(4):
                    mm = nc.tensor.transpose(bank[4][:, j * P:(j + 1) * P], xbcS[:, j, i * P:(i + 1) * P], ident[:])
                mm.then_inc(S("tok_turned"), 1)
                for g in range(SG):
                    mm = nc.tensor.transpose(bank[5][:, g * P:(g + 1) * P], xbcS[:, 4 + g, i * P:(i + 1) * P], ident[:])
                mm.then_inc(S("tok_turned"), 1)
            for i in range(NT):
                sl = slice(i * P, (i + 1) * P)
                if i >= 1:
                    pe.wait_ge(S("seg"), 2 * i)
                    pe.wait_ge(S("cbm"), i)
                for g in range(SG):
                    for h in range(4):
                        mm = nc.tensor.matmul(bank[6 + g][:, h * P:(h + 1) * P],
                                              dA[:, i, 4 * g + h:4 * g + h + 1].broadcast_to((P, P)), tri[:],
                                              start=True, stop=True)
                    mm.then_inc(S("abc_mm"), 1)
                if i == 0:
                    pe.wait_ge(S("acum"), 1)
                for g in range(SG):
                    mm = nc.tensor.matmul(bank[3][:, g * P:(g + 1) * P], xbcS[:, 4 + g, sl], xbcS[:, 6 + g, sl],
                                          start=True, stop=True)
                mm.then_inc(S("cb_mm"), 1)
                if i >= 1:
                    pe.wait_ge(S("state"), i)
                    for g in range(SG):
                        mm = nc.tensor.matmul(bank[1][:, g * 256:(g + 1) * 256], xbcS[:, 6 + g, sl],
                                              state[:, g * 256:(g + 1) * 256], start=True, stop=True)
                    mm.then_inc(S("yoff_mm"), 1)
                if i < NT - 1:
                    pe.wait_ge(S("xw"), i + 1)
                    pe.wait_ge(S("tok_out"), 2 * i + 2)
                    for g in range(SG):
                        mm = nc.tensor.matmul(bank[2][:, g * 256:(g + 1) * 256], btok[:, i, g * P:(g + 1) * P],
                                              xw[:, g * 256:(g + 1) * 256], start=True, stop=True)
                    mm.then_inc(S("st_mm"), 1)
                for g in range(SG):
                    pe.wait_ge(S("mt"), 2 * i + g + 1)
                    for h in range(4):
                        hh = 4 * g + h
                        mm = nc.tensor.matmul(bank[0][:, hh * SD:(hh + 1) * SD], seg[:, g, h, :],
                                              xdt[:, hh * SD:(hh + 1) * SD], start=True, stop=True)
                mm.then_inc(S("yd_mm"), 1)

            pe.wait_ge(S("T_in0"), 16)
            pe.wait_ge(S("selm"), NT - 1)
            pe.wait_ge(S("y_gated"), NT)
            even_att.pe(pe)
            even_att.done(pe)
            pe.wait_ge(S("ssm_row"), NT)
            turn_pe(pe, "eo", lambda i, k: rows_m[:, k // 4, i, (k % 4) * P:(k % 4 + 1) * P], lambda e, i: None)
            outproj_pe(pe, "eo", mixT, e_wo, None)

        def even_act(act):
            for half in range(2):
                act.wait_ge(S("bias_mm"), half + 1)
                nc.scalar.activation(brow[0:HEADS, half * 512:(half + 1) * 512], bank[4 + half][0:HEADS, :],
                                     ACT.Copy).then_inc(S("brow"), 1)
            norm_act(act, "n0", lambda e: e.wait_ge(S("x_in"), 16 * NT))
            for i in range(NT):
                turn_evac(act, "n0", hT, i, 0)

            def ev(n, dst, src, scale=1.0):
                act.wait_ge(S("ep_mm"), n + 1)
                return nc.scalar.activation(dst, src, ACT.Copy)
            for j in range(2):
                ev(J_IQ + j, iqT[:, j, :], bank[J_IQ + j][:, :]).then_inc(S("ep_ev"), 1)
            act.wait_ge(S("pads"), 2)
            ev(J_IK, ikA[0:HD, :], bank[J_IK][0:HD, :])
            nc.scalar.activation(ikB[HD:P, :], bank[J_IK][HD:P, :], ACT.Copy).then_inc(S("ep_ev"), 1)
            ev(J_IW, iw[:], split(bank[J_IW][:, 0:NT * IH], NT, IH)).then_inc(S("ep_ev"), 1)
            turned(act, "n0")
            for u, (i, h) in enumerate(SC):
                L = (i + 1) * P
                act.wait_ge(S("ix_mm"), u + 1)
                if u >= 2:
                    act.wait_ge(S("ix_acc"), u - 1)
                nc.scalar.activation(relu[:, u % 2, 0:L], bank[4 + u % 2][:, 0:L], ACT.Relu,
                                     scale=float(ID * IH) ** -0.5).then_inc(S("ix_relu"), 1)
            act.wait_ge(S("pads"), 3)
            for c in range(CT):
                n = J_XBC + c
                ev(n, xbcT[:, c, TAPS - 1:], bank[n % 4][:, :]).then_inc(S("ep_ev"), 1)
            for j in range(2):
                n = J_KV + j
                w = 2 * HD + SH
                ev(n, kvd[:, 2 * j:2 * j + 2, :], split(bank[n % 4][:, 0:2 * w], 2, w)).then_inc(S("ep_ev"), 1)
            for i in range(NT):
                n = J_Z + i
                ev(n, z[:, i, :], bank[n % 4][:, :]).then_inc(S("ep_ev"), 1)
            act.wait_ge(S("bias_out"), 16)
            for i in range(NT):
                n = J_Q + i
                ev(n, qrows[:, i, :], bank[n % 4][:, :]).then_inc(S("ep_ev"), 1)
            act.wait_ge(S("ep_mm"), J_END)
            act.wait_ge(S("ep_ev"), J_END)
            nc.scalar.activation(split(junk[:, 0:NT * HD], NT, HD), kvd[:, :, 0:HD], ACT.Square).then_inc(S("sq"), 1)
            for i in range(NT):
                act.wait_ge(S("ssq"), i + 1)
                nc.scalar.activation(junk, qrows[:, i, :], ACT.Square).then_inc(S("sq"), 1)
            act.wait_ge(S("dt_abs"), 1)
            act.wait_ge(S("par_in"), 16 * 12)
            nc.scalar.activation(dt_e[:], dt_e[:], ACT.Exp, scale=-1.0).then_inc(S("dt_exp"), 1)
            nc.scalar.activation(a_log[:], a_log[:], ACT.Exp).then_inc(S("a_exp"), 1)
            act.wait_ge(S("dt_exp"), 1)
            nc.scalar.activation(dt_e[:], dt_e[:], ACT.Ln, bias=1.0).then_inc(S("dt_ln"), 1)
            act.wait_ge(S("qk_turned"), 1)
            act.wait_ge(S("pads"), 5)
            act.wait_ge(S("hgain"), 1)
            nc.scalar.activation(kA[0:HD, :], bank[0][0:HD, :], ACT.Copy, scale=head_gain[0:HD, 1:2]).then_inc(S("qk_out"), 1)
            nc.scalar.activation(kB[HD:P, :], bank[0][HD:P, :], ACT.Copy, scale=head_gain[HD:P, 1:2]).then_inc(S("qk_out"), 1)
            for i in range(NT):
                act.wait_ge(S("qk_turned"), i + 2)
                nc.scalar.activation(eqT[:, :, i * P:(i + 1) * P], split(bank[1 + i % 2][:, :], 4, P), ACT.Copy,
                                     scale=head_gain[:, 0:1]).then_inc(S("qk_out"), 1)
            for c in range(CT):
                act.wait_ge(S("conv"), c + 1)
                nc.scalar.activation(xbcS[:, c, :], xbcS[:, c, :], ACT.Silu, bias=conv_b[:, c:c + 1]).then_inc(S("silu"), 1)
            nc.scalar.activation(z, z, ACT.Silu).then_inc(S("z_silu"), 1)
            for i in range(NT):
                act.wait_ge(S("tok_turned"), 2 * i + 1)
                nc.scalar.activation(xtok[:, i, :], bank[4][:, :], ACT.Copy).then_inc(S("tok_out"), 1)
                act.wait_ge(S("tok_turned"), 2 * i + 2)
                nc.scalar.activation(btok[:, i, :], bank[5][:, 0:SG * SN], ACT.Copy).then_inc(S("tok_out"), 1)
            act.wait_ge(S("acum"), 1)
            nc.scalar.activation(eac[:], acum[:], ACT.Exp).then_inc(S("eac"), 1)
            for i in range(NT):
                act.wait_ge(S("alast"), i + 1)
                nc.scalar.activation(to_end[:], to_end[:], ACT.Exp).then_inc(S("ends"), 1)
                nc.scalar.activation(cdecay[:], alast[:], ACT.Exp).then_inc(S("ends"), 1)
                for g in range(SG):
                    act.wait_ge(S("seg"), 2 * i + g + 1)
                    nc.scalar.activation(seg[:, g], seg[:, g], ACT.Exp).then_inc(S("decay"), 1)
                act.wait_ge(S("y_gated"), i + 1)
                for g in range(SG):
                    nc.scalar.activation(junk[:, g * 256:(g + 1) * 256], y_t[:, g * 256:(g + 1) * 256], ACT.Square,
                                         accum_out=ssg[:, g:g + 1]).then_inc(S("y_sq"), 1)
            even_att.act(act)
            for i in range(NT):
                turn_evac(act, "eo", mixT, i, 0)

        def even_pool(pool):
            steps = 0

            def c(ins_):
                nonlocal steps
                steps += 1
                ins_.then_inc(S("pool_const"), 1)
            g_ = nc.gpsimd
            c(g_.memset(ident[:], 0.0)); c(g_.memset(ones[:], 1.0)); c(g_.memset(tri[:], 1.0))
            c(g_.memset(tri_strict[:], 1.0)); c(g_.memset(score_base[:], 0.0)); c(g_.memset(nhalf[:], -0.5))
            c(g_.memset(half_of[:], 1.0))
            c(g_.iota(iota32[:], [[1, NE]], base=0, channel_multiplier=0, allow_small_or_imprecise_dtypes=True))
            c(g_.iota(row_off[:], [[CAP, NE]], base=0, channel_multiplier=0, allow_small_or_imprecise_dtypes=True))
            c(g_.iota(more_at[:], [[CAP, MORE]], base=CAP, channel_multiplier=0, allow_small_or_imprecise_dtypes=True))
            c(g_.iota(token2[:], [[2 * P, NT]], base=0, channel_multiplier=2, allow_small_or_imprecise_dtypes=True))
            pool.wait_ge(S("pool_const"), steps)
            c(g_.affine_select(out=ident[:], in_=ident[:], compare_op=ALU.not_equal, fill=1.0, base=0,
                               pattern=[[-1, P]], channel_multiplier=1))
            c(g_.affine_select(out=tri[:], in_=tri[:], compare_op=ALU.is_ge, fill=0.0, base=0,
                               pattern=[[1, P]], channel_multiplier=-1))
            c(g_.affine_select(out=tri_strict[:], in_=tri_strict[:], compare_op=ALU.is_gt, fill=0.0, base=0,
                               pattern=[[1, P]], channel_multiplier=-1))
            c(g_.affine_select(out=score_base[:, SEQ - P:], in_=score_base[:, SEQ - P:], compare_op=ALU.is_ge, fill=NEG,
                               base=0, pattern=[[-1, P]], channel_multiplier=1))
            c(g_.affine_select(out=half_of[:], in_=half_of[:], compare_op=ALU.is_ge, fill=0.0,
                               base=-CAP, pattern=[[0, 1]], channel_multiplier=1))
            c(g_.memset(zero_slots[:], 0.0))
            c(g_.memset(relb[:], 1.0))
            pool.wait_ge(S("pool_const"), steps)
            g_.tensor_copy(identb[:], ident[:]).then_inc(S("consts"), 1)
            g_.sem_inc(S("zeros"), 1)
            g_.sem_inc(S("relb_ones"), 1)
            g_.memset(ikA, 0.0).then_inc(S("pads"), 1)
            g_.memset(ikB, 0.0).then_inc(S("pads"), 1)
            g_.memset(xbcT[:, :, 0:TAPS - 1], 0.0).then_inc(S("pads"), 1)
            g_.memset(kA, 0.0).then_inc(S("pads"), 1)
            g_.memset(kB, 0.0).then_inc(S("pads"), 1)
            norm_pool(pool, "n0")
            pool.wait_ge(S("par_in"), 16 * 12)
            g_.tensor_scalar(head_gain[:, 0:1], head_gain[:, 0:1], HD ** -0.5, None, ALU.mult).then_inc(S("hgain"), 1)
            pool.wait_ge(S("ssq"), NT + 1)
            g_.tensor_scalar(ssq[:], ssq[:], 1.0 / HD, EPS, ALU.mult, ALU.add).then_inc(S("ssq_ms"), 1)
            pool.wait_ge(S("ssq_ms"), 1)
            g_.tensor_tensor(ssq[:], ssq[:], split(nhalf[:, 0:NT * (HEADS + 1)], NT, HEADS + 1), ALU.pow).then_inc(S("ssq_rstd"), 1)
            for i in range(NT):
                pool.wait_ge(S("y_sq"), 2 * i + 2)
                g_.tensor_scalar(ssg[:], ssg[:], 1.0 / (DI // SG), EPS, ALU.mult, ALU.add).then_inc(S("y_ms"), 1)
                pool.wait_ge(S("y_ms"), i + 1)
                g_.tensor_tensor(ssg[:], ssg[:], nhalf[:, 0:2], ALU.pow).then_inc(S("y_rstd"), 1)
            pool.wait_ge(S("qk_out"), NT + 2)
            pool.wait_ge(S("T_in0"), 16)
            pool.wait_ge(S("y_gated"), NT)
            pool.wait_ge(S("yd_mm"), NT)
            even_att.pool(pool)

        def heads_bc(ap, w):
            return ap.unsqueeze(2).broadcast_to((P, ap.shape[1], w))

        def even_dve(dve, link):
            v_ = nc.vector
            norm_dve(dve, "n0", 1)
            dve.wait_ge(S("ep_ev"), J_IW + 1)
            for u, (i, h) in enumerate(SC):
                L = (i + 1) * P
                dve.wait_ge(S("ix_relu"), u + 1)
                sc = score[:, i - 1, 0:L]
                v_.scalar_tensor_tensor(sc, relu[:, u % 2, 0:L], iw[:, i, h:h + 1],
                                        score_base[:, SEQ - L:] if h == 0 else sc, ALU.mult, ALU.add).then_inc(S("ix_acc"), 1)
                dve.wait_ge(S("ix_acc"), u + 1)
            for i in range(1, NT):
                L = (i + 1) * P
                sc = score[:, i - 1, 0:L]
                with dve.Fori(0, TOPK // 16) as r:
                    link.enter(r, 4)
                    for _ in range(2):
                        link(v_.max(m8[:], sc))
                        link(v_.match_replace(sc, m8[:], sc, TAKEN))
                    link.leave(TOPK // 16)
                v_.tensor_scalar(selm[:, i, 0:L], sc, TAKEN / 2, NEG, ALU.is_gt, ALU.mult).then_inc(S("selm"), 1)
            dve.wait_ge(S("ep_ev"), J_XBC + CT)
            dve.wait_ge(S("par_in"), 16 * 12)
            with dve.Fori(0, CT) as c:
                link.enter(c, TAPS - 1)
                o = xbcS[:, bass.ds(c, 1), :]
                for k in range(TAPS):
                    x_ = xbcT[:, bass.ds(c, 1), k:k + SEQ]
                    w_ = conv_w[:, k, bass.ds(c, 1)]
                    if k == 0:
                        link(v_.tensor_scalar(o, x_, w_, None, ALU.mult))
                    else:
                        ins_ = v_.scalar_tensor_tensor(o, x_, w_, o, ALU.mult, ALU.add)
                        if k < TAPS - 1:
                            link(ins_)
                        else:
                            ins_.then_inc(S("conv"), 1)
                link.leave(CT)
            dve.wait_ge(S("sq"), 1)
            v_.tensor_reduce(ssq[:, :, HEADS:HEADS + 1], split(junk[:, 0:NT * HD], NT, HD), AX.X, ALU.add).then_inc(S("ssq"), 1)
            for i in range(NT):
                dve.wait_ge(S("sq"), i + 2)
                v_.tensor_reduce(ssq[:, i, 0:HEADS], split(junk, HEADS, HD), AX.X, ALU.add).then_inc(S("ssq"), 1)
            link(v_.tensor_tensor(dt[:], kvd[:, :, 2 * HD:], dt_bias[:].unsqueeze(1).broadcast_to((P, NT, SH)), ALU.add))
            link(v_.tensor_scalar(dt_e[:], dt[:], -1.0, None, ALU.mult))
            v_.tensor_tensor(dt_e[:], dt_e[:], dt[:], ALU.max).then_inc(S("dt_abs"), 1)
            dve.wait_ge(S("ssq_rstd"), 1)
            for q in range(2):
                v_.tensor_tensor(krn[:, :, q * HD:(q + 1) * HD], kvd[:, :, 0:HD],
                                 ssq[:, :, HEADS:HEADS + 1].broadcast_to((P, NT, HD)), ALU.mult).then_inc(S("kn"), 1)
            for i in range(NT):
                q_ = split(qrows[:, i, :], HEADS, HD)
                v_.tensor_tensor(q_, q_, heads_bc(ssq[:, i, 0:HEADS], HD), ALU.mult).then_inc(S("qn"), 1)
            dve.wait_ge(S("dt_ln"), 1)
            link(v_.scalar_tensor_tensor(dt[:], dt[:], 0.0, dt_e[:], ALU.max, ALU.add))
            dve.wait_ge(S("a_exp"), 1)
            v_.scalar_tensor_tensor(dA[:], dt[:], -1.0, a_log[:].unsqueeze(1).broadcast_to((P, NT, SH)),
                                    ALU.mult, ALU.mult).then_inc(S("dA"), 1)
            dve.wait_ge(S("acum_mm"), 1)
            v_.tensor_copy(acum[:], split(bank[3][:, 0:NT * SH], NT, SH)).then_inc(S("acum"), 1)
            dve.wait_ge(S("acum"), 1)
            dve.wait_ge(S("eac"), 1)
            dve.wait_ge(S("z_silu"), 1)
            dve.wait_ge(S("ssm_gain_in"), 16)
            for i in range(NT):
                for g in range(SG):
                    dve.wait_ge(S("abc_mm"), 2 * i + g + 1)
                    link(v_.tensor_copy(alast[:, 4 * g:4 * g + 4], split(bank[6 + g][:, :], 4, P)[:, :, P - 1]))
                v_.tensor_tensor(to_end[:], alast[:], acum[:, i, :], ALU.subtract).then_inc(S("alast"), 1)
                if i >= 1:
                    dve.wait_ge(S("yd_mm"), i)
                for g in range(SG):
                    for h in range(4):
                        hh = 4 * g + h
                        ins_ = v_.tensor_scalar(seg[:, g, h, :], bank[6 + g][:, h * P:(h + 1) * P],
                                                acum[:, i, hh:hh + 1], 0.0, ALU.subtract, ALU.min)
                    ins_.then_inc(S("seg"), 1)
                dve.wait_ge(S("cb_mm"), i + 1)
                v_.tensor_tensor(cbm, split(bank[3][:, 0:SG * P], SG, P), tri[:].unsqueeze(1).broadcast_to((P, SG, P)),
                                 ALU.mult).then_inc(S("cbm"), 1)
                dve.wait_ge(S("tok_out"), 2 * i + 1)
                link(v_.tensor_tensor(split(xdt, SH, SD), split(xtok[:, i, :], SH, SD), heads_bc(dt[:, i, :], SD), ALU.mult))
                dve.wait_ge(S("ends"), 2 * i + 2)
                if i < NT - 1:
                    if i >= 1:
                        dve.wait_ge(S("st_mm"), i)
                    v_.tensor_tensor(split(xw, SH, SD), split(xdt, SH, SD), heads_bc(to_end[:], SD), ALU.mult).then_inc(S("xw"), 1)
                for g in range(SG):
                    dve.wait_ge(S("decay"), 2 * i + g + 1)
                    dve.wait_ge(S("cbm"), i + 1)
                    v_.tensor_tensor(seg[:, g], seg[:, g], cbm[:, g:g + 1, :].broadcast_to((P, 4, P)), ALU.mult).then_inc(S("mt"), 1)
                link(v_.tensor_tensor(split(y2, SH, SD), split(xtok[:, i, :], SH, SD), heads_bc(d_skip[:], SD), ALU.mult))
                if i >= 1:
                    dve.wait_ge(S("yoff_mm"), i)
                    dve.wait_ge(S("ssm_row"), i)
                    link(v_.tensor_tensor(split(y_t, SH, SD), split(bank[1][:, :], SH, SD), heads_bc(eac[:, i, :], SD), ALU.mult))
                    link(v_.tensor_tensor(y2, y2, y_t, ALU.add))
                if i < NT - 1:
                    dve.wait_ge(S("st_mm"), i + 1)
                    if i == 0:
                        v_.tensor_copy(state, bank[2][:, :]).then_inc(S("state"), 1)
                    else:
                        link(v_.tensor_tensor(split(state, SH, SD), split(state, SH, SD), heads_bc(cdecay[:], SD), ALU.mult))
                        v_.tensor_tensor(state, state, bank[2][:, :], ALU.add).then_inc(S("state"), 1)
                dve.wait_ge(S("yd_mm"), i + 1)
                link(v_.tensor_tensor(y2, y2, bank[0][:, :], ALU.add))
                v_.tensor_tensor(y_t, y2, z[:, i, :], ALU.mult).then_inc(S("y_gated"), 1)
                dve.wait_ge(S("y_rstd"), i + 1)
                for g in range(SG):
                    cs = slice(g * 256, (g + 1) * 256)
                    ins_ = v_.scalar_tensor_tensor(rows_m[:, 0, i, cs], y_t[:, cs], ssg[:, g:g + 1], ssm_gain[:, cs],
                                                   ALU.mult, ALU.mult)
                ins_.then_inc(S("ssm_row"), 1)
            dve.wait_ge(S("T_in0"), 16)
            even_att.dve(dve, link)
            for i in range(NT):
                turn_evac(dve, "eo", mixT, i, 1)
            outproj_dve(dve, "eo")

        @contextmanager
        def loop_pairs(eng, link=None):
            with eng.Fori(0, HEADS // 4) as it:
                if link:
                    link.enter(it, M)
                yield it, it
                if link:
                    link.leave(HEADS // 4)

        def flat(ap):
            return ap.rearrange("p a b -> p (a b)")

        def even_finish(a, dve, link, it, s, m, i):
            link(nc.vector.reciprocal(a.coef[:, m % 2, :], a.sums[:, m % 2, :]))
            o = rows_m[:, 1, i, :].rearrange("p (j q d) -> p j q d", q=2, d=HD)[:, bass.ds(2 * it + s, 1), :, :]
            return nc.vector.tensor_tensor(o, split(bank[4 + m % 2][:, 0:2 * HD], 1, 2, HD),
                                           a.coef[:, m % 2, :].unsqueeze(1).unsqueeze(3).broadcast_to((P, 1, 2, HD)), ALU.mult)

        def tile_bias(i):
            return slice(SEQ - P - i * P, SEQ - P - i * P + (i + 1) * P)

        even_branches = [[dict(L=(i + 1) * P, D=HD, bias=lambda b, i=i, q=q: b[:, q, tile_bias(i)],
                               k=lambda it, i=i, q=q: (kA, kB)[q][:, 0:(i + 1) * P],
                               mask=selm[:, i, 0:(i + 1) * P] if i else None,
                               v=lambda it, kt: kvd[:, kt, HD:2 * HD]) for q in range(2)] for i in range(NT)]
        even_att = Attention("ea", even_branches, loop_pairs, HEADS // 4,
                             [at(O_XBCS + n * SEQ, SEQ) for n in range(STAGES)],
                             [at(O_XBCS + STAGES * SEQ + n * 2 * TW, 2, TW) for n in range(STAGES)],
                             lambda it, s: flat(eqT[:, bass.ds(2 * it + s, 1), :]),
                             lambda it, s: split(arena[:, 0:HEADS * TW], HEADS // 2, 2, TW)[:, bass.ds(2 * it + s, 1), :, :],
                             O_EW, even_finish)

        o0 = HEADS * TW
        oqT = at(o0, HEADS, SEQ); o0 += HEADS * SEQ
        O_KROWS = o0
        krows = at(o0, 2, NT, OKV); o0 += 2 * NT * OKV
        kT = at(o0, 2, OG, SEQ); o0 += 2 * OG * SEQ
        vv = at(o0, 2, NT, OKV); o0 += 2 * NT * OKV
        O_CT = o0
        cT = at(o0, 2, OG, SEQ); o0 += 2 * OG * SEQ
        blk = [at(o0 + q * OG * CB * NC, CB, OG * NC) for q in range(2)]
        ojunk = at(o0, DM)
        o_work = o0
        o0 += 2 * OG * CB * NC
        O_OW = 2 * EW
        cw2 = at(o0, 2, OD); o0 += 2 * OD
        kcT = at(o0, OG, NC); o0 += OG * NC
        kc_rows, kc_sq, vc = (split(arena[0:NC, o0 + n * OG * OD:o0 + (n + 1) * OG * OD], OG, OD) for n in range(3))
        o0 += 3 * OG * OD
        assert o0 <= O_OW and 6 * SEQ <= 2 * OG * CB * NC and STAGES * TW <= 2 * NT * OKV and STAGES * SEQ <= 2 * OG * SEQ
        ow = [at(O_OW + n * KD * 512, KD, 512) for n in range(3)]
        cw1 = [at(O_OW + n * KD * 512, CB, OD) for n in range(3)]
        o_wo = [hT, ow[0]]
        gl = sb("gl", [P, NT, 3, HEADS])
        gates = sb("gates", [P, NT, HEADS, 3])
        oss = sb("oss", [P, NT, HEADS + 4])
        qk_gain = sb("qk_gain", [P, 4])
        posT = sb("posT", [P, 2, CB])
        hidT_c = sb("hidT_c", [P, 2, OG * NC])
        kc_ss = sb("kc_ss", [NC, OG])

        w_odd = ins["odd_w_in"][0]
        OD_CHUNKS = [[(C_OK, 512)], [(C_OK + 512, 256), (C_OK + 1024, 256)], [(C_OK + 768, 256), (C_OK + 1280, 256)],
                     [(0, 512)], [(512, 512)], [(C_GL, 3 * HEADS)]]
        K_C, K_K, K_V, K_Q, K_G, K_END = 0, 4, 8, 12, 20, 21
        OD_JOBS = [4, 8, 12, 16, 20, 21]

        def odd_sp(sp):
            sp.wait_ge(S("m_x"), 2 * NT)
            sp.dma_start(gain[:], bcast_rows(ins["attn_norm"][1, :], DM)).then_inc(S("gain_in"), 16)
            for c in range(3):
                load_chunk(sp, c, OD_CHUNKS, w_odd, ow, "op", OD_JOBS)
            for n, name in enumerate(("odd_q_norm", "odd_ks_norm", "odd_kw_norm", "odd_kc_norm")):
                sp.dma_start(qk_gain[:, n:n + 1], ins[name][0].rearrange("(p c) -> p c", c=1)).then_inc(S("opar_in"), 16)
            for n, name in enumerate(("odd_cmp_pos_k", "odd_cmp_pos_v")):
                sp.dma_start(posT[:, n, :], ins[name][0].rearrange("r d -> d r")).then_inc(S("opar_in"), 16)
            for n, name in enumerate(("odd_cmp_k_w2", "odd_cmp_v_w2")):
                sp.dma_start(cw2[:, n, :], ins[name][0]).then_inc(S("opar_in"), 16)
            for c in range(3, 6):
                load_chunk(sp, c, OD_CHUNKS, w_odd, ow, "op", OD_JOBS)
            load_bias(sp, "T_in1")
            for n, name in enumerate(("odd_cmp_k_w1", "odd_cmp_v_w1")):
                sp.wait_ge(S("op_mm"), past("op_mm") + OD_JOBS[3 + n])
                sp.dma_start(cw1[n], ins[name][0].rearrange("(r d) h -> d r h", d=OD)).then_inc(S(f"cw1_in{n}"), 16)
            sp.wait_ge(S("op_mm"), past("op_mm") + K_END)
            sp.dma_start(o_wo[0], ins["odd_w_out"][0, :, 0:512].rearrange("(k p) c -> p k c", p=P)).then_inc(S("oo_w0"), 16)
            sp.wait_ge(S("c_hid"), past("c_hid") + 2)
            sp.dma_start(o_wo[1], ins["odd_w_out"][0, :, 512:1024].rearrange("(k p) c -> p k c", p=P)).then_inc(S("oo_w1"), 16)

        def odd_pe(pe):
            turn_pe(pe, "n2", lambda i, k: rows[:, i, k * P:(k + 1) * P], lambda e, i: rows_ready(e, "n2", i + 1))
            turned(pe, "n2")

            def job(n, runs):
                if n >= 4:
                    pe.wait_ge(S("op_ev"), past("op_ev") + n - 3)
                for o, lhs, rhs in runs:
                    for k in range(KD):
                        mm = nc.tensor.matmul(o, lhs(k), rhs(k), start=(k == 0), stop=(k == KD - 1))
                mm.then_inc(S("op_mm"), 1)

            def tokens(n, w, i, cols):
                job(n, [(bank[n % 4][:, 0:cols], lambda k: hT[:, k, i * P:(i + 1) * P], lambda k: w[:, k, 0:cols])])

            pe.wait_ge(S("op_w0"), past("op_w0") + 16)
            for j in range(4):
                job(K_C + j, [(bank[j][:, :], lambda k: ow[0][:, k, j * P:(j + 1) * P], lambda k: hT[:, k, :])])
            for c, first in ((1, K_K), (2, K_V)):
                pe.wait_ge(S(f"op_w{c}"), past(f"op_w{c}") + 32)
                for i in range(NT):
                    tokens(first + i, ow[c], i, 512)
            for c in range(2):
                pe.wait_ge(S(f"op_w{3 + c}"), past(f"op_w{3 + c}") + 16)
                for i in range(NT):
                    tokens(K_Q + 4 * c + i, ow[c], i, 512)
            pe.wait_ge(S("op_w5"), past("op_w5") + 16)
            job(K_G, [(bank[K_G % 4][:, i * 3 * HEADS:(i + 1) * 3 * HEADS], lambda k, i=i: hT[:, k, i * P:(i + 1) * P],
                       lambda k: ow[2][:, k, 0:3 * HEADS]) for i in range(NT)])
            pe.wait_ge(S("op_ev"), past("op_ev") + K_END)

            for q in range(2):
                pe.wait_ge(S(f"cw1_in{q}"), past(f"cw1_in{q}") + 16)
                pe.wait_ge(S("blk"), past("blk") + 2 * q + 2)
                for r in range(CB):
                    mm = nc.tensor.matmul(bank[6 + q][:, 0:OG * NC], cw1[q][:, r, :], blk[q][:, r, :],
                                          start=(r == 0), stop=(r == CB - 1))
                mm.then_inc(S("c_hid"), 1)
            for i in range(NT):
                pe.wait_ge(S("ok_n"), past("ok_n") + 2 * i + 2)
                for q in range(2):
                    n = 2 * i + q
                    if n >= 2:
                        pe.wait_ge(S("ok_out"), past("ok_out") + n - 1)
                    for g in range(OG):
                        mm = nc.tensor.transpose(bank[n % 2][:, g * P:(g + 1) * P], krows[:, q, i, g * OD:(g + 1) * OD], ident[:])
                    mm.then_inc(S("ok_turned"), 1)
            for i in range(NT):
                pe.wait_ge(S("oq_n"), past("oq_n") + i + 1)
                for half in range(2):
                    n = 2 * i + half
                    if n >= 2:
                        pe.wait_ge(S("oq_out"), past("oq_out") + n - 1)
                    for j in range(4):
                        c = (4 * half + j) * P
                        mm = nc.tensor.transpose(bank[2 + n % 2][:, j * P:(j + 1) * P], rows[:, i, c:c + P], ident[:])
                    mm.then_inc(S("oq_turned"), 1)
            for q in range(2):
                pe.wait_ge(S("hid_c"), past("hid_c") + q + 1)
                for g in range(OG):
                    mm = nc.tensor.matmul(bank[4 + q][0:NC, g * P:(g + 1) * P], hidT_c[:, q, g * NC:(g + 1) * NC],
                                          cw2[:, q, :], start=True, stop=True)
                mm.then_inc(S("c_rows"), 1)
            pe.wait_ge(S("kc_n"), past("kc_n") + 1)
            for g in range(OG):
                mm = nc.tensor.transpose(bank[7][:, g * NC:(g + 1) * NC], kc_rows[:, g, :], ident[0:NC, 0:NC])
            mm.then_inc(S("kc_turned"), 1)
            pe.wait_ge(S("kcT"), past("kcT") + 1)
            pe.wait_ge(S("ok_out"), past("ok_out") + 2 * NT)
            pe.wait_ge(S("oq_out"), past("oq_out") + 2 * NT)
            odd_att.pe(pe)
            odd_att.done(pe)
            turn_pe(pe, "oo", lambda i, k: rows[:, i, k * P:(k + 1) * P], lambda e, i: None)
            outproj_pe(pe, "oo", mixT, o_wo, None)

        def odd_act(act):
            norm_act(act, "n2", lambda e: e.wait_ge(S("m_x"), 2 * NT))
            for i in range(NT):
                turn_evac(act, "n2", hT, i, 0)

            def ev(n, dst, src):
                act.wait_ge(S("op_mm"), past("op_mm") + n + 1)
                nc.scalar.activation(dst, src, ACT.Copy).then_inc(S("op_ev"), 1)
            for j in range(4):
                ev(K_C + j, cT[:, j // 2, j % 2, :], bank[j][:, :])
            for dst, first in ((krows, K_K), (vv, K_V)):
                for i in range(NT):
                    ev(first + i, dst[:, :, i, :], split(bank[(first + i) % 4][:, :], 2, OKV))
            turned(act, "n2")
            for c in range(2):
                for i in range(NT):
                    n = K_Q + 4 * c + i
                    ev(n, rows[:, i, c * 512:(c + 1) * 512], bank[n % 4][:, :])
            ev(K_G, gl[:], bank[K_G % 4][:, 0:NT * 3 * HEADS].rearrange("p (i b h) -> p i b h", i=NT, b=3))
            for q in range(2):
                act.wait_ge(S("c_hid"), past("c_hid") + q + 1)
                nc.scalar.activation(hidT_c[:, q, :], bank[6 + q][:, 0:OG * NC], ACT.Silu).then_inc(S("hid_c"), 1)
            act.wait_ge(S("op_ev"), past("op_ev") + K_END)
            nc.scalar.activation(gl[:], gl[:], ACT.Exp, scale=-1.0).then_inc(S("gl_exp"), 1)
            act.wait_ge(S("opar_in"), past("opar_in") + 16 * 8)
            for i in range(NT):
                for q in range(2):
                    act.wait_ge(S("ok_turned"), past("ok_turned") + 2 * i + q + 1)
                    nc.scalar.activation(kT[:, q, :, i * P:(i + 1) * P], split(bank[q][:, 0:2 * P], OG, P), ACT.Copy,
                                         scale=qk_gain[:, 1 + q:2 + q]).then_inc(S("ok_out"), 1)
            act.wait_ge(S("qscale"), past("qscale") + 1)
            for i in range(NT):
                for half in range(2):
                    act.wait_ge(S("oq_turned"), past("oq_turned") + 2 * i + half + 1)
                    nc.scalar.activation(oqT[:, 4 * half:4 * half + 4, i * P:(i + 1) * P], split(bank[2 + half][:, :], 4, P),
                                         ACT.Copy, scale=qk_gain[:, 0:1]).then_inc(S("oq_out"), 1)
            act.wait_ge(S("c_rows"), past("c_rows") + 1)
            nc.scalar.activation(kc_rows, split(bank[4][0:NC, 0:OG * OD], OG, OD), ACT.Copy).then_inc(S("kc_raw"), 1)
            act.wait_ge(S("c_rows"), past("c_rows") + 2)
            nc.scalar.activation(vc, split(bank[5][0:NC, 0:OG * OD], OG, OD), ACT.Copy).then_inc(S("kc_raw"), 1)
            act.wait_ge(S("kc_turned"), past("kc_turned") + 1)
            nc.scalar.activation(kcT, split(bank[7][:, 0:OG * NC], OG, NC), ACT.Copy, scale=qk_gain[:, 3:4]).then_inc(S("kcT"), 1)
            odd_att.act(act)
            for i in range(NT):
                turn_evac(act, "oo", mixT, i, 0)

        def odd_pool(pool):
            g_ = nc.gpsimd
            norm_pool(pool, "n2")
            pool.wait_ge(S("opar_in"), past("opar_in") + 16 * 8)
            g_.tensor_scalar(qk_gain[:, 0:1], qk_gain[:, 0:1], OD ** -0.5, None, ALU.mult).then_inc(S("qscale"), 1)
            pool.wait_ge(S("oss"), past("oss") + 3 * NT)
            g_.tensor_scalar(oss[:], oss[:], 1.0 / OD, EPS, ALU.mult, ALU.add).then_inc(S("oss_ms"), 1)
            pool.wait_ge(S("oss_ms"), past("oss_ms") + 1)
            g_.tensor_tensor(oss[:, 0:2], oss[:, 0:2], split(nhalf[:, 0:2 * 12], 2, 12), ALU.pow).then_inc(S("oss_rstd"), 1)
            g_.tensor_tensor(oss[:, 2:4], oss[:, 2:4], split(nhalf[:, 0:2 * 12], 2, 12), ALU.pow).then_inc(S("oss_rstd"), 1)
            pool.wait_ge(S("kc_ss"), past("kc_ss") + 1)
            g_.tensor_scalar(kc_ss[:], kc_ss[:], 1.0 / OD, EPS, ALU.mult, ALU.add).then_inc(S("kc_ms"), 1)
            pool.wait_ge(S("kc_ms"), past("kc_ms") + 1)
            g_.tensor_tensor(kc_ss[:], kc_ss[:], nhalf[0:NC, 0:OG], ALU.pow).then_inc(S("kc_rstd"), 1)
            pool.wait_ge(S("oq_out"), past("oq_out") + 2 * NT)
            pool.wait_ge(S("T_in1"), past("T_in1") + 16)
            pool.wait_ge(S("ok_turned"), past("ok_turned") + 2 * NT)
            pool.wait_ge(S("blk"), past("blk") + 4)
            odd_att.pool(pool)

        def odd_dve(dve, link):
            v_ = nc.vector
            norm_dve(dve, "n2", 3)
            for i in range(NT):
                dve.wait_ge(S("op_ev"), past("op_ev") + K_K + i + 1)
                for q in range(2):
                    k_ = krows[:, q, i, :]
                    link(v_.tensor_tensor(ojunk[:, 0:OKV], k_, k_, ALU.mult))
                    ins_ = v_.tensor_reduce(oss[:, i, HEADS + 2 * q:HEADS + 2 * q + 2], split(ojunk[:, 0:OKV], OG, OD), AX.X, ALU.add)
                    if q == 0:
                        link(ins_)
                    else:
                        ins_.then_inc(S("oss"), 1)
                        dve.wait_ge(S("oss"), past("oss") + i + 1)
            for c in range(2):
                for i in range(NT):
                    dve.wait_ge(S("op_ev"), past("op_ev") + K_Q + 4 * c + i + 1)
                    q_ = rows[:, i, c * 512:(c + 1) * 512]
                    link(v_.tensor_tensor(ojunk[:, 0:512], q_, q_, ALU.mult))
                    v_.tensor_reduce(oss[:, i, 4 * c:4 * c + 4], split(ojunk[:, 0:512], 4, OD), AX.X, ALU.add).then_inc(S("oss"), 1)
                    dve.wait_ge(S("oss"), past("oss") + NT + 4 * c + i + 1)
            dve.wait_ge(S("opar_in"), past("opar_in") + 16 * 8)
            for q in range(2):
                for g in range(OG):
                    src = cT[:, q, g, :]
                    win = bass.AP(src.tensor, src.offset, [list(src.ap[0]), [1, CB], [CS, NC]])
                    v_.tensor_tensor(blk[q][:, :, g * NC:(g + 1) * NC], win,
                                     posT[:, q, :].unsqueeze(2).broadcast_to((P, CB, NC)), ALU.add).then_inc(S("blk"), 1)
            dve.wait_ge(S("oss_rstd"), past("oss_rstd") + 2)
            for i in range(NT):
                for q in range(2):
                    k_ = split(krows[:, q, i, :], OG, OD)
                    v_.tensor_tensor(k_, k_, heads_bc(oss[:, i, HEADS + 2 * q:HEADS + 2 * q + 2], OD), ALU.mult).then_inc(S("ok_n"), 1)
            for i in range(NT):
                q_ = split(rows[:, i, :], HEADS, OD)
                v_.tensor_tensor(q_, q_, heads_bc(oss[:, i, 0:HEADS], OD), ALU.mult).then_inc(S("oq_n"), 1)
            dve.wait_ge(S("gl_exp"), past("gl_exp") + 1)
            link(v_.tensor_scalar(gl[:], gl[:], 1.0, None, ALU.add))
            link(v_.reciprocal(gates[:].rearrange("p i h b -> p i b h"), gl[:]))
            dve.wait_ge(S("kc_raw"), past("kc_raw") + 1)
            link(v_.tensor_tensor(kc_sq, kc_rows, kc_rows, ALU.mult))
            v_.tensor_reduce(kc_ss[:].unsqueeze(2), kc_sq, AX.X, ALU.add).then_inc(S("kc_ss"), 1)
            dve.wait_ge(S("kc_rstd"), past("kc_rstd") + 1)
            v_.tensor_tensor(kc_rows, kc_rows, kc_ss[:].unsqueeze(2).broadcast_to((NC, OG, OD)), ALU.mult).then_inc(S("kc_n"), 1)
            dve.wait_ge(S("T_in1"), past("T_in1") + 16)
            odd_att.dve(dve, link)
            for i in range(NT):
                turn_evac(dve, "oo", mixT, i, 1)
            outproj_dve(dve, "oo")

        @contextmanager
        def loop_heads(eng, link=None):
            links = 6 * M
            per = HPG // STAGES
            with eng.Fori(0, OG) as g:
                with eng.Fori(0, per) as n:
                    it = g * per + n
                    if link:
                        link.enter(it, links)
                    yield it, (g, it)
                    if link:
                        link.leave(1)
                        link.n -= links
            if link:
                link.n += OG * per * links

        def odd_finish(a, dve, link, v, s, m, i):
            h = bass.ds(2 * v[1] + s, 1)
            c_ = a.coef[:, m % 2, :]
            link(nc.vector.tensor_scalar(c_, a.sums[:, m % 2, :], 1e-30, None, ALU.max))
            link(nc.vector.reciprocal(c_, c_))
            link(nc.vector.tensor_tensor(c_, c_, flat(gates[:, i, h, :]), ALU.mult))
            y = flat(split(rows[:, i, :], HEADS, OD)[:, h, :])
            b_ = bank[4 + m % 2]
            link(nc.vector.tensor_scalar(y, b_[:, 0:OD], c_[:, 0:1], None, ALU.mult))
            link(nc.vector.scalar_tensor_tensor(y, b_[:, OD:2 * OD], c_[:, 1:2], y, ALU.mult, ALU.add))
            return nc.vector.scalar_tensor_tensor(y, b_[:, 2 * OD:3 * OD], c_[:, 2:3], y, ALU.mult, ALU.add)

        def o_compressed(i):
            u0 = tile_bias(i).start + CB - 1
            return dict(L=NC, D=OD, clamp=True, bias=lambda b: b[:, u0:u0 + CS * (NC - 1) + 1:CS],
                        k=lambda v: flat(kcT[:, bass.ds(v[0], 1), :]),
                        v=lambda v, kt: flat(vc[:, bass.ds(v[0], 1), :]))

        def o_branch(i, q):
            return dict(L=(i + 1) * P, D=OD, bias=lambda b: b[:, tile_bias(i)],
                        k=lambda v: flat(kT[:, q, bass.ds(v[0], 1), 0:(i + 1) * P]),
                        v=lambda v, kt: flat(split(vv[:, q, kt, :], OG, OD)[:, bass.ds(v[0], 1), :]))

        odd_att = Attention("oa", [[o_compressed(i), o_branch(i, 0), o_branch(i, 1)] for i in range(NT)],
                            loop_heads, HEADS // STAGES,
                            [at(O_CT + n * SEQ, SEQ) for n in range(STAGES)],
                            [at(O_KROWS + n * TW, TW) for n in range(STAGES)],
                            lambda v, s: flat(oqT[:, bass.ds(2 * v[1] + s, 1), :]),
                            lambda v, s: flat(T[:, bass.ds(2 * v[1] + s, 1), :]),
                            o_work, odd_finish, before=even_att)

        router_w = [sb(f"router_w{n}", [P, KD, NR]) for n in range(2)]
        dest = sb("dest", [P, 2, NT], I32)
        weight = sb("weight", [P, 2, NT])
        more_i = sb("more_i", [P, 1 + NX], I32)
        slot_rows = sb("slot_rows", [NBLK, P])
        slot_idx = sb("slot_idx", [P, NBLK], I32)
        idx_now = sb("idx_now", [P, RING], I32)
        xe = at(O_HT, RING, 512)
        xeT = at(O_HT + RING * 512, RING, 4, P)
        hidT = at(O_HT + 2 * RING * 512, 2, P)
        act_g = at(O_ROWS, FH)
        hid = at(O_ROWS + FH, FH)
        yb = at(O_ROWS + 2 * FH, RING, 512)
        y_rows = at(O_HT, 2, NT, DM)
        wgu = [at(u * EW, 2, KD, FF) for u in range(RING)]
        wd = [at(u * EW + 2 * KD * FF, FF // P, DM) for u in range(RING)]
        r0 = 2 * EW
        lgt = at(r0, NT, NR); r0 += NT * NR
        cand = at(r0, NT, EPG); r0 += NT * EPG
        eqs = at(r0, NT, EPG); r0 += NT * EPG
        oh_g = at(r0, NT, MG); r0 += NT * MG
        es = at(r0, NT, EPG); r0 += NT * EPG
        oh_e = at(r0, 2, NT, EPG); r0 += 2 * NT * EPG
        prod = at(r0, 2 * NT, NE); r0 += 2 * NT * NE
        oh = at(r0, 2, NT, NE); r0 += 2 * NT * NE
        oh_sum = at(r0, NT, NE); r0 += NT * NE
        before = at(r0, NT, NE); r0 += NT * NE
        load = at(r0, NE); r0 += NE
        xn = at(r0, NE); r0 += NE
        xend = at(r0, NE); r0 += NE
        xrow = at(r0, NE); r0 += NE
        cmp_ = at(r0, NE, MORE); r0 += NE * MORE
        cmpx = at(r0, NX, NE); r0 += NX * NE
        more_f = at(r0, 1 + NX); r0 += 1 + NX
        small = at(r0, 12, NT); r0 += 12 * NT
        pos = at(r0, 2 * NT); r0 += 2 * NT
        base = at(r0, 2 * NT); r0 += 2 * NT
        xbase = at(r0, 2 * NT); r0 += 2 * NT
        over = at(r0, 2 * NT); r0 += 2 * NT
        onesr = at(r0, NE); r0 += NE

        def weights(sp, t, layer, e, u):
            for n, name in enumerate(("moe_w_gate", "moe_w_up")):
                src = ins[name][layer, bass.ds(e, 1)].rearrange("e (h p j) f -> p (e h) (j f)", h=2, j=4)
                sp.dma_start(wgu[u][:, n].rearrange("p (h j) f -> p h (j f)", h=2), src).then_inc(S(f"{t}_wgu{u}"), 16)
            src = ins["moe_w_down"][layer, bass.ds(e, 1)].rearrange("e (h p j) d -> p (e h) (j d)", h=2, j=2)
            sp.dma_start(wd[u].rearrange("p (h j) d -> p h (j d)", h=2), src).then_inc(S(f"{t}_wd{u}"), 16)

        def turn_rows(u):
            for j in range(4):
                mm = nc.tensor.transpose(bank[0][:, j * P:(j + 1) * P], xe[:, u, j::4], ident[:])
            return mm

        def copy_x(u):
            return nc.scalar.activation(xeT[:, u], split(bank[0][:, :], 4, P), ACT.Copy)

        def gate_up_mms(u):
            for n in range(KD):
                half, j = n // 4, n % 4
                for fh in range(2):
                    mm = nc.tensor.matmul(bank[1][fh * CAP:(fh + 1) * CAP, :], xeT[:, u, j, half * CAP:(half + 1) * CAP],
                                          wgu[u][:, :, n, fh * FH:(fh + 1) * FH], start=(n == 0), stop=(n == KD - 1))
            return mm

        def turn_hidden():
            for j in range(2):
                mm = nc.tensor.transpose(bank[2][:, j * P:(j + 1) * P], hid[:, j::2], ident[:])
            return mm

        def down_mms(u):
            for n in range(FF // P):
                fh, j = n // 2, n % 2
                for dh in range(2):
                    mm = nc.tensor.matmul(bank[3][dh * CAP:(dh + 1) * CAP, :], hidT[:, j, fh * CAP:(fh + 1) * CAP],
                                          wd[u][:, n, dh * 512:(dh + 1) * 512], start=(n == 0), stop=(n == FF // P - 1))
            return mm

        def store_y(act, t, layer, u, blk_n):
            d = y_d[layer].rearrange("(b s) (h c) -> b h s c", s=CAP, h=2)[bass.ds(blk_n, 1)]
            for h in range(2):
                act.dma_start(d[:, h].rearrange("b s c -> (b s) c"), yb[h * CAP:(h + 1) * CAP, u, :]).then_inc(S(f"{t}_yout{u}"), 16)

        X_TURN, X_XT, X_GU, X_G, X_HID, X_HTURN, X_HT, X_DN, X_Y = range(1, 10)
        X_STEPS = 9

        def x_step(eng, x, j, step):
            eng.wait_ge(S(f"{x}_step"), j * X_STEPS + 1 + step)

        def gather(pool, t, layer, c, u, col):
            pool.wait_ge(S(f"{t}_idx"), c + 1)
            nc.gpsimd.tensor_copy(idx_now[:, u:u + 1], slot_idx[:, bass.ds(col, 1)]).then_inc(S(f"{t}_idx"), 1)
            wait_apart(pool, (S(f"{t}_idx"), c + 2))
            nc.gpsimd.indirect_dma_start(
                out=xe[:, u, :], out_offset=None, in_=h_d[layer].rearrange("t (h c) -> (t h) c", h=2),
                in_offset=bass.IndirectOffsetOnAxis(ap=idx_now[:, u:u + 1], axis=0)).then_inc(S(f"{t}_xe{u}"), 16)

        def x_turn(pe, t, c, cu, u):
            pe.wait_ge(S(f"{t}_xe{u}"), 16 * (cu + 1))
            pe.wait_ge(S(f"{t}_xT"), c + 1)
            turn_rows(u).then_inc(S(f"{t}_xturn"), 1)

        def gate_up(pe, t, c, cu, u):
            pe.wait_ge(S(f"{t}_xT"), c + 2)
            pe.wait_ge(S(f"{t}_hid"), c + 1)
            pe.wait_ge(S(f"{t}_wgu{u}"), 32 * (cu + 1))
            gate_up_mms(u).then_inc(S(f"{t}_gu"), 1)

        def hid_turn(pe, t, c):
            pe.wait_ge(S(f"{t}_hid"), c + 2)
            turn_hidden().then_inc(S(f"{t}_hturn"), 1)

        def down(pe, t, c, cu, u):
            pe.wait_ge(S(f"{t}_hT"), c + 2)
            pe.wait_ge(S(f"{t}_y"), c + 1)
            pe.wait_ge(S(f"{t}_wd{u}"), 16 * (cu + 1))
            down_mms(u).then_inc(S(f"{t}_dn"), 1)

        def x_out(act, t, c, u):
            act.wait_ge(S(f"{t}_xturn"), c + RING + 1)
            copy_x(u).then_inc(S(f"{t}_xT"), 1)

        def silu(act, t, c):
            act.wait_ge(S(f"{t}_gu"), c + 1)
            act.wait_ge(S(f"{t}_hid"), c + 1)
            nc.scalar.activation(act_g, bank[1][:, 0:FH], ACT.Silu).then_inc(S(f"{t}_g"), 1)

        def y_out(act, t, layer, c, cu, u, blk_n):
            act.wait_ge(S(f"{t}_dn"), c + 2)
            act.wait_ge(S(f"{t}_yout{u}"), 16 * (cu + 1))
            nc.scalar.activation(yb[:, u, :], bank[3][:, :], ACT.Copy).then_inc(S(f"{t}_y"), 1)
            act.wait_ge(S(f"{t}_y"), c + 2)
            store_y(act, t, layer, u, blk_n)

        def hidden(dve, t, c):
            dve.wait_ge(S(f"{t}_g"), c + 1)
            dve.wait_ge(S(f"{t}_hturn"), c + 1)
            nc.vector.tensor_tensor(hid, act_g, bank[1][:, FH:2 * FH], ALU.mult).then_inc(S(f"{t}_hid"), 1)

        def hid_out(dve, t, c):
            dve.wait_ge(S(f"{t}_hturn"), c + 2)
            nc.vector.tensor_copy(hidT, split(bank[2][:, 0:2 * P], 2, P)).then_inc(S(f"{t}_hT"), 1)

        def per_expert(eng, L, body):
            with eng.Fori(0, TRIPS) as it:
                for u in range(RING):
                    body(it * RING + u, it * RING + u + L * NE, it + L * uses(u), u, False)
            for u in range(NE - RING * TRIPS):
                e = RING * TRIPS + u
                body(e, e + L * NE, TRIPS + L * uses(u), u, e == NE - 1)

        def uses(u):
            return TRIPS + (1 if u < NE - RING * TRIPS else 0)

        def e_next(cu, u, L):
            n = (u + 1) % RING
            return cu - L * uses(u) + L * uses(n) + (1 if n == 0 else 0)

        def fence(eng, t, L):
            for u in range(RING):
                eng.wait_ge(S(f"{t}_yout{u}"), 32 * uses(u) * (L + 1) + 16)

        def further(eng, t, layer, body, first=None, last=None, none=None):
            n = eng.value_load(more_i[0:1, 0:1], min_val=0, max_val=NX)
            with eng.If(n > 0):
                fence(eng, t, layer)
                if first:
                    first()
                with eng.Fori(0, NX) as j:
                    with eng.If(n > j):
                        body(j)
                    with eng.Else():
                        eng.nop()
                    eng.nop()
                if last:
                    last(n)
            with eng.Else():
                if none:
                    none()
                else:
                    eng.nop()
            eng.nop()

        def moe_sp(sp, L, mixed, prev_norm):
            t, x = "m", f"mx{L}"
            rows_ready(sp, prev_norm, NT)
            sp.dma_start(gain[:], bcast_rows(ins["ffn_norm"][L, :], DM)).then_inc(S("gain_in"), 16)
            sp.dma_start(router_w[L][:, :, 0:MG], ins["moe_router_group"][L].rearrange("(k p) g -> p k g", p=P)).then_inc(S(f"{t}_rw"), 16)
            for g in range(MG):
                sp.dma_start(router_w[L][:, :, MG + g * EPG:MG + (g + 1) * EPG],
                             ins["moe_router_expert"][L, g].rearrange("(k p) e -> p k e", p=P)).then_inc(S(f"{t}_rw"), 16)
            sp.wait_ge(S(f"{mixed}_add"), past(f"{mixed}_add") + 2 * NT)
            for u in range(2):
                weights(sp, t, L, u, u)
            rows_ready(sp, f"m{L}n", NT)
            sp.dma_start(h_d[L].rearrange("(i p) c -> p i c", p=P), rows).then_inc(S(f"{t}_h"), 16)
            sp.wait_ge(S(f"{t}_scat"), 16 * 2 * NT * (L + 1))
            for h in range(2):
                sp.dma_start(slot_rows[:, h * CAP:(h + 1) * CAP], slot_d[L].rearrange("(b s) c -> b (s c)", s=CAP)).then_inc(S(f"{t}_rows"), 16)
            sp.wait_ge(S(f"{t}_routed"), past("m_routed") + L + 1)
            weights(sp, t, L, 2, 2)
            with sp.Fori(0, TRIPS - 1) as it:
                for u in range(RING):
                    sp.wait_ge(S(f"{t}_dn"), it * RING + u + 2 + L * NE)
                    weights(sp, t, L, it * RING + u + RING, u)
            for u in range(NE - RING * TRIPS):
                sp.wait_ge(S(f"{t}_dn"), RING * (TRIPS - 1) + u + 2 + L * NE)
                weights(sp, t, L, RING * TRIPS + u, u)

            def body(j):
                sp.wait_ge(S(f"{x}_step"), j * X_STEPS + 1)
                e = sp.value_load(more_i[0:1, bass.ds(j + 1, 1)], min_val=0, max_val=NE - 1)
                weights(sp, x, L, e, 0)
            further(sp, t, L, body)

        def moe_pe(pe, L):
            t, x = "m", f"mx{L}"
            pe.sem_inc(S(f"{x}_step"), 1)
            if L == 0:
                pe.sem_inc(S(f"{t}_dn"), 1)
                pe.sem_inc(S(f"{t}_hturn"), 1)
                pe.sem_inc(S(f"{t}_xturn"), RING)
            turn_pe(pe, f"m{L}n", lambda i, k: rows[:, i, k * P:(k + 1) * P], lambda e, i: rows_ready(e, f"m{L}n", i + 1))
            turned(pe, f"m{L}n")
            pe.wait_ge(S(f"{t}_rw"), past("m_rw") + 16 * 5 * (L + 1))
            for i in range(NT):
                for k in range(KD):
                    mm = nc.tensor.matmul(bank[4][:, i * NR:(i + 1) * NR], hT[:, k, i * P:(i + 1) * P], router_w[L][:, k, :],
                                          start=(k == 0), stop=(k == KD - 1))
            mm.then_inc(S(f"{t}_rmm"), 1)
            pe.wait_ge(S(f"{t}_oh"), past("m_oh") + L + 1)
            for i in range(NT):
                for j in range(i + 1):
                    mm = nc.tensor.matmul(bank[5][:, i * NE:(i + 1) * NE], (tri_strict if j == i else ones)[:], oh_sum[:, j, :],
                                          start=(j == 0), stop=(j == i))
            for j in range(NT):
                mm = nc.tensor.matmul(bank[6][:, 0:NE], ones[:], oh_sum[:, j, :], start=(j == 0), stop=(j == NT - 1))
            mm.then_inc(S(f"{t}_cnt"), 1)
            pe.wait_ge(S(f"{t}_rows"), 32 * (L + 1))
            nc.tensor.transpose(bank[7][:, 0:NBLK], slot_rows[:], ident[0:NBLK, 0:NBLK]).then_inc(S(f"{t}_sturn"), 1)
            x_turn(pe, t, L * NE, L * uses(0), 0)

            def body(e, c, cu, u, last):
                gate_up(pe, t, c, cu, u)
                if not last:
                    x_turn(pe, t, c + 1, e_next(cu, u, L), (u + 1) % RING)
                hid_turn(pe, t, c)
                down(pe, t, c, cu, u)
            per_expert(pe, L, body)

            def more(j):
                pe.wait_ge(S(f"{x}_xe0"), 16 * (j + 1))
                turn_rows(0).then_inc(S(f"{x}_step"), 1)
                x_step(pe, x, j, X_XT)
                pe.wait_ge(S(f"{x}_wgu0"), 32 * (j + 1))
                gate_up_mms(0).then_inc(S(f"{x}_step"), 1)
                x_step(pe, x, j, X_HID)
                turn_hidden().then_inc(S(f"{x}_step"), 1)
                x_step(pe, x, j, X_HT)
                pe.wait_ge(S(f"{x}_wd0"), 16 * (j + 1))
                down_mms(0).then_inc(S(f"{x}_step"), 1)
            further(pe, t, L, more)

        def moe_act(act, L, x_ready):
            t, x = "m", f"mx{L}"
            if L == 0:
                act.sem_inc(S(f"{t}_xT"), 1)
                act.sem_inc(S(f"{t}_y"), 1)
                for u in range(RING):
                    act.sem_inc(S(f"{t}_yout{u}"), 16)
            norm_act(act, f"m{L}n", x_ready)
            for i in range(NT):
                turn_evac(act, f"m{L}n", hT, i, 0)
            act.wait_ge(S(f"{t}_d"), 2 * L + 1)
            nc.scalar.activation(small[:, 0:4, :], small[:, 0:4, :], ACT.Exp).then_inc(S(f"{t}_exp"), 1)
            act.wait_ge(S(f"{t}_d"), 2 * L + 2)
            nc.scalar.activation(small[:, 8, :], small[:, 8, :], ACT.Exp).then_inc(S(f"{t}_exp"), 1)
            x_out(act, t, L * NE, 0)

            def body(e, c, cu, u, last):
                silu(act, t, c)
                if not last:
                    x_out(act, t, c + 1, (u + 1) % RING)
                y_out(act, t, L, c, cu * 2, u, e)
            per_expert(act, L, body)

            def more(j):
                x_step(act, x, j, X_TURN)
                copy_x(0).then_inc(S(f"{x}_step"), 1)
                x_step(act, x, j, X_GU)
                nc.scalar.activation(act_g, bank[1][:, 0:FH], ACT.Silu).then_inc(S(f"{x}_step"), 1)
                x_step(act, x, j, X_DN)
                nc.scalar.activation(yb[:, 0, :], bank[3][:, :], ACT.Copy).then_inc(S(f"{x}_y"), 1)
                act.wait_ge(S(f"{x}_y"), j + 1)
                store_y(act, x, L, 0, NE + j)
                act.wait_ge(S(f"{x}_yout0"), 32 * (j + 1))
                act.sem_inc(S(f"{x}_step"), 1)
            further(act, t, L, more)

        def moe_pool(pool, L):
            t, x = "m", f"mx{L}"
            for p_ in (x, t)[:2 - L]:
                pool.sem_inc(S(f"{p_}_idx"), 1)
            norm_pool(pool, f"m{L}n")
            pool.wait_ge(S("slots_zero"), 32)
            pool.wait_ge(S(f"{t}_dest"), past("m_dest") + L + 1)
            for k in range(2):
                for i in range(NT):
                    nc.gpsimd.indirect_dma_start(
                        out=slot_d[L], out_offset=bass.IndirectOffsetOnAxis(ap=dest[:, k, i:i + 1], axis=0),
                        in_=token2[:, i:i + 1], in_offset=None).then_inc(S(f"{t}_scat"), 16)
            pool.wait_ge(S(f"{t}_h"), past("m_h") + 16 * (L + 1))
            pool.wait_ge(S(f"{t}_sidx"), past("m_sidx") + L + 1)
            pool.wait_ge(S(f"{t}_rmm"), past("m_rmm") + L + 1)

            def body(e, c, cu, u, last):
                pool.wait_ge(S(f"{t}_xturn"), c + 1)
                gather(pool, t, L, c, u, e)
            per_expert(pool, L, body)

            def more(j):
                pool.wait_ge(S(f"{x}_step"), j * X_STEPS + 1)
                gather(pool, x, L, j, 0, NE + j)
            def zero_rows():
                nc.gpsimd.memset(y_rows[:, 0, 0, :], 0.0).then_inc(S(f"{x}_zero"), 1)
                pool.wait_ge(S(f"{x}_zero"), 1)
                pool.dma_start(y_d[L][NE * CAP:, :].rearrange("(a p) c -> p a c", p=4 * NX),
                               y_rows[0:4 * NX, 0, 0:1, :].broadcast_to((4 * NX, CAP // 4, DM))).then_inc(S(f"{x}_zero"), 16)
                pool.wait_ge(S(f"{x}_zero"), 17)

            def fetch(n_rows):
                for i in range(NT):
                    for k in range(2):
                        nc.gpsimd.indirect_dma_start(
                            out=y_rows[:, k, i, :], out_offset=None, in_=y_d[L][0:n_rows, :],
                            in_offset=bass.IndirectOffsetOnAxis(ap=dest[:, k, i:i + 1], axis=0)).then_inc(S(f"{t}_yin{i}"), 16)

            def all_made(n):
                wait_apart(pool, (S(f"{x}_step"), n * X_STEPS + 1))
                fetch(ROWS)

            def none():
                fence(pool, t, L)
                fetch(NE * CAP)
            further(pool, t, L, more, zero_rows, all_made, none)

        def moe_dve(dve, L, link, gain_n):
            t, x = "m", f"mx{L}"
            v_ = nc.vector
            if L == 0:
                dve.sem_inc(S(f"{t}_hid"), 1)
                dve.sem_inc(S(f"{t}_hT"), 1)
            norm_dve(dve, f"m{L}n", gain_n)
            dve.wait_ge(S(f"{t}_rmm"), past("m_rmm") + L + 1)
            link(v_.tensor_copy(lgt, split(bank[4][:, 0:NT * NR], NT, NR)))
            gl_, el_ = lgt[:, :, 0:MG], lgt[:, :, MG:].rearrange("p i (g e) -> p i g e", g=MG)

            def bc(ap, n):
                return ap.unsqueeze(2).broadcast_to((P, NT, n))

            def first_max(vals, n, mx, onehot):
                link(v_.tensor_reduce(mx.unsqueeze(2), vals, AX.X, ALU.max))
                link(v_.tensor_tensor(eqs[:, :, 0:n], vals, bc(mx, n), ALU.is_equal))
                link(v_.scalar_tensor_tensor(cand[:, :, 0:n], eqs[:, :, 0:n], -100.0,
                                             iota32[:, 0:n].unsqueeze(1).broadcast_to((P, NT, n)), ALU.mult, ALU.add))
                link(v_.tensor_reduce(small[:, 11, :].unsqueeze(2), cand[:, :, 0:n], AX.X, ALU.min))
                link(v_.tensor_tensor(onehot, cand[:, :, 0:n], bc(small[:, 11, :], n), ALU.is_equal))

            first_max(gl_, MG, small[:, 4, :], oh_g)
            v_.tensor_tensor(small[:, 0:4, :].rearrange("p g i -> p i g"), gl_, bc(small[:, 4, :], MG), ALU.subtract).then_inc(S(f"{t}_d"), 1)
            pg = prod[:, 0:NT, :].rearrange("p i (e g) -> p i e g", g=MG)
            link(v_.tensor_tensor(pg, el_.rearrange("p i g e -> p i e g"), oh_g.unsqueeze(2).broadcast_to((P, NT, EPG, MG)), ALU.mult))
            link(v_.tensor_reduce(es.unsqueeze(3), pg, AX.X, ALU.add))
            first_max(es, EPG, small[:, 5, :], oh_e[:, 0])
            link(v_.scalar_tensor_tensor(es, oh_e[:, 0], NEG, es, ALU.mult, ALU.add))
            first_max(es, EPG, small[:, 6, :], oh_e[:, 1])
            v_.tensor_tensor(small[:, 8, :], small[:, 6, :], small[:, 5, :], ALU.subtract).then_inc(S(f"{t}_d"), 1)
            for k in range(2):
                ins_ = v_.tensor_tensor(oh[:, k].rearrange("p i (g e) -> p i g e", g=MG), oh_g.unsqueeze(3).broadcast_to((P, NT, MG, EPG)),
                                        oh_e[:, k].unsqueeze(2).broadcast_to((P, NT, MG, EPG)), ALU.mult)
                link(ins_)
            v_.tensor_tensor(oh_sum, oh[:, 0], oh[:, 1], ALU.add).then_inc(S(f"{t}_oh"), 1)
            dve.wait_ge(S(f"{t}_exp"), 2 * L + 1)
            link(v_.tensor_reduce(small[:, 7, :].unsqueeze(2), small[:, 0:4, :].rearrange("p g i -> p i g"), AX.X, ALU.add))
            dve.wait_ge(S(f"{t}_exp"), 2 * L + 2)
            link(v_.tensor_scalar(small[:, 9, :], small[:, 8, :], 1.0, None, ALU.add))
            link(v_.tensor_tensor(small[:, 9, :], small[:, 9, :], small[:, 7, :], ALU.mult))
            link(v_.reciprocal(weight[:, 0, :], small[:, 9, :]))
            link(v_.tensor_tensor(weight[:, 1, :], weight[:, 0, :], small[:, 8, :], ALU.mult))
            dve.wait_ge(S(f"{t}_cnt"), past("m_cnt") + L + 1)
            v_.tensor_copy(before, split(bank[5][:, 0:NT * NE], NT, NE))
            link(v_.tensor_copy(load, bank[6][:, 0:NE]))
            link(v_.memset(onesr, 1.0))
            link(v_.tensor_tensor(cmp_, load.unsqueeze(2).broadcast_to((P, NE, MORE)), more_at[:].unsqueeze(1).broadcast_to((P, NE, MORE)), ALU.is_gt))
            link(v_.tensor_reduce(xn.unsqueeze(2), cmp_, AX.X, ALU.add))
            link(v_.tensor_tensor_scan(xend, onesr, xn, 0.0, ALU.mult, ALU.add))
            link(v_.tensor_tensor(xrow, xend, xn, ALU.subtract))
            link(v_.tensor_scalar(xrow, xrow, float(CAP), float(CAP * NE - CAP), ALU.mult, ALU.add))
            link(v_.tensor_tensor(cmpx, xend.unsqueeze(1).broadcast_to((P, NX, NE)), iota32[:, 0:NX].unsqueeze(2).broadcast_to((P, NX, NE)), ALU.is_le))
            link(v_.tensor_reduce(more_f[:, 1:].unsqueeze(2), cmpx, AX.X, ALU.add))
            link(v_.tensor_copy(more_f[:, 0:1], xend[:, NE - 1:NE]))
            link(v_.tensor_scalar(more_i[:], more_f, float(NE - 1), None, ALU.min))
            ohf = oh.rearrange("p k i e -> p (k i) e")
            for k in range(2):
                link(v_.tensor_tensor(split(prod.rearrange("p a b -> p (a b)"), 2, NT, NE)[:, k], oh[:, k], before, ALU.mult))
            link(v_.tensor_reduce(pos.unsqueeze(2), prod, AX.X, ALU.add))
            for tab, o in ((row_off[:], base), (xrow, xbase)):
                link(v_.tensor_tensor(prod, ohf, tab.unsqueeze(1).broadcast_to((P, 2 * NT, NE)), ALU.mult))
                link(v_.tensor_reduce(o.unsqueeze(2), prod, AX.X, ALU.add))
            link(v_.tensor_scalar(over, pos, float(CAP), None, ALU.is_ge))
            link(v_.tensor_tensor(xbase, xbase, base, ALU.subtract))
            link(v_.tensor_tensor(xbase, xbase, over, ALU.mult))
            link(v_.tensor_tensor(pos, pos, base, ALU.add))
            v_.tensor_tensor(dest[:].rearrange("p k i -> p (k i)"), pos, xbase, ALU.add).then_inc(S(f"{t}_dest"), 1)
            dve.wait_ge(S(f"{t}_dest"), past("m_dest") + L + 1)
            dve.sem_inc(S(f"{t}_routed"), 1)
            dve.wait_ge(S(f"{t}_sturn"), past("m_sturn") + L + 1)
            v_.tensor_tensor(slot_idx[:], bank[7][:, 0:NBLK], half_of[:].broadcast_to((P, NBLK)), ALU.add).then_inc(S(f"{t}_sidx"), 1)

            def body(e, c, cu, u, last):
                hidden(dve, t, c)
                hid_out(dve, t, c)
            per_expert(dve, L, body)

            def more(j):
                x_step(dve, x, j, X_G)
                nc.vector.tensor_tensor(hid, act_g, bank[1][:, FH:2 * FH], ALU.mult).then_inc(S(f"{x}_step"), 1)
                x_step(dve, x, j, X_HTURN)
                nc.vector.tensor_copy(hidT, split(bank[2][:, 0:2 * P], 2, P)).then_inc(S(f"{x}_step"), 1)
            further(dve, t, L, more)
            for i in range(NT):
                dve.wait_ge(S(f"{t}_yin{i}"), 32 * (L + 1))
                for k in range(2):
                    v_.scalar_tensor_tensor(xt[:, i, :], y_rows[:, k, i, :], weight[:, k, i:i + 1], xt[:, i, :],
                                            ALU.mult, ALU.add).then_inc(S(f"{t}_x"), 1)
                    dve.wait_ge(S(f"{t}_x"), 2 * NT * L + 2 * i + k + 1)

        block = ctx.enter_context(nc.Block())

        @block.sync
        def _(sp):
            even_sp(sp)
            moe_sp(sp, 0, "eo", "n0")
            odd_sp(sp)
            moe_sp(sp, 1, "oo", "n2")
            for i in range(NT):
                sp.wait_ge(S("m_x"), 2 * NT + 2 * i + 2)
                sp.dma_start(out[0, i * P:(i + 1) * P, :], xt[:, i, :]).then_inc(S("out"), 16)
            sp.wait_ge(S("out"), 16 * NT)

        @block.tensor
        def _(pe):
            even_pe(pe)
            moe_pe(pe, 0)
            odd_pe(pe)
            moe_pe(pe, 1)

        @block.scalar
        def _(act):
            even_act(act)
            moe_act(act, 0, lambda e: e.wait_ge(S("eo_add"), 2 * NT))
            odd_act(act)
            moe_act(act, 1, lambda e: e.wait_ge(S("oo_add"), past("oo_add") + 2 * NT))

        @block.gpsimd
        def _(pool):
            even_pool(pool)
            moe_pool(pool, 0)
            odd_pool(pool)
            moe_pool(pool, 1)

        @block.vector
        def _(dve):
            link = Chain(dve, S("dve_chain"))
            even_dve(dve, link)
            moe_dve(dve, 0, link, 2)
            odd_dve(dve, link)
            moe_dve(dve, 1, link, 4)


_INS = ['x', 'rel_bias', 'attn_norm', 'ffn_norm', 'even_w_in', 'even_conv_w', 'even_conv_b', 'even_dt_bias',
        'even_a_log', 'even_d_skip', 'even_ssm_norm', 'even_q_norm', 'even_k_norm', 'even_w_out', 'odd_w_in',
        'odd_q_norm', 'odd_kc_norm', 'odd_ks_norm', 'odd_kw_norm', 'odd_cmp_pos_k', 'odd_cmp_pos_v',
        'odd_cmp_k_w1', 'odd_cmp_k_w2', 'odd_cmp_v_w1', 'odd_cmp_v_w2', 'odd_w_out', 'moe_router_group',
        'moe_router_expert', 'moe_w_gate', 'moe_w_up', 'moe_w_down']


def kernel(**inputs):
    import concourse.bacc as bacc
    from concourse.bass_utils import run_bass_kernel_spmd

    nc = bacc.Bacc("TRN2", target_bir_lowering=False, num_devices=1)
    arrays, aps = {}, {}
    for name in _INS:
        arrays[f"in_{name}"] = np.ascontiguousarray(inputs[name])
    arrays["in_bucket_table"] = bucket_table()
    for name, a in arrays.items():
        aps[name[3:]] = nc.dram_tensor(name, a.shape, mybir.dt.from_np(a.dtype), kind="ExternalInput").ap()
    out = nc.dram_tensor("out_x", (1, SEQ, DM), F32, kind="ExternalOutput").ap()
    build(nc, aps, out)
    r = run_bass_kernel_spmd(nc, [arrays], core_ids=[0])
    return r.results[0]["out_x"]
```

```python
from contextlib import ExitStack, contextmanager

import numpy as np

import concourse.bass as bass
from concourse import mybir

F32 = mybir.dt.float32
BF16 = mybir.dt.bfloat16
I32 = mybir.dt.int32
ALU = mybir.AluOpType
ACT = mybir.ActivationFunctionType
AX = mybir.AxisListType

P = 128
SEQ, DM = 512, 1024
NT = SEQ // P
KD = DM // P
EPS = 1e-6
NEG = -1e30
CLAMP = 1e20
TAKEN = -3e38
NB, HEADS = 32, 8
BIAS_W = 2 * SEQ
TW = SEQ + P * (NT - 1)

SH, SD, SN, SG = 8, 64, 128, 2
DI = SH * SD
XBC = DI + 2 * SG * SN
CT = XBC // P
TAPS = 4
HD = 64
IH, ID = 4, 64
TOPK = min(256, SEQ // 4)
C_Z, C_XBC = 0, DI
C_DT = C_XBC + XBC
C_Q = C_DT + SH
C_K = C_Q + HEADS * HD
C_V = C_K + HD
C_IQ = C_V + HD
C_IK = C_IQ + IH * ID
C_IW = C_IK + ID
EVEN_COLS = C_IW + IH

OG, OD = 2, 128
HPG = HEADS // OG
CB, CS = 32, 16
NC = (SEQ - CB) // CS + 1
OKV = OG * OD
C_OK = HEADS * OD
C_GL = C_OK + 6 * OKV
ODD_COLS = C_GL + 3 * HEADS
assert SEQ // 64 <= 16 and SEQ <= 512

MG, EPG = 4, 8
NE = MG * EPG
FF = 512
NA = 2 * SEQ
CAP = 64
NX = (NA - 1) // (CAP + 1)
NBLK = NE + NX
ROWS = NBLK * CAP
NR = MG + NE
FH = FF // 2
EW = 2 * KD * FF + (FF // P) * DM
RING = 3
TRIPS = NE // RING
MORE = SEQ // CAP - 1

O_RING = 0
O_X = RING * EW
O_HT = O_X + NT * DM
O_ROWS = O_HT + KD * SEQ
ARENA = O_ROWS + NT * DM


def bucket_table():
    dist = np.arange(BIAS_W) - (SEQ - 1)
    d = np.maximum(dist, 1).astype(np.float32)
    large = NB // 2 + (np.log(d / np.float32(NB // 2)) / np.float32(np.log(128 / (NB // 2)))
                       * np.float32(NB // 2)).astype(np.int32)
    bucket = np.where(dist < NB // 2, np.maximum(dist, 0), np.minimum(large, NB - 1))
    table = np.zeros((NB + 1, BIAS_W), np.float32)
    table[:NB] = (np.arange(NB)[:, None] == bucket[None]) & (dist >= 0)[None]
    table[NB] = np.where(dist < 0, NEG, 0.0)
    return table


def wait_apart(eng, *waits):
    waits = [(sem, value if isinstance(value, int) else eng.to_reg(value)) for sem, value in waits]
    if not isinstance(waits[0][1], int):
        eng.wait_ge(waits[0][0], 1)
    for sem, value in waits:
        eng.wait_ge(sem, value)


class Chain:

    def __init__(self, eng, sem):
        self.eng, self.sem, self.n, self.term = eng, sem, 0, None

    def __call__(self, ins):
        self.n += 1
        ins.then_inc(self.sem, 1)
        if self.term is None:
            self.eng.wait_ge(self.sem, self.n)
        else:
            wait_apart(self.eng, (self.sem, self.n + self.term))

    def enter(self, i, per_trip):
        self.term, self.start, self.per = i * per_trip, self.n, per_trip

    def leave(self, trips):
        assert self.n - self.start == self.per, (self.n - self.start, self.per)
        self.n, self.term = self.start + trips * self.per, None


COUNTS_ON = {
    "T_in1": ("T_in0", 16), "opar_in": ("par_in", 192), "op_ev": ("ep_ev", 22), "op_mm": ("ep_mm", 22),
    "op_w0": ("ep_w0", 16), "op_w1": ("ep_w1", 16), "op_w2": ("ep_w2", 16), "op_w3": ("ep_w3", 32),
    "op_w4": ("ep_w4", 16), "op_w5": ("ep_w5", 16), "oo_add": ("eo_add", 8), "oo_mm": ("eo_mm", 8),
    "oo_w0": ("eo_w0", 16), "oo_w1": ("eo_w1", 16), "blk": ("seg", 8), "c_hid": ("cb_mm", 4),
    "c_rows": ("abc_mm", 8), "cw1_in0": ("table_in", 32), "cw1_in1": ("ssm_gain_in", 16), "gl_exp": ("eac", 1),
    "hid_c": ("decay", 8), "kcT": ("z_silu", 1), "kc_ms": ("y_ms", 4), "kc_n": ("dA", 1), "kc_raw": ("a_exp", 1),
    "kc_rstd": ("y_rstd", 4), "kc_ss": ("acum", 1), "kc_turned": ("acum_mm", 1), "ok_n": ("mt", 8),
    "ok_out": ("tok_out", 8), "ok_turned": ("tok_turned", 8), "oq_n": ("qn", 4), "oq_out": ("qk_out", 6),
    "oq_turned": ("qk_turned", 5), "oss": ("ssq", 5), "oss_ms": ("ssq_ms", 1), "oss_rstd": ("ssq_rstd", 1),
    "qscale": ("hgain", 1),
    "m_rw": ("bias_out", 16), "m_rmm": ("bias_mm", 2), "m_oh": ("conv", 8),
    "m_cnt": ("ix_mm", 12), "m_dest": ("ix_acc", 12), "m_routed": ("selm", 3), 
    
}


def past(name):
    return COUNTS_ON[name][1] if name in COUNTS_ON else 0


class Env:

    def __init__(self, nc, ctx):
        self.nc, self.ctx, self.sems = nc, ctx, {}

    def sb(self, name, shape, dt=F32):
        return self.ctx.enter_context(self.nc.sbuf_tensor(name, shape, dt))

    def s(self, name):
        name = COUNTS_ON[name][0] if name in COUNTS_ON else name
        if name not in self.sems:
            self.sems[name] = self.ctx.enter_context(self.nc.semaphore(name))
        return self.sems[name]


def bcast_rows(ap, n, parts=P):
    return bass.AP(ap.tensor, ap.offset, [[0, parts], [1, n]])


def split(ap, *dims):
    names = "abcd"[:len(dims)]
    return ap.rearrange(f"p ({' '.join(names)}) -> p {' '.join(names)}", **dict(zip(names, dims)))


def build(nc, ins, out):
    ctx = ExitStack()
    with ctx:
        ctx.enter_context(nc.allow_non_contiguous_dma(reason="small parameters, channels onto partitions"))
        env = Env(nc, ctx)
        sb, S = env.sb, env.s
        dram = lambda name, shape: nc.dram_tensor(name, shape, F32, kind="Internal").ap()

        arena = sb("arena", [P, ARENA])
        bank = [ctx.enter_context(nc.psum_tensor(f"bank{n}", [P, 512], F32)) for n in range(8)]

        def at(off, *dims):
            n = int(np.prod(dims))
            return split(arena[:, off:off + n], *dims) if len(dims) > 1 else arena[:, off:off + n]

        bias_row_d = dram("bias_row_d", [HEADS, BIAS_W])
        y_d = [dram(f"y_d{n}", [ROWS, DM]) for n in range(2)]

        ident = sb("ident", [P, P])
        identb = sb("identb", [P, P], BF16)
        ones = sb("ones", [P, P])
        tri = sb("tri", [P, P])
        tri_strict = sb("tri_strict", [P, P])
        score_base = sb("score_base", [P, SEQ])
        minus1 = sb("minus1", [P, 3])
        nhalf = sb("nhalf", [P, 36])
        iota32 = sb("iota32", [P, NE])
        row_off = sb("row_off", [P, NE])
        more_at = sb("more_at", [P, MORE])
        first_rows = sb("first_rows", [P, CAP])
        gain = sb("gain", [P, DM])
        ss = sb("ss", [P, NT])
        rstd = sb("rstd", [P, NT])

        xt = at(O_X, NT, DM)
        hT = at(O_HT, KD, SEQ)
        rows = at(O_ROWS, NT, DM)

        NORM = {"n0": 0, "m0n": 1, "n2": 2, "m1n": 3}
        TURN = {"n0": 0, "eo": 1, "m0n": 2, "n2": 3, "oo": 4, "m1n": 5}

        def rows_ready(eng, tag, tiles):
            eng.wait_ge(S("norm_row"), NT * NORM[tag] + tiles)

        def norm_act(act, tag, x_ready):
            x_ready(act)
            for i in range(NT):
                nc.scalar.activation(rows[:, i, :], xt[:, i, :], ACT.Square,
                                     accum_out=ss[:, i:i + 1]).then_inc(S("norm_sq"), 1)

        def norm_pool(pool, tag):
            pool.wait_ge(S("norm_sq"), NT * (NORM[tag] + 1))
            nc.gpsimd.tensor_scalar(ss[:], ss[:], 1.0 / DM, EPS, ALU.mult, ALU.add).then_inc(S("norm_ms"), 1)
            pool.wait_ge(S("norm_ms"), NORM[tag] + 1)
            nc.gpsimd.tensor_tensor(rstd[:], ss[:], nhalf[:, 0:NT], ALU.pow).then_inc(S("norm_rstd"), 1)

        def norm_dve(dve, tag, gain_n):
            dve.wait_ge(S("norm_rstd"), NORM[tag] + 1)
            dve.wait_ge(S("gain_in"), 16 * gain_n)

            def row(i):
                nc.vector.scalar_tensor_tensor(rows[:, i, :], xt[:, i, :], rstd[:, i:i + 1], gain[:], ALU.mult,
                                               ALU.mult).then_inc(S("norm_row"), 1)
            row(0)
            for i in range(NT):
                if i + 1 < NT:
                    row(i + 1)
                turn_evac(dve, tag, hT, i, 1)

        def turn_pe(pe, tag, src, ready):
            for i in range(NT):
                ready(pe, i)
                for half in range(2):
                    if i >= 2:
                        pe.wait_ge(S(f"turn_out{half}"), NT * TURN[tag] + i - 1)
                    for k in range(4):
                        mm = nc.tensor.transpose(bank[(2 * i + half) % 4][:, k * P:(k + 1) * P],
                                                 src(i, 4 * half + k), ident[:])
                    mm.then_inc(S("turned"), 1)

        def turn_evac(eng, tag, dst, i, half):
            eng.wait_ge(S("turned"), 2 * NT * TURN[tag] + 2 * i + half + 1)
            d = dst[:, 4 * half:4 * half + 4, i * P:(i + 1) * P]
            b = split(bank[(2 * i + half) % 4][:, :], 4, P)
            ins_ = nc.vector.tensor_copy(d, b) if half else nc.scalar.activation(d, b, ACT.Copy)
            ins_.then_inc(S(f"turn_out{half}"), 1)

        def turned(eng, tag):
            eng.wait_ge(S("turn_out0"), NT * (TURN[tag] + 1))
            eng.wait_ge(S("turn_out1"), NT * (TURN[tag] + 1))

        STAGES = 2
        M = STAGES * NT
        O_FIRST = 6
        score_bank = [bank[0], bank[1], bank[6], bank[7]]

        class Attention:
            def __init__(self, tag, branches, loop, trips, queries, biases, q_of, b_of, work, weigh, finish, before=None):
                self.trips, self.weigh = trips, weigh
                self.loop, self.queries, self.biases, self.q_of, self.b_of = loop, queries, biases, q_of, b_of
                self.finish, self.first = finish, before is None
                self.NB = len(branches[0])
                self.units = [(s, i, b, branches[i][b]) for s in range(STAGES) for i in range(NT) for b in range(self.NB)]
                self.U = len(self.units)
                self.t0, self.u0, self.m0 = (0, 0, 0) if before is None else before.after
                self.after = self.t0 + trips, self.u0 + trips * self.U, self.m0 + trips * M
                self.p = at(work, 4, SEQ)
                self.pT = at(work + 4 * SEQ, 2, 4, P)
                self.negm = sb(f"{tag}_negm", [P, 4])
                self.sums = sb(f"{tag}_sums", [P, 4, self.NB])
                self.coef = sb(f"{tag}_coef", [P, 4, self.NB])

            def sem(self, what):
                return S(f"att_{what}")

            def staged(self, it, s):
                return self.sem("staged"), 2 * STAGES * (self.t0 + it) + 2 * s + 2

            def macros_ago(self, it, m, k):
                return self.sem("o"), self.m0 + it * M + m - k + 1 + O_FIRST

            def pe(self, pe):
                if self.first:
                    pe.sem_inc(self.sem("tr"), 4)
                    pe.sem_inc(self.sem("pv"), 2)
                with self.loop(pe) as (it, v):
                    for t in range(self.U + 3):
                        if t < self.U:
                            s, i, b, br = self.units[t]
                            n = self.u0 + it * self.U + t
                            if i == 0 and b == 0:
                                pe.wait_ge(*self.staged(it, s))
                            pe.wait_ge(self.sem("lg"), n + 1)
                            o = score_bank[t % 4][:, 0:br["L"]]
                            mm = nc.tensor.matmul(o, self.queries[s][:, i * P:(i + 1) * P], br["k"](v),
                                                  start=True, stop=not br.get("mask"))
                            if br.get("mask"):
                                mm = nc.tensor.matmul(o, identb[:], br["mask"], start=False, stop=True)
                            mm.then_inc(self.sem("qk"), 1)
                        if 2 <= t < self.U + 2:
                            s, i, b, br = self.units[t - 2]
                            n = self.u0 + it * self.U + t - 2
                            pe.wait_ge(self.sem("ex"), n + 1)
                            pe.wait_ge(self.sem("pt"), n + 1)
                            for kt in range((br["L"] + P - 1) // P):
                                w = min(P, br["L"] - kt * P)
                                mm = nc.tensor.transpose(bank[2 + t % 2][0:w, kt * P:(kt + 1) * P],
                                                         self.p[:, (t - 2) % 4, kt * P:kt * P + w], ident[:])
                            mm.then_inc(self.sem("tr"), 1)
                        if t >= 3:
                            s, i, b, br = self.units[t - 3]
                            m = NT * s + i
                            n = self.u0 + it * self.U + t - 3
                            wait_apart(pe, (self.sem("pt"), n + 3), *([self.macros_ago(it, m, 2)] if b == 0 else []))
                            D = br["D"]
                            nk = (br["L"] + P - 1) // P
                            for kt in range(nk):
                                w = min(P, br["L"] - kt * P)
                                mm = nc.tensor.matmul(bank[4 + m % 2][:, b * D:(b + 1) * D],
                                                      self.pT[0:w, (t - 3) % 2, kt, :], br["v"](v, kt),
                                                      start=(kt == 0), stop=(kt == nk - 1))
                            mm.then_inc(self.sem("pv"), 1)

            def act(self, act):
                if self.first:
                    act.sem_inc(self.sem("pt"), 2)
                with self.loop(act) as (it, v):
                    for t in range(self.U + 2):
                        if t < self.U:
                            s, i, b, br = self.units[t]
                            m = NT * s + i
                            n = self.u0 + it * self.U + t
                            p = self.p[:, t % 4, 0:br["L"]]
                            act.wait_ge(self.sem("lg"), n + 5)
                            if b == 0:
                                act.wait_ge(*self.macros_ago(it, m, 4))
                            nc.scalar.activation(p, p, ACT.Exp, bias=self.negm[:, t % 4:t % 4 + 1], scale=-1.0,
                                                 accum_out=self.sums[:, m % 4, b:b + 1]).then_inc(self.sem("ex"), 1)
                        if t >= 2:
                            s, i, b, br = self.units[t - 2]
                            n = self.u0 + it * self.U + t - 2
                            act.wait_ge(self.sem("tr"), n + 5)
                            act.wait_ge(self.sem("pv"), n + 1)
                            w = min(P, br["L"])
                            nk = (br["L"] + P - 1) // P
                            nc.scalar.activation(self.pT[0:w, t % 2, 0:nk, :], split(bank[2 + t % 2][0:w, 0:nk * P], nk, P),
                                                 ACT.Copy).then_inc(self.sem("pt"), 1)

            def dve(self, dve, link):
                if self.first:
                    dve.sem_inc(self.sem("lg"), 4)
                    dve.sem_inc(self.sem("o"), O_FIRST)
                with self.loop(dve, link) as (it, v):
                    for t in range(self.U + 4):
                        if t < self.U:
                            s, i, b, br = self.units[t]
                            n = self.u0 + it * self.U + t
                            L = br["L"]
                            negm = self.negm[:, t % 4:t % 4 + 1]
                            first = i == 0 and b == 0
                            wait_apart(dve, (self.sem("qk"), n + 1), (self.sem("tr"), n + 1),
                                       *([self.staged(it, s)] if first else []))
                            ins_ = nc.vector.tensor_tensor_reduce(
                                out=self.p[:, t % 4, 0:L], in0=score_bank[t % 4][:, 0:L], in1=br["bias"](self.biases[s]),
                                scale=-1.0, scalar=3e38, op0=ALU.add, op1=ALU.min, accum_out=negm)
                            if br.get("clamp"):
                                link(ins_)
                                ins_ = nc.vector.tensor_scalar(negm, negm, CLAMP, None, ALU.min)
                            ins_.then_inc(self.sem("lg"), 1)
                        if t >= 4:
                            s, i, b, br = self.units[t - 4]
                            if b == self.NB - 1:
                                m = NT * s + i
                                dve.wait_ge(self.sem("coef"), self.m0 + it * M + m + 1)
                                dve.wait_ge(self.sem("pv"), self.u0 + it * self.U + t - 4 + 3)
                                self.finish(self, dve, link, v, s, m, i).then_inc(self.sem("o"), 1)

            def stage(self, pool, it, s):
                wait_apart(pool, (self.sem("o"), self.m0 + (it - 1) * M + (s + 1) * NT + O_FIRST))
                nc.gpsimd.tensor_copy(self.queries[s], self.q_of(it, s)).then_inc(self.sem("staged"), 1)
                nc.gpsimd.tensor_copy(self.biases[s][..., ::-1], self.b_of(it, s)).then_inc(self.sem("staged"), 1)

            def weights_of(self, pool, it, s, i):
                m = NT * s + i
                wait_apart(pool, (self.sem("ex"), self.u0 + it * self.U + (m + 1) * self.NB),
                           self.macros_ago(it, m, 4))
                self.weigh(self, pool, it, s, m, i).then_inc(self.sem("coef"), 1)

            def pool(self, pool):
                for s in range(STAGES):
                    self.stage(pool, 0, s)

                def trip(it, more):
                    for s in range(STAGES):
                        for i in range(NT):
                            self.weights_of(pool, it, s, i)
                            if more and s == 1 and i == 0:
                                self.stage(pool, it + 1, 0)
                    if more:
                        self.stage(pool, it + 1, 1)
                with pool.Fori(0, self.trips - 1) as it:
                    trip(it, True)
                trip(self.trips - 1, False)

            def done(self, eng):
                eng.wait_ge(self.sem("o"), self.after[2] + O_FIRST)

        def outproj_pe(pe, tag, mixT, wo, loads):
            turned(pe, tag)
            for half in range(2):
                pe.wait_ge(S(f"{tag}_w{half}"), past(f"{tag}_w{half}") + 16)
                for i in range(NT):
                    n = half * NT + i
                    if n >= 4:
                        pe.wait_ge(S(f"{tag}_add"), past(f"{tag}_add") + n - 3)
                    for k in range(KD):
                        mm = nc.tensor.matmul(bank[4 + n % 4][:, :], mixT[:, k, i * P:(i + 1) * P], wo[half][:, k, :],
                                              start=(k == 0), stop=(k == KD - 1))
                    mm.then_inc(S(f"{tag}_mm"), 1)

        def outproj_dve(dve, tag):
            for half in range(2):
                for i in range(NT):
                    n = half * NT + i
                    dve.wait_ge(S(f"{tag}_mm"), past(f"{tag}_mm") + n + 1)
                    xs = xt[:, i, half * 512:(half + 1) * 512]
                    nc.vector.tensor_tensor(xs, xs, bank[4 + n % 4][:, :], ALU.add).then_inc(S(f"{tag}_add"), 1)

        e0 = O_RING
        T = at(e0, HEADS, TW); e0 += HEADS * TW
        xbcT = at(e0, CT, SEQ + TAPS - 1)
        xtok = at(e0, NT, DI)
        btok = at(e0 + NT * DI, NT, SG * SN)
        state = at(e0 + NT * (DI + SG * SN), DI)
        y_t = at(e0 + NT * (DI + SG * SN) + DI, DI)
        e0 += CT * (SEQ + TAPS - 1)
        O_XBCS = e0
        xbcS = at(e0, CT, SEQ); e0 += CT * SEQ
        z = at(e0, NT, DI); e0 += NT * DI
        O_QROWS = e0
        assert STAGES * (SEQ + 2 * TW) <= CT * SEQ + NT * DI
        qrows = at(e0, NT, HEADS * HD); e0 += NT * HEADS * HD
        eqT = at(e0, 4, SEQ); e0 += 4 * SEQ
        kA = at(e0, SEQ); kB = at(e0 + SEQ, SEQ); e0 += 2 * SEQ
        kvd = at(e0, NT, 2 * HD + SH); e0 += NT * (2 * HD + SH)
        selm = split(arena[:, e0:e0 + NT * SEQ // 2].bitcast(BF16), NT, SEQ); e0 += NT * SEQ // 2
        score = at(e0, NT - 1, SEQ); e0 += (NT - 1) * SEQ
        iqT = at(e0, 2, SEQ); ikA = at(e0 + 2 * SEQ, SEQ); ikB = at(e0 + 3 * SEQ, SEQ); e0 += 4 * SEQ
        O_EW = e0
        ew = [at(e0, KD, 512), at(e0 + KD * 512, KD, 512)]
        assert e0 + 2 * KD * 512 <= RING * EW, e0
        seg = at(O_EW, SG, 4, P)
        cbm = at(O_EW + 1024, SG, P)
        xdt = at(O_EW + 1280, DI)
        xw = at(O_EW + 1792, DI)
        y2 = at(O_EW + 2304, DI)
        ssm_gain = at(O_EW + 2816, DI)
        krn = at(O_EW + 3328, NT, P)
        junk = at(O_ROWS + NT * DI, DI)
        e_wo = [hT, at(O_EW + KD * 512, KD, 512)]
        relu = at(O_ROWS, 2, SEQ)
        rows_m = at(O_ROWS, 2, NT, DI)
        mixT = at(O_EW, KD, SEQ)
        table = at(O_QROWS, BIAS_W)
        brow = at(O_QROWS + BIAS_W, BIAS_W)

        relb = sb("relb", [NB + 1, HEADS])
        conv_w = sb("conv_w", [P, TAPS, CT])
        conv_b = sb("conv_b", [P, CT])
        dt_bias = sb("dt_bias", [P, SH]); a_log = sb("a_log", [P, SH]); d_skip = sb("d_skip", [P, SH])
        head_gain = sb("head_gain", [P, 2])
        iw = sb("iw", [P, NT, IH])
        m8 = sb("m8", [P, 8])
        dt = sb("dt", [P, NT, SH]); dt_e = sb("dt_e", [P, NT, SH]); dA = sb("dA", [P, NT, SH])
        acum = sb("acum", [P, NT, SH]); eac = sb("eac", [P, NT, SH])
        alast = sb("alast", [P, SH]); cdecay = sb("cdecay", [P, SH]); to_end = sb("to_end", [P, SH])
        ssq = sb("ssq", [P, NT, HEADS + 1])
        ssg = sb("ssg", [P, 2])

        w_in = ins["even_w_in"][0]
        EV_CHUNKS = [[(C_IQ, EVEN_COLS - C_IQ)], [(C_XBC, 512)], [(C_XBC + 512, 512)],
                     [(C_K, 2 * HD), (C_DT, SH)], [(C_Z, DI)], [(C_Q, HEADS * HD)]]
        J_IQ, J_IK, J_IW, J_XBC, J_KV, J_Z, J_Q, J_END = 0, 2, 3, 4, 12, 14, 18, 22
        CHUNK_JOBS = [J_XBC, J_XBC + 4, J_KV, J_Z, J_Q, J_END]
        SC = [(i, h) for i in range(1, NT) for h in range(IH)]

        def load_chunk(sp, c, chunks, src, bufs, tag, done_jobs):
            nbuf = len(bufs)
            if c >= nbuf:
                sp.wait_ge(S(f"{tag}_mm"), past(f"{tag}_mm") + done_jobs[c - nbuf])
            off = 0
            for c0, n in chunks[c]:
                sp.dma_start(bufs[c % nbuf][:, :, off:off + n],
                             src[:, c0:c0 + n].rearrange("(k p) c -> p k c", p=P)).then_inc(S(f"{tag}_w{c}"), 16)
                off += n

        def even_sp(sp):
            for i in range(NT):
                sp.dma_start(xt[:, i, :], ins["x"][0, i * P:(i + 1) * P, :]).then_inc(S("x_in"), 16)
            sp.dma_start(gain[:], bcast_rows(ins["attn_norm"][0, :], DM)).then_inc(S("gain_in"), 16)
            load_chunk(sp, 0, EV_CHUNKS, w_in, ew, "ep", CHUNK_JOBS)
            sp.wait_ge(S("relb_ones"), 1)
            sp.dma_start(relb[0:NB, :], ins["rel_bias"]).then_inc(S("table_in"), 16)
            sp.dma_start(table[0:NB + 1, :], ins["bucket_table"]).then_inc(S("table_in"), 16)
            load_chunk(sp, 1, EV_CHUNKS, w_in, ew, "ep", CHUNK_JOBS)
            sp.dma_start(conv_b[:], ins["even_conv_b"][0].rearrange("(c p) -> p c", p=P)).then_inc(S("par_in"), 16)
            for k in range(TAPS):
                sp.dma_start(conv_w[:, k, :],
                             ins["even_conv_w"][0, k].rearrange("(c p) -> p c", p=P)).then_inc(S("par_in"), 16)
            for t_, name in ((dt_bias, "even_dt_bias"), (a_log, "even_a_log"), (d_skip, "even_d_skip")):
                sp.dma_start(t_[:], bcast_rows(ins[name][0], SH)).then_inc(S("par_in"), 16)
            for n, name in enumerate(("even_q_norm", "even_k_norm")):
                for half in range(2):
                    sp.dma_start(head_gain[half * HD:(half + 1) * HD, n:n + 1],
                                 ins[name][0].rearrange("(p c) -> p c", c=1)).then_inc(S("par_in"), 16)
            sp.wait_ge(S("brow"), 2)
            sp.dma_start(bias_row_d, brow[0:HEADS, :]).then_inc(S("bias_out"), 16)
            sp.wait_ge(S("bias_out"), 16)
            load_bias(sp, "T_in0")
            for c in range(2, 6):
                load_chunk(sp, c, EV_CHUNKS, w_in, ew, "ep", CHUNK_JOBS)
            sp.wait_ge(S("ep_mm"), J_END)
            sp.dma_start(e_wo[0], ins["even_w_out"][0, :, 0:512].rearrange("(k p) c -> p k c", p=P)).then_inc(S("eo_w0"), 16)
            sp.dma_start(ssm_gain, bcast_rows(ins["even_ssm_norm"][0], DI)).then_inc(S("ssm_gain_in"), 16)
            sp.dma_start(e_wo[1], ins["even_w_out"][0, :, 512:1024].rearrange("(k p) c -> p k c", p=P)).then_inc(S("eo_w1"), 16)

        def load_bias(sp, done):
            src = bass.AP(bias_row_d.tensor, 0, [[1, P], [BIAS_W, HEADS], [1, TW]])
            sp.dma_start(T, src).then_inc(S(done), 16)

        def even_pe(pe):
            pe.wait_ge(S("table_in"), 32)
            pe.wait_ge(S("consts"), 1)
            for half in range(2):
                nc.tensor.matmul(bank[4 + half][0:HEADS, :], relb[:], table[0:NB + 1, half * 512:(half + 1) * 512],
                                 start=True, stop=True).then_inc(S("bias_mm"), 1)
            turn_pe(pe, "n0", lambda i, k: rows[:, i, k * P:(k + 1) * P], lambda e, i: rows_ready(e, "n0", i + 1))
            turned(pe, "n0")

            def job(n, mms):
                if n >= 4:
                    pe.wait_ge(S("ep_ev"), n - 3)
                for mm_args in mms:
                    for k in range(KD):
                        o, l, r = mm_args(k)
                        mm = nc.tensor.matmul(o, l, r, start=(k == 0), stop=(k == KD - 1))
                mm.then_inc(S("ep_mm"), 1)

            def channels(n, w, c0, hTk=hT):
                b = bank[n % 4]
                job(n, [lambda k: (b[:, :], w[:, k, c0:c0 + P], hT[:, k, :])])

            def tokens(n, w, tiles, cols):
                b = bank[n % 4]
                job(n, [lambda k, i=i, s=s: (b[:, s * cols:(s + 1) * cols], hT[:, k, i * P:(i + 1) * P], w[:, k, 0:cols])
                        for s, i in enumerate(tiles)])

            pe.wait_ge(S("ep_w0"), 16)
            for j in range(2):
                channels(J_IQ + j, ew[0], j * P)
            b = bank[J_IK % 4]
            c0 = IH * ID
            job(J_IK, [lambda k, q=q: (b[q * HD:(q + 1) * HD, :], ew[0][:, k, c0:c0 + ID], hT[:, k, :]) for q in range(2)])
            b2 = bank[J_IW % 4]
            c1 = c0 + ID
            job(J_IW, [lambda k, i=i: (b2[:, i * IH:(i + 1) * IH], hT[:, k, i * P:(i + 1) * P], ew[0][:, k, c1:c1 + IH])
                       for i in range(NT)])
            pe.wait_ge(S("ep_ev"), J_IK + 1)
            pe.wait_ge(S("brow"), 2)
            for u, (i, h) in enumerate(SC):
                if u >= 2:
                    pe.wait_ge(S("ix_relu"), u - 1)
                L = (i + 1) * P
                nc.tensor.matmul(bank[4 + u % 2][:, 0:L], iqT[:, h // 2, i * P:(i + 1) * P], (ikA, ikB)[h % 2][:, 0:L],
                                 start=True, stop=True).then_inc(S("ix_mm"), 1)
            for c in range(2):
                pe.wait_ge(S(f"ep_w{1 + c}"), 16)
                for j in range(4):
                    channels(J_XBC + 4 * c + j, ew[(1 + c) % 2], j * P)
            pe.wait_ge(S("ep_w3"), 32)
            for j in range(2):
                tokens(J_KV + j, ew[1], (2 * j, 2 * j + 1), 2 * HD + SH)
            pe.wait_ge(S("ep_w4"), 16)
            for i in range(NT):
                tokens(J_Z + i, ew[0], (i,), DI)
            pe.wait_ge(S("ep_w5"), 16)
            for i in range(NT):
                tokens(J_Q + i, ew[1], (i,), HEADS * HD)

            pe.wait_ge(S("ep_ev"), J_END)
            pe.wait_ge(S("kn"), 2)
            for i in range(NT):
                mm = nc.tensor.transpose(bank[0][:, i * P:(i + 1) * P], krn[:, i, :], ident[:])
            mm.then_inc(S("qk_turned"), 1)
            for i in range(NT):
                pe.wait_ge(S("qn"), i + 1)
                if i >= 2:
                    pe.wait_ge(S("qk_out"), i + 1)
                for j in range(4):
                    mm = nc.tensor.transpose(bank[1 + i % 2][:, j * P:(j + 1) * P], qrows[:, i, j * P:(j + 1) * P], ident[:])
                mm.then_inc(S("qk_turned"), 1)

            pe.wait_ge(S("dA"), 1)
            for i in range(NT):
                mm = nc.tensor.matmul(bank[3][:, i * SH:(i + 1) * SH], tri[:], dA[:, i, :], start=True, stop=True)
            mm.then_inc(S("acum_mm"), 1)
            pe.wait_ge(S("silu"), CT)
            pe.wait_ge(S("qk_out"), NT + 2)
            for i in range(NT):
                if i >= 1:
                    pe.wait_ge(S("tok_out"), 2 * i)
                for j in range(4):
                    mm = nc.tensor.transpose(bank[4][:, j * P:(j + 1) * P], xbcS[:, j, i * P:(i + 1) * P], ident[:])
                mm.then_inc(S("tok_turned"), 1)
                for g in range(SG):
                    mm = nc.tensor.transpose(bank[5][:, g * P:(g + 1) * P], xbcS[:, 4 + g, i * P:(i + 1) * P], ident[:])
                mm.then_inc(S("tok_turned"), 1)
            for i in range(NT):
                sl = slice(i * P, (i + 1) * P)
                if i >= 1:
                    pe.wait_ge(S("seg"), 2 * i)
                    pe.wait_ge(S("cbm"), i)
                for g in range(SG):
                    for h in range(4):
                        mm = nc.tensor.matmul(bank[6 + g][:, h * P:(h + 1) * P],
                                              dA[:, i, 4 * g + h:4 * g + h + 1].broadcast_to((P, P)), tri[:],
                                              start=True, stop=True)
                    mm.then_inc(S("abc_mm"), 1)
                if i == 0:
                    pe.wait_ge(S("acum"), 1)
                for g in range(SG):
                    mm = nc.tensor.matmul(bank[3][:, g * P:(g + 1) * P], xbcS[:, 4 + g, sl], xbcS[:, 6 + g, sl],
                                          start=True, stop=True)
                mm.then_inc(S("cb_mm"), 1)
                if i >= 1:
                    pe.wait_ge(S("state"), i)
                    for g in range(SG):
                        mm = nc.tensor.matmul(bank[1][:, g * 256:(g + 1) * 256], xbcS[:, 6 + g, sl],
                                              state[:, g * 256:(g + 1) * 256], start=True, stop=True)
                    mm.then_inc(S("yoff_mm"), 1)
                if i < NT - 1:
                    pe.wait_ge(S("xw"), i + 1)
                    pe.wait_ge(S("tok_out"), 2 * i + 2)
                    for g in range(SG):
                        mm = nc.tensor.matmul(bank[2][:, g * 256:(g + 1) * 256], btok[:, i, g * P:(g + 1) * P],
                                              xw[:, g * 256:(g + 1) * 256], start=True, stop=True)
                    mm.then_inc(S("st_mm"), 1)
                for g in range(SG):
                    pe.wait_ge(S("mt"), 2 * i + g + 1)
                    for h in range(4):
                        hh = 4 * g + h
                        mm = nc.tensor.matmul(bank[0][:, hh * SD:(hh + 1) * SD], seg[:, g, h, :],
                                              xdt[:, hh * SD:(hh + 1) * SD], start=True, stop=True)
                mm.then_inc(S("yd_mm"), 1)

            pe.wait_ge(S("T_in0"), 16)
            pe.wait_ge(S("selm"), NT - 1)
            pe.wait_ge(S("y_gated"), NT)
            even_att.pe(pe)
            even_att.done(pe)
            pe.wait_ge(S("ssm_row"), NT)
            turn_pe(pe, "eo", lambda i, k: rows_m[:, k // 4, i, (k % 4) * P:(k % 4 + 1) * P], lambda e, i: None)
            outproj_pe(pe, "eo", mixT, e_wo, None)

        def even_act(act):
            for half in range(2):
                act.wait_ge(S("bias_mm"), half + 1)
                nc.scalar.activation(brow[0:HEADS, half * 512:(half + 1) * 512], bank[4 + half][0:HEADS, :],
                                     ACT.Copy).then_inc(S("brow"), 1)
            norm_act(act, "n0", lambda e: e.wait_ge(S("x_in"), 16 * NT))
            for i in range(NT):
                turn_evac(act, "n0", hT, i, 0)

            def ev(n, dst, src, scale=1.0):
                act.wait_ge(S("ep_mm"), n + 1)
                return nc.scalar.activation(dst, src, ACT.Copy)
            for j in range(2):
                ev(J_IQ + j, iqT[:, j, :], bank[J_IQ + j][:, :]).then_inc(S("ep_ev"), 1)
            act.wait_ge(S("pads"), 2)
            ev(J_IK, ikA[0:HD, :], bank[J_IK][0:HD, :])
            nc.scalar.activation(ikB[HD:P, :], bank[J_IK][HD:P, :], ACT.Copy).then_inc(S("ep_ev"), 1)
            ev(J_IW, iw[:], split(bank[J_IW][:, 0:NT * IH], NT, IH)).then_inc(S("ep_ev"), 1)
            turned(act, "n0")
            for u, (i, h) in enumerate(SC):
                L = (i + 1) * P
                act.wait_ge(S("ix_mm"), u + 1)
                if u >= 2:
                    act.wait_ge(S("ix_acc"), u - 1)
                nc.scalar.activation(relu[:, u % 2, 0:L], bank[4 + u % 2][:, 0:L], ACT.Relu,
                                     scale=float(ID * IH) ** -0.5).then_inc(S("ix_relu"), 1)
            act.wait_ge(S("pads"), 3)
            for c in range(CT):
                n = J_XBC + c
                ev(n, xbcT[:, c, TAPS - 1:], bank[n % 4][:, :]).then_inc(S("ep_ev"), 1)
            for j in range(2):
                n = J_KV + j
                w = 2 * HD + SH
                ev(n, kvd[:, 2 * j:2 * j + 2, :], split(bank[n % 4][:, 0:2 * w], 2, w)).then_inc(S("ep_ev"), 1)
            for i in range(NT):
                n = J_Z + i
                ev(n, z[:, i, :], bank[n % 4][:, :]).then_inc(S("ep_ev"), 1)
            act.wait_ge(S("bias_out"), 16)
            for i in range(NT):
                n = J_Q + i
                ev(n, qrows[:, i, :], bank[n % 4][:, :]).then_inc(S("ep_ev"), 1)
            act.wait_ge(S("ep_mm"), J_END)
            act.wait_ge(S("ep_ev"), J_END)
            nc.scalar.activation(split(junk[:, 0:NT * HD], NT, HD), kvd[:, :, 0:HD], ACT.Square).then_inc(S("sq"), 1)
            for i in range(NT):
                act.wait_ge(S("ssq"), i + 1)
                nc.scalar.activation(junk, qrows[:, i, :], ACT.Square).then_inc(S("sq"), 1)
            act.wait_ge(S("dt_abs"), 1)
            act.wait_ge(S("par_in"), 16 * 12)
            nc.scalar.activation(dt_e[:], dt_e[:], ACT.Exp, scale=-1.0).then_inc(S("dt_exp"), 1)
            nc.scalar.activation(a_log[:], a_log[:], ACT.Exp).then_inc(S("a_exp"), 1)
            act.wait_ge(S("dt_exp"), 1)
            nc.scalar.activation(dt_e[:], dt_e[:], ACT.Ln, bias=1.0).then_inc(S("dt_ln"), 1)
            act.wait_ge(S("qk_turned"), 1)
            act.wait_ge(S("pads"), 5)
            act.wait_ge(S("hgain"), 1)
            nc.scalar.activation(kA[0:HD, :], bank[0][0:HD, :], ACT.Copy, scale=head_gain[0:HD, 1:2]).then_inc(S("qk_out"), 1)
            nc.scalar.activation(kB[HD:P, :], bank[0][HD:P, :], ACT.Copy, scale=head_gain[HD:P, 1:2]).then_inc(S("qk_out"), 1)
            for i in range(NT):
                act.wait_ge(S("qk_turned"), i + 2)
                nc.scalar.activation(eqT[:, :, i * P:(i + 1) * P], split(bank[1 + i % 2][:, :], 4, P), ACT.Copy,
                                     scale=head_gain[:, 0:1]).then_inc(S("qk_out"), 1)
            for c in range(CT):
                act.wait_ge(S("conv"), c + 1)
                nc.scalar.activation(xbcS[:, c, :], xbcS[:, c, :], ACT.Silu, bias=conv_b[:, c:c + 1]).then_inc(S("silu"), 1)
            nc.scalar.activation(z, z, ACT.Silu).then_inc(S("z_silu"), 1)
            for i in range(NT):
                act.wait_ge(S("tok_turned"), 2 * i + 1)
                nc.scalar.activation(xtok[:, i, :], bank[4][:, :], ACT.Copy).then_inc(S("tok_out"), 1)
                act.wait_ge(S("tok_turned"), 2 * i + 2)
                nc.scalar.activation(btok[:, i, :], bank[5][:, 0:SG * SN], ACT.Copy).then_inc(S("tok_out"), 1)
            act.wait_ge(S("acum"), 1)
            nc.scalar.activation(eac[:], acum[:], ACT.Exp).then_inc(S("eac"), 1)
            for i in range(NT):
                act.wait_ge(S("alast"), i + 1)
                nc.scalar.activation(to_end[:], to_end[:], ACT.Exp).then_inc(S("ends"), 1)
                nc.scalar.activation(cdecay[:], alast[:], ACT.Exp).then_inc(S("ends"), 1)
                for g in range(SG):
                    act.wait_ge(S("seg"), 2 * i + g + 1)
                    nc.scalar.activation(seg[:, g], seg[:, g], ACT.Exp).then_inc(S("decay"), 1)
                act.wait_ge(S("y_gated"), i + 1)
                for g in range(SG):
                    nc.scalar.activation(junk[:, g * 256:(g + 1) * 256], y_t[:, g * 256:(g + 1) * 256], ACT.Square,
                                         accum_out=ssg[:, g:g + 1]).then_inc(S("y_sq"), 1)
            even_att.act(act)
            for i in range(NT):
                turn_evac(act, "eo", mixT, i, 0)

        def even_pool(pool):
            steps = 0

            def c(ins_):
                nonlocal steps
                steps += 1
                ins_.then_inc(S("pool_const"), 1)
            g_ = nc.gpsimd
            c(g_.memset(ident[:], 0.0)); c(g_.memset(ones[:], 1.0)); c(g_.memset(tri[:], 1.0))
            c(g_.memset(tri_strict[:], 1.0)); c(g_.memset(score_base[:], 0.0)); c(g_.memset(nhalf[:], -0.5))
            c(g_.memset(minus1[:], -1.0))
            c(g_.iota(iota32[:], [[1, NE]], base=0, channel_multiplier=0, allow_small_or_imprecise_dtypes=True))
            c(g_.iota(row_off[:], [[CAP, NE]], base=0, channel_multiplier=0, allow_small_or_imprecise_dtypes=True))
            c(g_.iota(more_at[:], [[CAP, MORE]], base=CAP, channel_multiplier=0, allow_small_or_imprecise_dtypes=True))
            c(g_.iota(first_rows[:], [[1, CAP]], base=0, channel_multiplier=0, allow_small_or_imprecise_dtypes=True))
            pool.wait_ge(S("pool_const"), steps)
            c(g_.affine_select(out=ident[:], in_=ident[:], compare_op=ALU.not_equal, fill=1.0, base=0,
                               pattern=[[-1, P]], channel_multiplier=1))
            c(g_.affine_select(out=tri[:], in_=tri[:], compare_op=ALU.is_ge, fill=0.0, base=0,
                               pattern=[[1, P]], channel_multiplier=-1))
            c(g_.affine_select(out=tri_strict[:], in_=tri_strict[:], compare_op=ALU.is_gt, fill=0.0, base=0,
                               pattern=[[1, P]], channel_multiplier=-1))
            c(g_.affine_select(out=score_base[:, SEQ - P:], in_=score_base[:, SEQ - P:], compare_op=ALU.is_ge, fill=NEG,
                               base=0, pattern=[[-1, P]], channel_multiplier=1))
            c(g_.memset(relb[:], 1.0))
            pool.wait_ge(S("pool_const"), steps)
            g_.tensor_copy(identb[:], ident[:]).then_inc(S("consts"), 1)
            g_.sem_inc(S("relb_ones"), 1)
            g_.memset(ikA, 0.0).then_inc(S("pads"), 1)
            g_.memset(ikB, 0.0).then_inc(S("pads"), 1)
            g_.memset(xbcT[:, :, 0:TAPS - 1], 0.0).then_inc(S("pads"), 1)
            g_.memset(kA, 0.0).then_inc(S("pads"), 1)
            g_.memset(kB, 0.0).then_inc(S("pads"), 1)
            norm_pool(pool, "n0")
            pool.wait_ge(S("par_in"), 16 * 12)
            g_.tensor_scalar(head_gain[:, 0:1], head_gain[:, 0:1], HD ** -0.5, None, ALU.mult).then_inc(S("hgain"), 1)
            pool.wait_ge(S("ssq"), NT + 1)
            g_.tensor_scalar(ssq[:], ssq[:], 1.0 / HD, EPS, ALU.mult, ALU.add).then_inc(S("ssq_ms"), 1)
            pool.wait_ge(S("ssq_ms"), 1)
            g_.tensor_tensor(ssq[:], ssq[:], split(nhalf[:, 0:NT * (HEADS + 1)], NT, HEADS + 1), ALU.pow).then_inc(S("ssq_rstd"), 1)
            for i in range(NT):
                pool.wait_ge(S("y_sq"), 2 * i + 2)
                g_.tensor_scalar(ssg[:], ssg[:], 1.0 / (DI // SG), EPS, ALU.mult, ALU.add).then_inc(S("y_ms"), 1)
                pool.wait_ge(S("y_ms"), i + 1)
                g_.tensor_tensor(ssg[:], ssg[:], nhalf[:, 0:2], ALU.pow).then_inc(S("y_rstd"), 1)
            pool.wait_ge(S("qk_out"), NT + 2)
            pool.wait_ge(S("T_in0"), 16)
            pool.wait_ge(S("y_gated"), NT)
            pool.wait_ge(S("yd_mm"), NT)
            even_att.pool(pool)

        def heads_bc(ap, w):
            return ap.unsqueeze(2).broadcast_to((P, ap.shape[1], w))

        def even_dve(dve, link):
            v_ = nc.vector
            norm_dve(dve, "n0", 1)
            dve.wait_ge(S("ep_ev"), J_IW + 1)
            for u, (i, h) in enumerate(SC):
                L = (i + 1) * P
                dve.wait_ge(S("ix_relu"), u + 1)
                sc = score[:, i - 1, 0:L]
                v_.scalar_tensor_tensor(sc, relu[:, u % 2, 0:L], iw[:, i, h:h + 1],
                                        score_base[:, SEQ - L:] if h == 0 else sc, ALU.mult, ALU.add).then_inc(S("ix_acc"), 1)
                dve.wait_ge(S("ix_acc"), u + 1)
            for i in range(1, NT):
                L = (i + 1) * P
                sc = score[:, i - 1, 0:L]
                with dve.Fori(0, TOPK // 16) as r:
                    link.enter(r, 4)
                    for _ in range(2):
                        link(v_.max(m8[:], sc))
                        link(v_.match_replace(sc, m8[:], sc, TAKEN))
                    link.leave(TOPK // 16)
                v_.tensor_scalar(selm[:, i, 0:L], sc, TAKEN / 2, NEG, ALU.is_gt, ALU.mult).then_inc(S("selm"), 1)
            dve.wait_ge(S("ep_ev"), J_XBC + CT)
            dve.wait_ge(S("par_in"), 16 * 12)
            with dve.Fori(0, CT) as c:
                link.enter(c, TAPS - 1)
                o = xbcS[:, bass.ds(c, 1), :]
                for k in range(TAPS):
                    x_ = xbcT[:, bass.ds(c, 1), k:k + SEQ]
                    w_ = conv_w[:, k, bass.ds(c, 1)]
                    if k == 0:
                        link(v_.tensor_scalar(o, x_, w_, None, ALU.mult))
                    else:
                        ins_ = v_.scalar_tensor_tensor(o, x_, w_, o, ALU.mult, ALU.add)
                        if k < TAPS - 1:
                            link(ins_)
                        else:
                            ins_.then_inc(S("conv"), 1)
                link.leave(CT)
            dve.wait_ge(S("sq"), 1)
            v_.tensor_reduce(ssq[:, :, HEADS:HEADS + 1], split(junk[:, 0:NT * HD], NT, HD), AX.X, ALU.add).then_inc(S("ssq"), 1)
            for i in range(NT):
                dve.wait_ge(S("sq"), i + 2)
                v_.tensor_reduce(ssq[:, i, 0:HEADS], split(junk, HEADS, HD), AX.X, ALU.add).then_inc(S("ssq"), 1)
            link(v_.tensor_tensor(dt[:], kvd[:, :, 2 * HD:], dt_bias[:].unsqueeze(1).broadcast_to((P, NT, SH)), ALU.add))
            link(v_.tensor_scalar(dt_e[:], dt[:], -1.0, None, ALU.mult))
            v_.tensor_tensor(dt_e[:], dt_e[:], dt[:], ALU.max).then_inc(S("dt_abs"), 1)
            dve.wait_ge(S("ssq_rstd"), 1)
            for q in range(2):
                v_.tensor_tensor(krn[:, :, q * HD:(q + 1) * HD], kvd[:, :, 0:HD],
                                 ssq[:, :, HEADS:HEADS + 1].broadcast_to((P, NT, HD)), ALU.mult).then_inc(S("kn"), 1)
            for i in range(NT):
                q_ = split(qrows[:, i, :], HEADS, HD)
                v_.tensor_tensor(q_, q_, heads_bc(ssq[:, i, 0:HEADS], HD), ALU.mult).then_inc(S("qn"), 1)
            dve.wait_ge(S("dt_ln"), 1)
            link(v_.scalar_tensor_tensor(dt[:], dt[:], 0.0, dt_e[:], ALU.max, ALU.add))
            dve.wait_ge(S("a_exp"), 1)
            v_.scalar_tensor_tensor(dA[:], dt[:], -1.0, a_log[:].unsqueeze(1).broadcast_to((P, NT, SH)),
                                    ALU.mult, ALU.mult).then_inc(S("dA"), 1)
            dve.wait_ge(S("acum_mm"), 1)
            v_.tensor_copy(acum[:], split(bank[3][:, 0:NT * SH], NT, SH)).then_inc(S("acum"), 1)
            dve.wait_ge(S("acum"), 1)
            dve.wait_ge(S("eac"), 1)
            dve.wait_ge(S("z_silu"), 1)
            dve.wait_ge(S("ssm_gain_in"), 16)
            for i in range(NT):
                for g in range(SG):
                    dve.wait_ge(S("abc_mm"), 2 * i + g + 1)
                    link(v_.tensor_copy(alast[:, 4 * g:4 * g + 4], split(bank[6 + g][:, :], 4, P)[:, :, P - 1]))
                v_.tensor_tensor(to_end[:], alast[:], acum[:, i, :], ALU.subtract).then_inc(S("alast"), 1)
                if i >= 1:
                    dve.wait_ge(S("yd_mm"), i)
                for g in range(SG):
                    for h in range(4):
                        hh = 4 * g + h
                        ins_ = v_.tensor_scalar(seg[:, g, h, :], bank[6 + g][:, h * P:(h + 1) * P],
                                                acum[:, i, hh:hh + 1], 0.0, ALU.subtract, ALU.min)
                    ins_.then_inc(S("seg"), 1)
                dve.wait_ge(S("cb_mm"), i + 1)
                v_.tensor_tensor(cbm, split(bank[3][:, 0:SG * P], SG, P), tri[:].unsqueeze(1).broadcast_to((P, SG, P)),
                                 ALU.mult).then_inc(S("cbm"), 1)
                dve.wait_ge(S("tok_out"), 2 * i + 1)
                link(v_.tensor_tensor(split(xdt, SH, SD), split(xtok[:, i, :], SH, SD), heads_bc(dt[:, i, :], SD), ALU.mult))
                dve.wait_ge(S("ends"), 2 * i + 2)
                if i < NT - 1:
                    if i >= 1:
                        dve.wait_ge(S("st_mm"), i)
                    v_.tensor_tensor(split(xw, SH, SD), split(xdt, SH, SD), heads_bc(to_end[:], SD), ALU.mult).then_inc(S("xw"), 1)
                for g in range(SG):
                    dve.wait_ge(S("decay"), 2 * i + g + 1)
                    dve.wait_ge(S("cbm"), i + 1)
                    v_.tensor_tensor(seg[:, g], seg[:, g], cbm[:, g:g + 1, :].broadcast_to((P, 4, P)), ALU.mult).then_inc(S("mt"), 1)
                link(v_.tensor_tensor(split(y2, SH, SD), split(xtok[:, i, :], SH, SD), heads_bc(d_skip[:], SD), ALU.mult))
                if i >= 1:
                    dve.wait_ge(S("yoff_mm"), i)
                    dve.wait_ge(S("ssm_row"), i)
                    link(v_.tensor_tensor(split(y_t, SH, SD), split(bank[1][:, :], SH, SD), heads_bc(eac[:, i, :], SD), ALU.mult))
                    link(v_.tensor_tensor(y2, y2, y_t, ALU.add))
                if i < NT - 1:
                    dve.wait_ge(S("st_mm"), i + 1)
                    if i == 0:
                        v_.tensor_copy(state, bank[2][:, :]).then_inc(S("state"), 1)
                    else:
                        link(v_.tensor_tensor(split(state, SH, SD), split(state, SH, SD), heads_bc(cdecay[:], SD), ALU.mult))
                        v_.tensor_tensor(state, state, bank[2][:, :], ALU.add).then_inc(S("state"), 1)
                dve.wait_ge(S("yd_mm"), i + 1)
                link(v_.tensor_tensor(y2, y2, bank[0][:, :], ALU.add))
                v_.tensor_tensor(y_t, y2, z[:, i, :], ALU.mult).then_inc(S("y_gated"), 1)
                dve.wait_ge(S("y_rstd"), i + 1)
                for g in range(SG):
                    cs = slice(g * 256, (g + 1) * 256)
                    ins_ = v_.scalar_tensor_tensor(rows_m[:, 0, i, cs], y_t[:, cs], ssg[:, g:g + 1], ssm_gain[:, cs],
                                                   ALU.mult, ALU.mult)
                ins_.then_inc(S("ssm_row"), 1)
            dve.wait_ge(S("T_in0"), 16)
            even_att.dve(dve, link)
            for i in range(NT):
                turn_evac(dve, "eo", mixT, i, 1)
            outproj_dve(dve, "eo")

        @contextmanager
        def loop_pairs(eng, link=None):
            with eng.Fori(0, HEADS // 4) as it:
                if link:
                    link.enter(it, 0)
                yield it, it
                if link:
                    link.leave(HEADS // 4)

        def flat(ap):
            return ap.rearrange("p a b -> p (a b)")

        def even_weigh(a, pool, it, s, m, i):
            return nc.gpsimd.tensor_tensor(a.coef[:, m % 4, :], a.sums[:, m % 4, :], minus1[:, 0:2], ALU.pow)

        def even_finish(a, dve, link, it, s, m, i):
            o = rows_m[:, 1, i, :].rearrange("p (j q d) -> p j q d", q=2, d=HD)[:, bass.ds(2 * it + s, 1), :, :]
            return nc.vector.tensor_tensor(o, split(bank[4 + m % 2][:, 0:2 * HD], 1, 2, HD),
                                           a.coef[:, m % 4, :].unsqueeze(1).unsqueeze(3).broadcast_to((P, 1, 2, HD)), ALU.mult)

        def tile_bias(i):
            return slice(SEQ - P - i * P, SEQ - P - i * P + (i + 1) * P)

        even_branches = [[dict(L=(i + 1) * P, D=HD, bias=lambda b, i=i, q=q: b[:, q, tile_bias(i)],
                               k=lambda it, i=i, q=q: (kA, kB)[q][:, 0:(i + 1) * P],
                               mask=selm[:, i, 0:(i + 1) * P] if i else None,
                               v=lambda it, kt: kvd[:, kt, HD:2 * HD]) for q in range(2)] for i in range(NT)]
        even_att = Attention("ea", even_branches, loop_pairs, HEADS // 4,
                             [at(O_XBCS + n * SEQ, SEQ) for n in range(STAGES)],
                             [at(O_XBCS + STAGES * SEQ + n * 2 * TW, 2, TW) for n in range(STAGES)],
                             lambda it, s: flat(eqT[:, bass.ds(2 * it + s, 1), :]),
                             lambda it, s: split(arena[:, 0:HEADS * TW], HEADS // 2, 2, TW)[:, bass.ds(2 * it + s, 1), :, :],
                             O_EW, even_weigh, even_finish)

        o0 = HEADS * TW
        oqT = at(o0, HEADS, SEQ); o0 += HEADS * SEQ
        O_KROWS = o0
        krows = at(o0, 2, NT, OKV); o0 += 2 * NT * OKV
        kT = at(o0, 2, OG, SEQ); o0 += 2 * OG * SEQ
        vv = at(o0, 2, NT, OKV); o0 += 2 * NT * OKV
        O_CT = o0
        cT = at(o0, 2, OG, SEQ); o0 += 2 * OG * SEQ
        blk = [at(o0 + q * OG * CB * NC, CB, OG * NC) for q in range(2)]
        ojunk = at(o0, DM)
        o_work = o0
        o0 += 2 * OG * CB * NC
        O_OW = 2 * EW
        cw2 = at(o0, 2, OD); o0 += 2 * OD
        kcT = at(o0, OG, NC); o0 += OG * NC
        kc_rows, kc_sq, vc = (split(arena[0:NC, o0 + n * OG * OD:o0 + (n + 1) * OG * OD], OG, OD) for n in range(3))
        o0 += 3 * OG * OD
        assert o0 <= O_OW and 6 * SEQ <= 2 * OG * CB * NC and STAGES * TW <= 2 * NT * OKV and STAGES * SEQ <= 2 * OG * SEQ
        ow = [at(O_OW + n * KD * 512, KD, 512) for n in range(3)]
        cw1 = [at(O_OW + n * KD * 512, CB, OD) for n in range(3)]
        o_wo = [hT, ow[0]]
        o_mixT = at(O_OW + KD * 512, KD, SEQ)
        gl = sb("gl", [P, NT, 3, HEADS])
        gates = sb("gates", [P, NT, HEADS, 3])
        oss = sb("oss", [P, NT, HEADS + 4])
        qk_gain = sb("qk_gain", [P, 4])
        posT = sb("posT", [P, 2, CB])
        hidT_c = sb("hidT_c", [P, 2, OG * NC])
        kc_ss = sb("kc_ss", [NC, OG])

        w_odd = ins["odd_w_in"][0]
        OD_CHUNKS = [[(C_OK, 512)], [(C_OK + 512, 256), (C_OK + 1024, 256)], [(C_OK + 768, 256), (C_OK + 1280, 256)],
                     [(0, 512)], [(512, 512)], [(C_GL, 3 * HEADS)]]
        K_C, K_K, K_V, K_Q, K_G, K_END = 0, 4, 8, 12, 20, 21
        OD_JOBS = [4, 8, 12, 16, 20, 21]

        def odd_sp(sp):
            sp.wait_ge(S("m_x"), 2 * NT)
            sp.dma_start(gain[:], bcast_rows(ins["attn_norm"][1, :], DM)).then_inc(S("gain_in"), 16)
            for c in range(3):
                load_chunk(sp, c, OD_CHUNKS, w_odd, ow, "op", OD_JOBS)
            for n, name in enumerate(("odd_q_norm", "odd_ks_norm", "odd_kw_norm", "odd_kc_norm")):
                sp.dma_start(qk_gain[:, n:n + 1], ins[name][0].rearrange("(p c) -> p c", c=1)).then_inc(S("opar_in"), 16)
            for n, name in enumerate(("odd_cmp_pos_k", "odd_cmp_pos_v")):
                sp.dma_start(posT[:, n, :], ins[name][0].rearrange("r d -> d r")).then_inc(S("opar_in"), 16)
            for n, name in enumerate(("odd_cmp_k_w2", "odd_cmp_v_w2")):
                sp.dma_start(cw2[:, n, :], ins[name][0]).then_inc(S("opar_in"), 16)
            for c in range(3, 6):
                load_chunk(sp, c, OD_CHUNKS, w_odd, ow, "op", OD_JOBS)
            load_bias(sp, "T_in1")
            for n, name in enumerate(("odd_cmp_k_w1", "odd_cmp_v_w1")):
                sp.wait_ge(S("op_mm"), past("op_mm") + OD_JOBS[3 + n])
                sp.dma_start(cw1[n], ins[name][0].rearrange("(r d) h -> d r h", d=OD)).then_inc(S(f"cw1_in{n}"), 16)
            sp.wait_ge(S("op_mm"), past("op_mm") + K_END)
            sp.dma_start(o_wo[0], ins["odd_w_out"][0, :, 0:512].rearrange("(k p) c -> p k c", p=P)).then_inc(S("oo_w0"), 16)
            sp.wait_ge(S("c_hid"), past("c_hid") + 2)
            sp.dma_start(o_wo[1], ins["odd_w_out"][0, :, 512:1024].rearrange("(k p) c -> p k c", p=P)).then_inc(S("oo_w1"), 16)

        def odd_pe(pe):
            turn_pe(pe, "n2", lambda i, k: rows[:, i, k * P:(k + 1) * P], lambda e, i: rows_ready(e, "n2", i + 1))
            turned(pe, "n2")

            def job(n, runs):
                if n >= 4:
                    pe.wait_ge(S("op_ev"), past("op_ev") + n - 3)
                for o, lhs, rhs in runs:
                    for k in range(KD):
                        mm = nc.tensor.matmul(o, lhs(k), rhs(k), start=(k == 0), stop=(k == KD - 1))
                mm.then_inc(S("op_mm"), 1)

            def tokens(n, w, i, cols):
                job(n, [(bank[n % 4][:, 0:cols], lambda k: hT[:, k, i * P:(i + 1) * P], lambda k: w[:, k, 0:cols])])

            pe.wait_ge(S("op_w0"), past("op_w0") + 16)
            for j in range(4):
                job(K_C + j, [(bank[j][:, :], lambda k: ow[0][:, k, j * P:(j + 1) * P], lambda k: hT[:, k, :])])
            for c, first in ((1, K_K), (2, K_V)):
                pe.wait_ge(S(f"op_w{c}"), past(f"op_w{c}") + 32)
                for i in range(NT):
                    tokens(first + i, ow[c], i, 512)
            for c in range(2):
                pe.wait_ge(S(f"op_w{3 + c}"), past(f"op_w{3 + c}") + 16)
                for i in range(NT):
                    tokens(K_Q + 4 * c + i, ow[c], i, 512)
            pe.wait_ge(S("op_w5"), past("op_w5") + 16)
            job(K_G, [(bank[K_G % 4][:, i * 3 * HEADS:(i + 1) * 3 * HEADS], lambda k, i=i: hT[:, k, i * P:(i + 1) * P],
                       lambda k: ow[2][:, k, 0:3 * HEADS]) for i in range(NT)])
            pe.wait_ge(S("op_ev"), past("op_ev") + K_END)

            for q in range(2):
                pe.wait_ge(S(f"cw1_in{q}"), past(f"cw1_in{q}") + 16)
                pe.wait_ge(S("blk"), past("blk") + 2 * q + 2)
                for r in range(CB):
                    mm = nc.tensor.matmul(bank[6 + q][:, 0:OG * NC], cw1[q][:, r, :], blk[q][:, r, :],
                                          start=(r == 0), stop=(r == CB - 1))
                mm.then_inc(S("c_hid"), 1)
            for i in range(NT):
                pe.wait_ge(S("ok_n"), past("ok_n") + 2 * i + 2)
                for q in range(2):
                    n = 2 * i + q
                    if n >= 2:
                        pe.wait_ge(S("ok_out"), past("ok_out") + n - 1)
                    for g in range(OG):
                        mm = nc.tensor.transpose(bank[n % 2][:, g * P:(g + 1) * P], krows[:, q, i, g * OD:(g + 1) * OD], ident[:])
                    mm.then_inc(S("ok_turned"), 1)
            for i in range(NT):
                pe.wait_ge(S("oq_n"), past("oq_n") + i + 1)
                for half in range(2):
                    n = 2 * i + half
                    if n >= 2:
                        pe.wait_ge(S("oq_out"), past("oq_out") + n - 1)
                    for j in range(4):
                        c = (4 * half + j) * P
                        mm = nc.tensor.transpose(bank[2 + n % 2][:, j * P:(j + 1) * P], rows[:, i, c:c + P], ident[:])
                    mm.then_inc(S("oq_turned"), 1)
            for q in range(2):
                pe.wait_ge(S("hid_c"), past("hid_c") + q + 1)
                for g in range(OG):
                    mm = nc.tensor.matmul(bank[4 + q][0:NC, g * P:(g + 1) * P], hidT_c[:, q, g * NC:(g + 1) * NC],
                                          cw2[:, q, :], start=True, stop=True)
                mm.then_inc(S("c_rows"), 1)
            pe.wait_ge(S("kc_n"), past("kc_n") + 1)
            for g in range(OG):
                mm = nc.tensor.transpose(bank[7][:, g * NC:(g + 1) * NC], kc_rows[:, g, :], ident[0:NC, 0:NC])
            mm.then_inc(S("kc_turned"), 1)
            pe.wait_ge(S("kcT"), past("kcT") + 1)
            pe.wait_ge(S("ok_out"), past("ok_out") + 2 * NT)
            pe.wait_ge(S("oq_out"), past("oq_out") + 2 * NT)
            odd_att.pe(pe)
            odd_att.done(pe)
            turn_pe(pe, "oo", lambda i, k: rows[:, i, k * P:(k + 1) * P], lambda e, i: None)
            outproj_pe(pe, "oo", o_mixT, o_wo, None)

        def odd_act(act):
            norm_act(act, "n2", lambda e: e.wait_ge(S("m_x"), 2 * NT))
            for i in range(NT):
                turn_evac(act, "n2", hT, i, 0)

            def ev(n, dst, src):
                act.wait_ge(S("op_mm"), past("op_mm") + n + 1)
                nc.scalar.activation(dst, src, ACT.Copy).then_inc(S("op_ev"), 1)
            for j in range(4):
                ev(K_C + j, cT[:, j // 2, j % 2, :], bank[j][:, :])
            for dst, first in ((krows, K_K), (vv, K_V)):
                for i in range(NT):
                    ev(first + i, dst[:, :, i, :], split(bank[(first + i) % 4][:, :], 2, OKV))
            turned(act, "n2")
            for c in range(2):
                for i in range(NT):
                    n = K_Q + 4 * c + i
                    ev(n, rows[:, i, c * 512:(c + 1) * 512], bank[n % 4][:, :])
            ev(K_G, gl[:], bank[K_G % 4][:, 0:NT * 3 * HEADS].rearrange("p (i b h) -> p i b h", i=NT, b=3))
            for q in range(2):
                act.wait_ge(S("c_hid"), past("c_hid") + q + 1)
                nc.scalar.activation(hidT_c[:, q, :], bank[6 + q][:, 0:OG * NC], ACT.Silu).then_inc(S("hid_c"), 1)
            act.wait_ge(S("op_ev"), past("op_ev") + K_END)
            nc.scalar.activation(gl[:], gl[:], ACT.Exp, scale=-1.0).then_inc(S("gl_exp"), 1)
            act.wait_ge(S("opar_in"), past("opar_in") + 16 * 8)
            for i in range(NT):
                for q in range(2):
                    act.wait_ge(S("ok_turned"), past("ok_turned") + 2 * i + q + 1)
                    nc.scalar.activation(kT[:, q, :, i * P:(i + 1) * P], split(bank[q][:, 0:2 * P], OG, P), ACT.Copy,
                                         scale=qk_gain[:, 1 + q:2 + q]).then_inc(S("ok_out"), 1)
            act.wait_ge(S("qscale"), past("qscale") + 1)
            for i in range(NT):
                for half in range(2):
                    act.wait_ge(S("oq_turned"), past("oq_turned") + 2 * i + half + 1)
                    nc.scalar.activation(oqT[:, 4 * half:4 * half + 4, i * P:(i + 1) * P], split(bank[2 + half][:, :], 4, P),
                                         ACT.Copy, scale=qk_gain[:, 0:1]).then_inc(S("oq_out"), 1)
            act.wait_ge(S("c_rows"), past("c_rows") + 1)
            nc.scalar.activation(kc_rows, split(bank[4][0:NC, 0:OG * OD], OG, OD), ACT.Copy).then_inc(S("kc_raw"), 1)
            act.wait_ge(S("c_rows"), past("c_rows") + 2)
            nc.scalar.activation(vc, split(bank[5][0:NC, 0:OG * OD], OG, OD), ACT.Copy).then_inc(S("kc_raw"), 1)
            act.wait_ge(S("kc_turned"), past("kc_turned") + 1)
            nc.scalar.activation(kcT, split(bank[7][:, 0:OG * NC], OG, NC), ACT.Copy, scale=qk_gain[:, 3:4]).then_inc(S("kcT"), 1)
            odd_att.act(act)
            for i in range(NT):
                turn_evac(act, "oo", o_mixT, i, 0)

        def odd_pool(pool):
            g_ = nc.gpsimd
            norm_pool(pool, "n2")
            pool.wait_ge(S("opar_in"), past("opar_in") + 16 * 8)
            g_.tensor_scalar(qk_gain[:, 0:1], qk_gain[:, 0:1], OD ** -0.5, None, ALU.mult).then_inc(S("qscale"), 1)
            pool.wait_ge(S("oss"), past("oss") + 3 * NT)
            g_.tensor_scalar(oss[:], oss[:], 1.0 / OD, EPS, ALU.mult, ALU.add).then_inc(S("oss_ms"), 1)
            pool.wait_ge(S("oss_ms"), past("oss_ms") + 1)
            g_.tensor_tensor(oss[:, 0:2], oss[:, 0:2], split(nhalf[:, 0:2 * 12], 2, 12), ALU.pow).then_inc(S("oss_rstd"), 1)
            g_.tensor_tensor(oss[:, 2:4], oss[:, 2:4], split(nhalf[:, 0:2 * 12], 2, 12), ALU.pow).then_inc(S("oss_rstd"), 1)
            pool.wait_ge(S("kc_ss"), past("kc_ss") + 1)
            g_.tensor_scalar(kc_ss[:], kc_ss[:], 1.0 / OD, EPS, ALU.mult, ALU.add).then_inc(S("kc_ms"), 1)
            pool.wait_ge(S("kc_ms"), past("kc_ms") + 1)
            g_.tensor_tensor(kc_ss[:], kc_ss[:], nhalf[0:NC, 0:OG], ALU.pow).then_inc(S("kc_rstd"), 1)
            pool.wait_ge(S("oq_out"), past("oq_out") + 2 * NT)
            pool.wait_ge(S("T_in1"), past("T_in1") + 16)
            pool.wait_ge(S("ok_turned"), past("ok_turned") + 2 * NT)
            pool.wait_ge(S("blk"), past("blk") + 4)
            pool.wait_ge(S("gates"), 1)
            odd_att.pool(pool)

        def odd_dve(dve, link):
            v_ = nc.vector
            norm_dve(dve, "n2", 3)
            for i in range(NT):
                dve.wait_ge(S("op_ev"), past("op_ev") + K_K + i + 1)
                for q in range(2):
                    k_ = krows[:, q, i, :]
                    link(v_.tensor_tensor(ojunk[:, 0:OKV], k_, k_, ALU.mult))
                    ins_ = v_.tensor_reduce(oss[:, i, HEADS + 2 * q:HEADS + 2 * q + 2], split(ojunk[:, 0:OKV], OG, OD), AX.X, ALU.add)
                    if q == 0:
                        link(ins_)
                    else:
                        ins_.then_inc(S("oss"), 1)
                        dve.wait_ge(S("oss"), past("oss") + i + 1)
            for c in range(2):
                for i in range(NT):
                    dve.wait_ge(S("op_ev"), past("op_ev") + K_Q + 4 * c + i + 1)
                    q_ = rows[:, i, c * 512:(c + 1) * 512]
                    link(v_.tensor_tensor(ojunk[:, 0:512], q_, q_, ALU.mult))
                    v_.tensor_reduce(oss[:, i, 4 * c:4 * c + 4], split(ojunk[:, 0:512], 4, OD), AX.X, ALU.add).then_inc(S("oss"), 1)
                    dve.wait_ge(S("oss"), past("oss") + NT + 4 * c + i + 1)
            dve.wait_ge(S("opar_in"), past("opar_in") + 16 * 8)
            for q in range(2):
                for g in range(OG):
                    src = cT[:, q, g, :]
                    win = bass.AP(src.tensor, src.offset, [list(src.ap[0]), [1, CB], [CS, NC]])
                    v_.tensor_tensor(blk[q][:, :, g * NC:(g + 1) * NC], win,
                                     posT[:, q, :].unsqueeze(2).broadcast_to((P, CB, NC)), ALU.add).then_inc(S("blk"), 1)
            dve.wait_ge(S("oss_rstd"), past("oss_rstd") + 2)
            for i in range(NT):
                for q in range(2):
                    k_ = split(krows[:, q, i, :], OG, OD)
                    v_.tensor_tensor(k_, k_, heads_bc(oss[:, i, HEADS + 2 * q:HEADS + 2 * q + 2], OD), ALU.mult).then_inc(S("ok_n"), 1)
            for i in range(NT):
                q_ = split(rows[:, i, :], HEADS, OD)
                v_.tensor_tensor(q_, q_, heads_bc(oss[:, i, 0:HEADS], OD), ALU.mult).then_inc(S("oq_n"), 1)
            dve.wait_ge(S("gl_exp"), past("gl_exp") + 1)
            link(v_.tensor_scalar(gl[:], gl[:], 1.0, None, ALU.add))
            v_.reciprocal(gates[:].rearrange("p i h b -> p i b h"), gl[:]).then_inc(S("gates"), 1)
            dve.wait_ge(S("kc_raw"), past("kc_raw") + 1)
            link(v_.tensor_tensor(kc_sq, kc_rows, kc_rows, ALU.mult))
            v_.tensor_reduce(kc_ss[:].unsqueeze(2), kc_sq, AX.X, ALU.add).then_inc(S("kc_ss"), 1)
            dve.wait_ge(S("kc_rstd"), past("kc_rstd") + 1)
            v_.tensor_tensor(kc_rows, kc_rows, kc_ss[:].unsqueeze(2).broadcast_to((NC, OG, OD)), ALU.mult).then_inc(S("kc_n"), 1)
            dve.wait_ge(S("T_in1"), past("T_in1") + 16)
            odd_att.dve(dve, link)
            for i in range(NT):
                turn_evac(dve, "oo", o_mixT, i, 1)
            outproj_dve(dve, "oo")

        @contextmanager
        def loop_heads(eng, link=None):
            links = 3 * M
            per = HPG // STAGES
            with eng.Fori(0, OG) as g:
                with eng.Fori(0, per) as n:
                    it = g * per + n
                    if link:
                        link.enter(it, links)
                    yield it, (g, it)
                    if link:
                        link.leave(1)
                        link.n -= links
            if link:
                link.n += OG * per * links

        def odd_weigh(a, pool, it, s, m, i):
            c_ = a.coef[:, m % 4, :]
            nc.gpsimd.tensor_scalar(c_, a.sums[:, m % 4, :], 1e-30, None, ALU.max).then_inc(S("recip"), 1)
            wait_apart(pool, (S("recip"), 2 * (it * M + m) + 1))
            nc.gpsimd.tensor_tensor(c_, c_, minus1[:], ALU.pow).then_inc(S("recip"), 1)
            wait_apart(pool, (S("recip"), 2 * (it * M + m) + 2))
            return nc.gpsimd.tensor_tensor(c_, c_, flat(gates[:, i, bass.ds(2 * it + s, 1), :]), ALU.mult)

        def odd_finish(a, dve, link, v, s, m, i):
            h = bass.ds(2 * v[1] + s, 1)
            c_ = a.coef[:, m % 4, :]
            y = flat(split(rows[:, i, :], HEADS, OD)[:, h, :])
            b_ = bank[4 + m % 2]
            link(nc.vector.tensor_scalar(y, b_[:, 0:OD], c_[:, 0:1], None, ALU.mult))
            link(nc.vector.scalar_tensor_tensor(y, b_[:, OD:2 * OD], c_[:, 1:2], y, ALU.mult, ALU.add))
            return nc.vector.scalar_tensor_tensor(y, b_[:, 2 * OD:3 * OD], c_[:, 2:3], y, ALU.mult, ALU.add)

        def o_compressed(i):
            u0 = tile_bias(i).start + CB - 1
            return dict(L=NC, D=OD, clamp=True, bias=lambda b: b[:, u0:u0 + CS * (NC - 1) + 1:CS],
                        k=lambda v: flat(kcT[:, bass.ds(v[0], 1), :]),
                        v=lambda v, kt: flat(vc[:, bass.ds(v[0], 1), :]))

        def o_branch(i, q):
            return dict(L=(i + 1) * P, D=OD, bias=lambda b: b[:, tile_bias(i)],
                        k=lambda v: flat(kT[:, q, bass.ds(v[0], 1), 0:(i + 1) * P]),
                        v=lambda v, kt: flat(split(vv[:, q, kt, :], OG, OD)[:, bass.ds(v[0], 1), :]))

        odd_att = Attention("oa", [[o_compressed(i), o_branch(i, 0), o_branch(i, 1)] for i in range(NT)],
                            loop_heads, HEADS // STAGES,
                            [at(O_CT + n * SEQ, SEQ) for n in range(STAGES)],
                            [at(O_KROWS + n * TW, TW) for n in range(STAGES)],
                            lambda it, s: flat(oqT[:, bass.ds(2 * it + s, 1), :]),
                            lambda it, s: flat(T[:, bass.ds(2 * it + s, 1), :]),
                            o_work, odd_weigh, odd_finish, before=even_att)

        router_w = [sb(f"router_w{n}", [P, KD, NR]) for n in range(2)]
        dest = sb("dest", [P, 2, NT], I32)
        weight = sb("weight", [P, 2, NT])
        more_i = sb("more_i", [P, 1 + NX], I32)
        dest_f = sb("dest_f", [P, 2 * NT])
        blk_rows = sb("blk_rows", [P, CAP])
        xe = at(O_HT, 512)
        xeT = at(O_HT + 512, 4, P)
        hidT = at(O_HT + 1024, 2, P)
        act_g = at(O_HT + 1280, FH)
        hid = at(O_HT + 1536, FH)
        yb = at(O_HT + 1792, RING, 512)
        same = at(O_HT + 3328, 2, NT, CAP)
        pick = at(O_HT + 3328 + 2 * NT * CAP, NT, CAP)
        y_rows = at(O_HT, 2, NT, DM)
        wgu = [at(u * EW, 2, KD, FF) for u in range(RING)]
        wd = [at(u * EW + 2 * KD * FF, FF // P, DM) for u in range(RING)]
        r0 = 2 * EW + 2 * KD * FF
        lgt = at(r0, NT, NR); r0 += NT * NR
        cand = at(r0, NT, EPG); r0 += NT * EPG
        eqs = at(r0, NT, EPG); r0 += NT * EPG
        oh_g = at(r0, NT, MG); r0 += NT * MG
        es = at(r0, NT, EPG); r0 += NT * EPG
        oh_e = at(r0, 2, NT, EPG); r0 += 2 * NT * EPG
        prod = at(r0, 2 * NT, NE); r0 += 2 * NT * NE
        oh = at(r0, 2, NT, NE); r0 += 2 * NT * NE
        oh_sum = at(r0, NT, NE); r0 += NT * NE
        before = at(r0, NT, NE); r0 += NT * NE
        load = at(r0, NE); r0 += NE
        xn = at(r0, NE); r0 += NE
        xend = at(r0, NE); r0 += NE
        xrow = at(r0, NE); r0 += NE
        cmp_ = at(r0, NE, MORE); r0 += NE * MORE
        cmpx = at(r0, NX, NE); r0 += NX * NE
        more_f = at(r0, 1 + NX); r0 += 1 + NX
        small = at(r0, 12, NT); r0 += 12 * NT
        pos = at(r0, 2 * NT); r0 += 2 * NT
        base = at(r0, 2 * NT); r0 += 2 * NT
        xbase = at(r0, 2 * NT); r0 += 2 * NT
        over = at(r0, 2 * NT); r0 += 2 * NT
        onesr = at(r0, NE); r0 += NE
        assert r0 <= RING * EW and 3328 + 3 * NT * CAP <= KD * SEQ

        def gate_up_weights(sp, t, layer, e, u):
            for n, name in enumerate(("moe_w_gate", "moe_w_up")):
                src = ins[name][layer, bass.ds(e, 1)].rearrange("e (h p j) f -> p (e h) (j f)", h=2, j=4)
                sp.dma_start(wgu[u][:, n].rearrange("p (h j) f -> p h (j f)", h=2), src).then_inc(S(f"{t}_wgu{u}"), 16)

        def down_weights(sp, t, layer, e, u):
            src = ins["moe_w_down"][layer, bass.ds(e, 1)].rearrange("e (h p j) d -> p (e h) (j d)", h=2, j=2)
            sp.dma_start(wd[u].rearrange("p (h j) d -> p h (j d)", h=2), src).then_inc(S(f"{t}_wd{u}"), 16)

        def weights(sp, t, layer, e, u):
            gate_up_weights(sp, t, layer, e, u)
            down_weights(sp, t, layer, e, u)

        def pick_ones(link):
            link(nc.vector.tensor_tensor(
                same.rearrange("p a b c -> p (a b) c"), dest_f[:].unsqueeze(2).broadcast_to((P, 2 * NT, CAP)),
                blk_rows[:].unsqueeze(1).broadcast_to((P, 2 * NT, CAP)), ALU.is_equal))
            link(nc.vector.tensor_scalar(blk_rows[:], blk_rows[:], float(CAP), None, ALU.add))
            return nc.vector.tensor_tensor(pick, same[:, 0], same[:, 1], ALU.add)

        def pick_rows():
            for i in range(NT):
                for h in range(2):
                    mm = nc.tensor.matmul(bank[4][h * CAP:(h + 1) * CAP, :], pick[:, i, :], rows[:, i, h * 512:(h + 1) * 512],
                                          start=(i == 0), stop=(i == NT - 1))
            return mm

        def copy_picked():
            return nc.scalar.activation(xe, bank[4][:, :], ACT.Copy)

        def turn_rows():
            for j in range(4):
                mm = nc.tensor.transpose(bank[0][:, j * P:(j + 1) * P], xe[:, j::4], ident[:])
            return mm

        def copy_x():
            return nc.scalar.activation(xeT, split(bank[0][:, :], 4, P), ACT.Copy)

        def gate_up_mms(u):
            for n in range(KD):
                half, j = n // 4, n % 4
                for fh in range(2):
                    mm = nc.tensor.matmul(bank[1][fh * CAP:(fh + 1) * CAP, :], xeT[:, j, half * CAP:(half + 1) * CAP],
                                          wgu[u][:, :, n, fh * FH:(fh + 1) * FH], start=(n == 0), stop=(n == KD - 1))
            return mm

        def turn_hidden():
            for j in range(2):
                mm = nc.tensor.transpose(bank[2][:, j * P:(j + 1) * P], hid[:, j::2], ident[:])
            return mm

        def down_mms(u):
            for n in range(FF // P):
                fh, j = n // 2, n % 2
                for dh in range(2):
                    mm = nc.tensor.matmul(bank[3][dh * CAP:(dh + 1) * CAP, :], hidT[:, j, fh * CAP:(fh + 1) * CAP],
                                          wd[u][:, n, dh * 512:(dh + 1) * 512], start=(n == 0), stop=(n == FF // P - 1))
            return mm

        def store_y(act, t, layer, u, blk_n):
            d = y_d[layer].rearrange("(b s) (h c) -> b h s c", s=CAP, h=2)[bass.ds(blk_n, 1)]
            for h in range(2):
                act.dma_start(d[:, h].rearrange("b s c -> (b s) c"), yb[h * CAP:(h + 1) * CAP, u, :]).then_inc(S(f"{t}_yout{u}"), 16)

        (X_ONES, X_PICKED, X_ROWS, X_TURN, X_XT, X_GU, X_G, X_HID, X_HTURN, X_HT, X_DN, X_Y) = range(1, 13)
        X_STEPS = 12

        def x_step(eng, x, j, step):
            eng.wait_ge(S(f"{x}_step"), j * X_STEPS + 1 + step)

        def ones_for(dve, t, c, link):
            wait_apart(dve, (S(f"{t}_picked"), c + 1))
            pick_ones(link).then_inc(S(f"{t}_ones"), 1)

        def picked(pe, t, c):
            pe.wait_ge(S(f"{t}_ones"), c + 1)
            pe.wait_ge(S(f"{t}_rows"), c + 1)
            pick_rows().then_inc(S(f"{t}_picked"), 1)

        def rows_out(act, t, c):
            act.wait_ge(S(f"{t}_picked"), c + 2)
            act.wait_ge(S(f"{t}_xturn"), c + 1)
            copy_picked().then_inc(S(f"{t}_rows"), 1)

        def x_turn(pe, t, c):
            pe.wait_ge(S(f"{t}_rows"), c + 2)
            pe.wait_ge(S(f"{t}_xT"), c + 1)
            turn_rows().then_inc(S(f"{t}_xturn"), 1)

        def gate_up(pe, t, c, cu, u):
            pe.wait_ge(S(f"{t}_xT"), c + 2)
            pe.wait_ge(S(f"{t}_hid"), c + 1)
            pe.wait_ge(S(f"{t}_wgu{u}"), 32 * (cu + 1))
            gate_up_mms(u).then_inc(S(f"{t}_gu"), 1)

        def hid_turn(pe, t, c):
            pe.wait_ge(S(f"{t}_hid"), c + 2)
            turn_hidden().then_inc(S(f"{t}_hturn"), 1)

        def down(pe, t, c, cu, u):
            pe.wait_ge(S(f"{t}_hT"), c + 2)
            pe.wait_ge(S(f"{t}_y"), c + 1)
            pe.wait_ge(S(f"{t}_wd{u}"), 16 * (cu + 1))
            down_mms(u).then_inc(S(f"{t}_dn"), 1)

        def x_out(act, t, c):
            act.wait_ge(S(f"{t}_xturn"), c + 2)
            copy_x().then_inc(S(f"{t}_xT"), 1)

        def silu(act, t, c):
            act.wait_ge(S(f"{t}_gu"), c + 1)
            act.wait_ge(S(f"{t}_hid"), c + 1)
            nc.scalar.activation(act_g, bank[1][:, 0:FH], ACT.Silu).then_inc(S(f"{t}_g"), 1)

        def y_out(act, t, layer, c, cu, u, blk_n):
            act.wait_ge(S(f"{t}_dn"), c + 2)
            act.wait_ge(S(f"{t}_yout{u}"), 16 * (cu + 1))
            nc.scalar.activation(yb[:, u, :], bank[3][:, :], ACT.Copy).then_inc(S(f"{t}_y"), 1)
            act.wait_ge(S(f"{t}_y"), c + 2)
            store_y(act, t, layer, u, blk_n)

        def hidden(dve, t, c):
            dve.wait_ge(S(f"{t}_g"), c + 1)
            dve.wait_ge(S(f"{t}_hturn"), c + 1)
            nc.vector.tensor_tensor(hid, act_g, bank[1][:, FH:2 * FH], ALU.mult).then_inc(S(f"{t}_hid"), 1)

        def hid_out(dve, t, c):
            dve.wait_ge(S(f"{t}_hturn"), c + 2)
            nc.vector.tensor_copy(hidT, split(bank[2][:, 0:2 * P], 2, P)).then_inc(S(f"{t}_hT"), 1)

        def per_expert(eng, L, body, link=None):
            with eng.Fori(0, TRIPS) as it:
                if link:
                    link.enter(it, 2 * RING)
                for u in range(RING):
                    body(it * RING + u, it * RING + u + L * NE, it + L * uses(u), u, 2)
                if link:
                    link.leave(TRIPS)
            for u in range(NE - RING * TRIPS):
                e = RING * TRIPS + u
                body(e, e + L * NE, TRIPS + L * uses(u), u, NE - 1 - e)

        def uses(u):
            return TRIPS + (1 if u < NE - RING * TRIPS else 0)

        def fence(eng, t, L):
            for u in range(RING):
                eng.wait_ge(S(f"{t}_yout{u}"), 32 * uses(u) * (L + 1) + 16)

        def further(eng, t, layer, body, first=None, last=None, none=None):
            n = eng.value_load(more_i[0:1, 0:1], min_val=0, max_val=NX)
            with eng.If(n > 0):
                fence(eng, t, layer)
                if first:
                    first()
                if body:
                    with eng.Fori(0, NX) as j:
                        with eng.If(n > j):
                            body(j)
                        with eng.Else():
                            eng.nop()
                        eng.nop()
                if last:
                    last(n)
            with eng.Else():
                if none:
                    none()
                else:
                    eng.nop()
            eng.nop()

        def moe_sp(sp, L, mixed, prev_norm, att):
            t, x = "m", f"mx{L}"
            rows_ready(sp, prev_norm, NT)
            sp.dma_start(gain[:], bcast_rows(ins["ffn_norm"][L, :], DM)).then_inc(S("gain_in"), 16)
            sp.dma_start(router_w[L][:, :, 0:MG], ins["moe_router_group"][L].rearrange("(k p) g -> p k g", p=P)).then_inc(S(f"{t}_rw"), 16)
            for g in range(MG):
                sp.dma_start(router_w[L][:, :, MG + g * EPG:MG + (g + 1) * EPG],
                             ins["moe_router_expert"][L, g].rearrange("(k p) e -> p k e", p=P)).then_inc(S(f"{t}_rw"), 16)
            att.done(sp)
            for u in range(2):
                weights(sp, t, L, u, u)
            sp.wait_ge(S(f"{mixed}_add"), past(f"{mixed}_add") + 2 * NT)
            gate_up_weights(sp, t, L, 2, 2)
            sp.wait_ge(S(f"{t}_routed"), past("m_routed") + L + 1)
            down_weights(sp, t, L, 2, 2)
            with sp.Fori(0, TRIPS - 1) as it:
                for u in range(RING):
                    sp.wait_ge(S(f"{t}_dn"), it * RING + u + 2 + L * NE)
                    weights(sp, t, L, it * RING + u + RING, u)
            for u in range(NE - RING * TRIPS):
                sp.wait_ge(S(f"{t}_dn"), RING * (TRIPS - 1) + u + 2 + L * NE)
                weights(sp, t, L, RING * TRIPS + u, u)

            def body(j):
                sp.wait_ge(S(f"{x}_step"), j * X_STEPS + 1)
                e = sp.value_load(more_i[0:1, bass.ds(j + 1, 1)], min_val=0, max_val=NE - 1)
                weights(sp, x, L, e, 0)
            further(sp, t, L, body)

        def moe_pe(pe, L):
            t, x = "m", f"mx{L}"
            pe.sem_inc(S(f"{x}_step"), 1)
            if L == 0:
                pe.sem_inc(S(f"{t}_dn"), 1)
                pe.sem_inc(S(f"{t}_hturn"), 1)
                pe.sem_inc(S(f"{t}_xturn"), 1)
                pe.sem_inc(S(f"{t}_picked"), 1)
            turn_pe(pe, f"m{L}n", lambda i, k: rows[:, i, k * P:(k + 1) * P], lambda e, i: rows_ready(e, f"m{L}n", i + 1))
            turned(pe, f"m{L}n")
            pe.wait_ge(S(f"{t}_rw"), past("m_rw") + 16 * 5 * (L + 1))
            for i in range(NT):
                for k in range(KD):
                    mm = nc.tensor.matmul(bank[4][:, i * NR:(i + 1) * NR], hT[:, k, i * P:(i + 1) * P], router_w[L][:, k, :],
                                          start=(k == 0), stop=(k == KD - 1))
            mm.then_inc(S(f"{t}_rmm"), 1)
            pe.wait_ge(S(f"{t}_oh"), past("m_oh") + L + 1)
            for i in range(NT):
                for j in range(i + 1):
                    mm = nc.tensor.matmul(bank[5][:, i * NE:(i + 1) * NE], (tri_strict if j == i else ones)[:], oh_sum[:, j, :],
                                          start=(j == 0), stop=(j == i))
            for j in range(NT):
                mm = nc.tensor.matmul(bank[6][:, 0:NE], ones[:], oh_sum[:, j, :], start=(j == 0), stop=(j == NT - 1))
            mm.then_inc(S(f"{t}_cnt"), 1)
            picked(pe, t, L * NE)
            x_turn(pe, t, L * NE)
            picked(pe, t, L * NE + 1)

            def body(e, c, cu, u, after):
                gate_up(pe, t, c, cu, u)
                if after >= 1:
                    x_turn(pe, t, c + 1)
                if after >= 2:
                    picked(pe, t, c + 2)
                hid_turn(pe, t, c)
                down(pe, t, c, cu, u)
            per_expert(pe, L, body)

            def more(j):
                x_step(pe, x, j, X_ONES)
                pick_rows().then_inc(S(f"{x}_step"), 1)
                x_step(pe, x, j, X_ROWS)
                turn_rows().then_inc(S(f"{x}_step"), 1)
                x_step(pe, x, j, X_XT)
                pe.wait_ge(S(f"{x}_wgu0"), 32 * (j + 1))
                gate_up_mms(0).then_inc(S(f"{x}_step"), 1)
                x_step(pe, x, j, X_HID)
                turn_hidden().then_inc(S(f"{x}_step"), 1)
                x_step(pe, x, j, X_HT)
                pe.wait_ge(S(f"{x}_wd0"), 16 * (j + 1))
                down_mms(0).then_inc(S(f"{x}_step"), 1)
            further(pe, t, L, more)

        def moe_act(act, L, x_ready):
            t, x = "m", f"mx{L}"
            if L == 0:
                act.sem_inc(S(f"{t}_xT"), 1)
                act.sem_inc(S(f"{t}_y"), 1)
                act.sem_inc(S(f"{t}_rows"), 1)
                for u in range(RING):
                    act.sem_inc(S(f"{t}_yout{u}"), 16)
            norm_act(act, f"m{L}n", x_ready)
            for i in range(NT):
                turn_evac(act, f"m{L}n", hT, i, 0)
            act.wait_ge(S(f"{t}_d"), 2 * L + 1)
            nc.scalar.activation(small[:, 0:4, :], small[:, 0:4, :], ACT.Exp).then_inc(S(f"{t}_exp"), 1)
            act.wait_ge(S(f"{t}_d"), 2 * L + 2)
            nc.scalar.activation(small[:, 8, :], small[:, 8, :], ACT.Exp).then_inc(S(f"{t}_exp"), 1)
            rows_out(act, t, L * NE)
            x_out(act, t, L * NE)
            rows_out(act, t, L * NE + 1)

            def body(e, c, cu, u, after):
                silu(act, t, c)
                if after >= 1:
                    x_out(act, t, c + 1)
                if after >= 2:
                    rows_out(act, t, c + 2)
                y_out(act, t, L, c, cu * 2, u, e)
            per_expert(act, L, body)

            def more(j):
                x_step(act, x, j, X_PICKED)
                copy_picked().then_inc(S(f"{x}_step"), 1)
                x_step(act, x, j, X_TURN)
                copy_x().then_inc(S(f"{x}_step"), 1)
                x_step(act, x, j, X_GU)
                nc.scalar.activation(act_g, bank[1][:, 0:FH], ACT.Silu).then_inc(S(f"{x}_step"), 1)
                x_step(act, x, j, X_DN)
                nc.scalar.activation(yb[:, 0, :], bank[3][:, :], ACT.Copy).then_inc(S(f"{x}_y"), 1)
                act.wait_ge(S(f"{x}_y"), j + 1)
                store_y(act, x, L, 0, NE + j)
                act.wait_ge(S(f"{x}_yout0"), 32 * (j + 1))
                act.sem_inc(S(f"{x}_step"), 1)
            further(act, t, L, more, first=lambda: act.wait_ge(S(f"{x}_zero"), 16))

        def moe_pool(pool, L):
            t, x = "m", f"mx{L}"
            norm_pool(pool, f"m{L}n")
            pool.wait_ge(S(f"{t}_dest"), past("m_dest") + L + 1)
            def zero_rows():
                nc.gpsimd.memset(y_rows[:, 0, 0, :], 0.0).then_inc(S(f"{x}_zeroed"), 1)
                pool.wait_ge(S(f"{x}_zeroed"), 1)
                pool.dma_start(y_d[L][NE * CAP:, :].rearrange("(a p) c -> p a c", p=4 * NX),
                               y_rows[0:4 * NX, 0, 0:1, :].broadcast_to((4 * NX, CAP // 4, DM))).then_inc(S(f"{x}_zero"), 16)
                pool.wait_ge(S(f"{x}_zero"), 16)

            def fetch(n_rows):
                for i in range(NT):
                    for k in range(2):
                        nc.gpsimd.indirect_dma_start(
                            out=y_rows[:, k, i, :], out_offset=None, in_=y_d[L][0:n_rows, :],
                            in_offset=bass.IndirectOffsetOnAxis(ap=dest[:, k, i:i + 1], axis=0)).then_inc(S(f"{t}_yin{i}"), 16)

            def all_made(n):
                wait_apart(pool, (S(f"{x}_step"), n * X_STEPS + 1))
                fetch(ROWS)

            def none():
                fence(pool, t, L)
                fetch(NE * CAP)
            further(pool, t, L, None, zero_rows, all_made, none)

        def moe_dve(dve, L, link, gain_n):
            t, x = "m", f"mx{L}"
            v_ = nc.vector
            if L == 0:
                dve.sem_inc(S(f"{t}_hid"), 1)
                dve.sem_inc(S(f"{t}_hT"), 1)
            norm_dve(dve, f"m{L}n", gain_n)
            dve.wait_ge(S(f"{t}_rmm"), past("m_rmm") + L + 1)
            link(v_.tensor_copy(lgt, split(bank[4][:, 0:NT * NR], NT, NR)))
            gl_, el_ = lgt[:, :, 0:MG], lgt[:, :, MG:].rearrange("p i (g e) -> p i g e", g=MG)

            def bc(ap, n):
                return ap.unsqueeze(2).broadcast_to((P, NT, n))

            def first_max(vals, n, mx, onehot):
                link(v_.tensor_reduce(mx.unsqueeze(2), vals, AX.X, ALU.max))
                link(v_.tensor_tensor(eqs[:, :, 0:n], vals, bc(mx, n), ALU.is_equal))
                link(v_.scalar_tensor_tensor(cand[:, :, 0:n], eqs[:, :, 0:n], -100.0,
                                             iota32[:, 0:n].unsqueeze(1).broadcast_to((P, NT, n)), ALU.mult, ALU.add))
                link(v_.tensor_reduce(small[:, 11, :].unsqueeze(2), cand[:, :, 0:n], AX.X, ALU.min))
                link(v_.tensor_tensor(onehot, cand[:, :, 0:n], bc(small[:, 11, :], n), ALU.is_equal))

            first_max(gl_, MG, small[:, 4, :], oh_g)
            v_.tensor_tensor(small[:, 0:4, :].rearrange("p g i -> p i g"), gl_, bc(small[:, 4, :], MG), ALU.subtract).then_inc(S(f"{t}_d"), 1)
            pg = prod[:, 0:NT, :].rearrange("p i (e g) -> p i e g", g=MG)
            link(v_.tensor_tensor(pg, el_.rearrange("p i g e -> p i e g"), oh_g.unsqueeze(2).broadcast_to((P, NT, EPG, MG)), ALU.mult))
            link(v_.tensor_reduce(es.unsqueeze(3), pg, AX.X, ALU.add))
            first_max(es, EPG, small[:, 5, :], oh_e[:, 0])
            link(v_.scalar_tensor_tensor(es, oh_e[:, 0], NEG, es, ALU.mult, ALU.add))
            first_max(es, EPG, small[:, 6, :], oh_e[:, 1])
            v_.tensor_tensor(small[:, 8, :], small[:, 6, :], small[:, 5, :], ALU.subtract).then_inc(S(f"{t}_d"), 1)
            for k in range(2):
                ins_ = v_.tensor_tensor(oh[:, k].rearrange("p i (g e) -> p i g e", g=MG), oh_g.unsqueeze(3).broadcast_to((P, NT, MG, EPG)),
                                        oh_e[:, k].unsqueeze(2).broadcast_to((P, NT, MG, EPG)), ALU.mult)
                link(ins_)
            v_.tensor_tensor(oh_sum, oh[:, 0], oh[:, 1], ALU.add).then_inc(S(f"{t}_oh"), 1)
            dve.wait_ge(S(f"{t}_exp"), 2 * L + 1)
            link(v_.tensor_reduce(small[:, 7, :].unsqueeze(2), small[:, 0:4, :].rearrange("p g i -> p i g"), AX.X, ALU.add))
            dve.wait_ge(S(f"{t}_exp"), 2 * L + 2)
            link(v_.tensor_scalar(small[:, 9, :], small[:, 8, :], 1.0, None, ALU.add))
            link(v_.tensor_tensor(small[:, 9, :], small[:, 9, :], small[:, 7, :], ALU.mult))
            link(v_.reciprocal(weight[:, 0, :], small[:, 9, :]))
            link(v_.tensor_tensor(weight[:, 1, :], weight[:, 0, :], small[:, 8, :], ALU.mult))
            dve.wait_ge(S(f"{t}_cnt"), past("m_cnt") + L + 1)
            v_.tensor_copy(before, split(bank[5][:, 0:NT * NE], NT, NE))
            link(v_.tensor_copy(load, bank[6][:, 0:NE]))
            link(v_.memset(onesr, 1.0))
            link(v_.tensor_tensor(cmp_, load.unsqueeze(2).broadcast_to((P, NE, MORE)), more_at[:].unsqueeze(1).broadcast_to((P, NE, MORE)), ALU.is_gt))
            link(v_.tensor_reduce(xn.unsqueeze(2), cmp_, AX.X, ALU.add))
            link(v_.tensor_tensor_scan(xend, onesr, xn, 0.0, ALU.mult, ALU.add))
            link(v_.tensor_tensor(xrow, xend, xn, ALU.subtract))
            link(v_.tensor_scalar(xrow, xrow, float(CAP), float(CAP * NE - CAP), ALU.mult, ALU.add))
            link(v_.tensor_tensor(cmpx, xend.unsqueeze(1).broadcast_to((P, NX, NE)), iota32[:, 0:NX].unsqueeze(2).broadcast_to((P, NX, NE)), ALU.is_le))
            link(v_.tensor_reduce(more_f[:, 1:].unsqueeze(2), cmpx, AX.X, ALU.add))
            link(v_.tensor_copy(more_f[:, 0:1], xend[:, NE - 1:NE]))
            link(v_.tensor_scalar(more_i[:], more_f, float(NE - 1), None, ALU.min))
            ohf = oh.rearrange("p k i e -> p (k i) e")
            for k in range(2):
                link(v_.tensor_tensor(split(prod.rearrange("p a b -> p (a b)"), 2, NT, NE)[:, k], oh[:, k], before, ALU.mult))
            link(v_.tensor_reduce(pos.unsqueeze(2), prod, AX.X, ALU.add))
            for tab, o in ((row_off[:], base), (xrow, xbase)):
                link(v_.tensor_tensor(prod, ohf, tab.unsqueeze(1).broadcast_to((P, 2 * NT, NE)), ALU.mult))
                link(v_.tensor_reduce(o.unsqueeze(2), prod, AX.X, ALU.add))
            link(v_.tensor_scalar(over, pos, float(CAP), None, ALU.is_ge))
            link(v_.tensor_tensor(xbase, xbase, base, ALU.subtract))
            link(v_.tensor_tensor(xbase, xbase, over, ALU.mult))
            link(v_.tensor_tensor(pos, pos, base, ALU.add))
            link(v_.tensor_tensor(dest_f[:], pos, xbase, ALU.add))
            link(v_.tensor_copy(blk_rows[:], first_rows[:]))
            v_.tensor_copy(dest[:].rearrange("p k i -> p (k i)"), dest_f[:]).then_inc(S(f"{t}_dest"), 1)
            dve.wait_ge(S(f"{t}_dest"), past("m_dest") + L + 1)
            dve.sem_inc(S(f"{t}_routed"), 1)
            for c in range(2):
                ones_for(dve, t, L * NE + c, link)

            def body(e, c, cu, u, after):
                if after >= 2:
                    ones_for(dve, t, c + 2, link)
                hidden(dve, t, c)
                hid_out(dve, t, c)
            per_expert(dve, L, body, link)
            more_link = Chain(dve, S(f"{x}_chain"))

            def more(j):
                dve.wait_ge(S(f"{x}_step"), j * X_STEPS + 1)
                more_link.enter(j, 2)
                pick_ones(more_link).then_inc(S(f"{x}_step"), 1)
                more_link.leave(NX)
                x_step(dve, x, j, X_G)
                nc.vector.tensor_tensor(hid, act_g, bank[1][:, FH:2 * FH], ALU.mult).then_inc(S(f"{x}_step"), 1)
                x_step(dve, x, j, X_HTURN)
                nc.vector.tensor_copy(hidT, split(bank[2][:, 0:2 * P], 2, P)).then_inc(S(f"{x}_step"), 1)
            further(dve, t, L, more)
            for i in range(NT):
                dve.wait_ge(S(f"{t}_yin{i}"), 32 * (L + 1))
                for k in range(2):
                    v_.scalar_tensor_tensor(xt[:, i, :], y_rows[:, k, i, :], weight[:, k, i:i + 1], xt[:, i, :],
                                            ALU.mult, ALU.add).then_inc(S(f"{t}_x"), 1)
                    dve.wait_ge(S(f"{t}_x"), 2 * NT * L + 2 * i + k + 1)

        block = ctx.enter_context(nc.Block())

        @block.sync
        def _(sp):
            even_sp(sp)
            moe_sp(sp, 0, "eo", "n0", even_att)
            odd_sp(sp)
            moe_sp(sp, 1, "oo", "n2", odd_att)
            for i in range(NT):
                sp.wait_ge(S("m_x"), 2 * NT + 2 * i + 2)
                sp.dma_start(out[0, i * P:(i + 1) * P, :], xt[:, i, :]).then_inc(S("out"), 16)
            sp.wait_ge(S("out"), 16 * NT)

        @block.tensor
        def _(pe):
            even_pe(pe)
            moe_pe(pe, 0)
            odd_pe(pe)
            moe_pe(pe, 1)

        @block.scalar
        def _(act):
            even_act(act)
            moe_act(act, 0, lambda e: e.wait_ge(S("eo_add"), 2 * NT))
            odd_act(act)
            moe_act(act, 1, lambda e: e.wait_ge(S("oo_add"), past("oo_add") + 2 * NT))

        @block.gpsimd
        def _(pool):
            even_pool(pool)
            moe_pool(pool, 0)
            odd_pool(pool)
            moe_pool(pool, 1)

        @block.vector
        def _(dve):
            link = Chain(dve, S("dve_chain"))
            even_dve(dve, link)
            moe_dve(dve, 0, link, 2)
            odd_dve(dve, link)
            moe_dve(dve, 1, link, 4)


_INS = ['x', 'rel_bias', 'attn_norm', 'ffn_norm', 'even_w_in', 'even_conv_w', 'even_conv_b', 'even_dt_bias',
        'even_a_log', 'even_d_skip', 'even_ssm_norm', 'even_q_norm', 'even_k_norm', 'even_w_out', 'odd_w_in',
        'odd_q_norm', 'odd_kc_norm', 'odd_ks_norm', 'odd_kw_norm', 'odd_cmp_pos_k', 'odd_cmp_pos_v',
        'odd_cmp_k_w1', 'odd_cmp_k_w2', 'odd_cmp_v_w1', 'odd_cmp_v_w2', 'odd_w_out', 'moe_router_group',
        'moe_router_expert', 'moe_w_gate', 'moe_w_up', 'moe_w_down']


def kernel(**inputs):
    import concourse.bacc as bacc
    from concourse.bass_utils import run_bass_kernel_spmd

    nc = bacc.Bacc("TRN2", target_bir_lowering=False, num_devices=1)
    arrays, aps = {}, {}
    for name in _INS:
        arrays[f"in_{name}"] = np.ascontiguousarray(inputs[name])
    arrays["in_bucket_table"] = bucket_table()
    for name, a in arrays.items():
        aps[name[3:]] = nc.dram_tensor(name, a.shape, mybir.dt.from_np(a.dtype), kind="ExternalInput").ap()
    out = nc.dram_tensor("out_x", (1, SEQ, DM), F32, kind="ExternalOutput").ap()
    build(nc, aps, out)
    r = run_bass_kernel_spmd(nc, [arrays], core_ids=[0])
    return r.results[0]["out_x"]
```

```python
from contextlib import ExitStack, contextmanager

import numpy as np

import concourse.bass as bass
from concourse import mybir

F32 = mybir.dt.float32
BF16 = mybir.dt.bfloat16
I32 = mybir.dt.int32
ALU = mybir.AluOpType
ACT = mybir.ActivationFunctionType
AX = mybir.AxisListType

P = 128
SEQ, DM = 512, 1024
NT = SEQ // P
KD = DM // P
EPS = 1e-6
NEG = -1e30
CLAMP = 1e20
TAKEN = -3e38
NB, HEADS = 32, 8
BIAS_W = 2 * SEQ
TW = SEQ + P * (NT - 1)

SH, SD, SN, SG = 8, 64, 128, 2
DI = SH * SD
XBC = DI + 2 * SG * SN
CT = XBC // P
TAPS = 4
HD = 64
IH, ID = 4, 64
TOPK = min(256, SEQ // 4)
C_Z, C_XBC = 0, DI
C_DT = C_XBC + XBC
C_Q = C_DT + SH
C_K = C_Q + HEADS * HD
C_V = C_K + HD
C_IQ = C_V + HD
C_IK = C_IQ + IH * ID
C_IW = C_IK + ID
EVEN_COLS = C_IW + IH

OG, OD = 2, 128
HPG = HEADS // OG
CB, CS = 32, 16
NC = (SEQ - CB) // CS + 1
OKV = OG * OD
C_OK = HEADS * OD
C_GL = C_OK + 6 * OKV
ODD_COLS = C_GL + 3 * HEADS
assert SEQ // 64 <= 16 and SEQ <= 512

MG, EPG = 4, 8
NE = MG * EPG
FF = 512
NA = 2 * SEQ
CAP = 64
NX = (NA - 1) // (CAP + 1)
NBLK = NE + NX
ROWS = NBLK * CAP
NR = MG + NE
FH = FF // 2
EW = 2 * KD * FF + (FF // P) * DM
RING = 3
TRIPS = NE // RING
MORE = SEQ // CAP - 1

O_RING = 0
O_X = RING * EW
O_HT = O_X + NT * DM
O_ROWS = O_HT + KD * SEQ
ARENA = O_ROWS + NT * DM


def bucket_table():
    dist = np.arange(BIAS_W) - (SEQ - 1)
    d = np.maximum(dist, 1).astype(np.float32)
    large = NB // 2 + (np.log(d / np.float32(NB // 2)) / np.float32(np.log(128 / (NB // 2)))
                       * np.float32(NB // 2)).astype(np.int32)
    bucket = np.where(dist < NB // 2, np.maximum(dist, 0), np.minimum(large, NB - 1))
    table = np.zeros((NB + 1, BIAS_W), np.float32)
    table[:NB] = (np.arange(NB)[:, None] == bucket[None]) & (dist >= 0)[None]
    table[NB] = np.where(dist < 0, NEG, 0.0)
    return table


def wait_apart(eng, *waits):
    waits = [(sem, value if isinstance(value, int) else eng.to_reg(value)) for sem, value in waits]
    if not isinstance(waits[0][1], int):
        eng.wait_ge(waits[0][0], 1)
    for sem, value in waits:
        eng.wait_ge(sem, value)


class Chain:

    def __init__(self, eng, sem):
        self.eng, self.sem, self.n, self.term = eng, sem, 0, None

    def __call__(self, ins):
        self.n += 1
        ins.then_inc(self.sem, 1)
        if self.term is None:
            self.eng.wait_ge(self.sem, self.n)
        else:
            wait_apart(self.eng, (self.sem, self.n + self.term))

    def loose(self, ins):
        self.n += 1
        ins.then_inc(self.sem, 1)

    def enter(self, i, per_trip):
        self.term, self.start, self.per = i * per_trip, self.n, per_trip

    def leave(self, trips):
        assert self.n - self.start == self.per, (self.n - self.start, self.per)
        self.n, self.term = self.start + trips * self.per, None


COUNTS_ON = {
    "T_in1": ("T_in0", 16), "opar_in": ("par_in", 192), "op_ev": ("ep_ev", 22), "op_mm": ("ep_mm", 22),
    "op_w0": ("ep_w0", 16), "op_w1": ("ep_w1", 16), "op_w2": ("ep_w2", 16), "op_w3": ("ep_w3", 32),
    "op_w4": ("ep_w4", 16), "op_w5": ("ep_w5", 16), "oo_add": ("eo_add", 8), "oo_mm": ("eo_mm", 8),
    "oo_w0": ("eo_w0", 16), "oo_w1": ("eo_w1", 16), "blk": ("seg", 8), "c_hid": ("cb_mm", 4),
    "c_rows": ("abc_mm", 8), "cw1_in0": ("table_in", 32), "cw1_in1": ("ssm_gain_in", 16), "gl_exp": ("eac", 1),
    "hid_c": ("decay", 8), "kcT": ("z_silu", 4), "kc_ms": ("y_ms", 4), "kc_n": ("dA", 1), "kc_raw": ("a_exp", 1),
    "kc_rstd": ("y_rstd", 4), "kc_ss": ("acum", 1), "kc_turned": ("acum_mm", 1), "ok_n": ("mt", 8),
    "ok_out": ("tok_out", 8), "ok_turned": ("tok_turned", 8), "oq_n": ("qn", 4), "oq_out": ("qk_out", 6),
    "oq_turned": ("qk_turned", 5), "oss": ("ssq", 5), "oss_ms": ("ssq_ms", 5), "oss_rstd": ("ssq_rstd", 5),
    "qscale": ("hgain", 1),
    "m_rw": ("bias_out", 16), "m_rmm": ("bias_mm", 2), "m_oh": ("conv", 8),
    "m_cnt": ("ix_mm", 12), "m_dest": ("ix_acc", 12), "m_routed": ("selm", 3), 
    
}


def past(name):
    return COUNTS_ON[name][1] if name in COUNTS_ON else 0


class Env:

    def __init__(self, nc, ctx):
        self.nc, self.ctx, self.sems = nc, ctx, {}

    def sb(self, name, shape, dt=F32):
        return self.ctx.enter_context(self.nc.sbuf_tensor(name, shape, dt))

    def s(self, name):
        name = COUNTS_ON[name][0] if name in COUNTS_ON else name
        if name not in self.sems:
            self.sems[name] = self.ctx.enter_context(self.nc.semaphore(name))
        return self.sems[name]


def bcast_rows(ap, n, parts=P):
    return bass.AP(ap.tensor, ap.offset, [[0, parts], [1, n]])


def split(ap, *dims):
    names = "abcd"[:len(dims)]
    return ap.rearrange(f"p ({' '.join(names)}) -> p {' '.join(names)}", **dict(zip(names, dims)))


def build(nc, ins, out):
    ctx = ExitStack()
    with ctx:
        ctx.enter_context(nc.allow_non_contiguous_dma(reason="small parameters, channels onto partitions"))
        env = Env(nc, ctx)
        sb, S = env.sb, env.s
        dram = lambda name, shape: nc.dram_tensor(name, shape, F32, kind="Internal").ap()

        arena = sb("arena", [P, ARENA])
        bank = [ctx.enter_context(nc.psum_tensor(f"bank{n}", [P, 512], F32)) for n in range(8)]

        def at(off, *dims):
            n = int(np.prod(dims))
            return split(arena[:, off:off + n], *dims) if len(dims) > 1 else arena[:, off:off + n]

        bias_row_d = dram("bias_row_d", [HEADS, BIAS_W])
        y_d = [dram(f"y_d{n}", [ROWS, DM]) for n in range(2)]

        ident = sb("ident", [P, P])
        identb = sb("identb", [P, P], BF16)
        ones = sb("ones", [P, P])
        tri = sb("tri", [P, P])
        onesb = sb("onesb", [P, P], BF16)
        tri_strict = sb("tri_strict", [P, P], BF16)
        score_base = sb("score_base", [P, SEQ])
        minus1 = sb("minus1", [P, 3])
        nhalf = sb("nhalf", [P, 36])
        iota32 = sb("iota32", [P, NE])
        row_off = sb("row_off", [P, NE])
        more_at = sb("more_at", [P, MORE])
        first_rows = sb("first_rows", [P, CAP])
        gain = sb("gain", [P, DM])
        ss = sb("ss", [P, NT])
        rstd = sb("rstd", [P, NT])

        xt = at(O_X, NT, DM)
        hT = at(O_HT, KD, SEQ)
        rows = at(O_ROWS, NT, DM)

        NORM = {"n0": 0, "m0n": 1, "n2": 2, "m1n": 3}
        TURN = {"n0": 0, "eo": 1, "m0n": 2, "n2": 3, "oo": 4, "m1n": 5}

        def rows_ready(eng, tag, tiles):
            eng.wait_ge(S("norm_row"), NT * NORM[tag] + tiles)

        def norm_act(act, tag, x_ready):
            for i in range(NT):
                x_ready(act, i)
                nc.scalar.activation(rows[:, i, :], xt[:, i, :], ACT.Square,
                                     accum_out=ss[:, i:i + 1]).then_inc(S("norm_sq"), 1)

        def norm_pool(pool, tag):
            for i in range(NT):
                n = NT * NORM[tag] + i + 1
                pool.wait_ge(S("norm_sq"), n)
                s_ = ss[:, i:i + 1]
                nc.gpsimd.tensor_scalar(s_, s_, 1.0 / DM, EPS, ALU.mult, ALU.add).then_inc(S("norm_ms"), 1)
                pool.wait_ge(S("norm_ms"), n)
                nc.gpsimd.tensor_tensor(rstd[:, i:i + 1], s_, nhalf[:, 0:1], ALU.pow).then_inc(S("norm_rstd"), 1)

        def norm_row(dve, tag, i):
            dve.wait_ge(S("norm_rstd"), NT * NORM[tag] + i + 1)
            dve.wait_ge(S("gain_in"), 16 * (NORM[tag] + 1))
            nc.vector.scalar_tensor_tensor(rows[:, i, :], xt[:, i, :], rstd[:, i:i + 1], gain[:], ALU.mult,
                                           ALU.mult).then_inc(S("norm_row"), 1)

        def norm_turns(dve, tag):
            for i in range(NT):
                turn_evac(dve, tag, hT, i, 1)

        def turn_pe(pe, tag, src, ready, then=None):
            for i in range(NT + 1):
                if i == NT:
                    if then:
                        then(i - 1)
                    break
                ready(pe, i)
                for half in range(2):
                    if i >= 2:
                        pe.wait_ge(S(f"turn_out{half}"), NT * TURN[tag] + i - 1)
                    for k in range(4):
                        mm = nc.tensor.transpose(bank[(2 * i + half) % 4][:, k * P:(k + 1) * P],
                                                 src(i, 4 * half + k), ident[:])
                    mm.then_inc(S("turned"), 1)
                if then and i >= 1:
                    then(i - 1)

        def turn_evac(eng, tag, dst, i, half):
            eng.wait_ge(S("turned"), 2 * NT * TURN[tag] + 2 * i + half + 1)
            d = dst[:, 4 * half:4 * half + 4, i * P:(i + 1) * P]
            b = split(bank[(2 * i + half) % 4][:, :], 4, P)
            ins_ = nc.vector.tensor_copy(d, b) if half else nc.scalar.activation(d, b, ACT.Copy)
            ins_.then_inc(S(f"turn_out{half}"), 1)

        def turned(eng, tag):
            eng.wait_ge(S("turn_out0"), NT * (TURN[tag] + 1))
            eng.wait_ge(S("turn_out1"), NT * (TURN[tag] + 1))

        STAGES = 2
        M = STAGES * NT
        O_FIRST = 6
        score_bank = [bank[0], bank[1], bank[6], bank[7]]

        class Attention:
            def __init__(self, tag, branches, loop, trips, queries, biases, q_of, b_of, work, weigh, finish, before=None):
                self.trips, self.weigh = trips, weigh
                self.loop, self.queries, self.biases, self.q_of, self.b_of = loop, queries, biases, q_of, b_of
                self.finish, self.first = finish, before is None
                self.NB = len(branches[0])
                self.units = [(s, i, b, branches[i][b]) for s in range(STAGES) for i in range(NT) for b in range(self.NB)]
                self.U = len(self.units)
                self.t0, self.u0, self.m0 = (0, 0, 0) if before is None else before.after
                self.after = self.t0 + trips, self.u0 + trips * self.U, self.m0 + trips * M
                self.p = at(work, 4, SEQ)
                self.pT = at(work + 4 * SEQ, 2, 4, P)
                self.negm = sb(f"{tag}_negm", [P, 4])
                self.sums = sb(f"{tag}_sums", [P, 4, self.NB])
                self.coef = sb(f"{tag}_coef", [P, 4, self.NB])

            def sem(self, what):
                return S(f"att_{what}")

            def staged(self, it, s):
                return STAGES * (self.t0 + it) + s + 1

            def macros_ago(self, it, m, k):
                return self.sem("o"), self.m0 + it * M + m - k + 1 + O_FIRST

            def pe(self, pe):
                if self.first:
                    pe.sem_inc(self.sem("tr"), 4)
                    pe.sem_inc(self.sem("pv"), 2)
                with self.loop(pe) as (it, v):
                    for t in range(self.U + 3):
                        if t < self.U:
                            s, i, b, br = self.units[t]
                            n = self.u0 + it * self.U + t
                            if i == 0 and b == 0:
                                pe.wait_ge(self.sem("queries"), self.staged(it, s))
                            pe.wait_ge(self.sem("lg"), n + 1)
                            o = score_bank[t % 4][:, 0:br["L"]]
                            mm = nc.tensor.matmul(o, self.queries[s][:, i * P:(i + 1) * P], br["k"](v),
                                                  start=True, stop=not br.get("mask"))
                            if br.get("mask"):
                                mm = nc.tensor.matmul(o, identb[:], br["mask"], start=False, stop=True)
                            mm.then_inc(self.sem("qk"), 1)
                        if 2 <= t < self.U + 2:
                            s, i, b, br = self.units[t - 2]
                            n = self.u0 + it * self.U + t - 2
                            pe.wait_ge(self.sem("ex"), n + 1)
                            pe.wait_ge(self.sem("pt"), n + 1)
                            for kt in range((br["L"] + P - 1) // P):
                                w = min(P, br["L"] - kt * P)
                                mm = nc.tensor.transpose(bank[2 + t % 2][0:w, kt * P:(kt + 1) * P],
                                                         self.p[:, (t - 2) % 4, kt * P:kt * P + w], ident[:])
                            mm.then_inc(self.sem("tr"), 1)
                        if t >= 3:
                            s, i, b, br = self.units[t - 3]
                            m = NT * s + i
                            n = self.u0 + it * self.U + t - 3
                            wait_apart(pe, (self.sem("pt"), n + 3), *([self.macros_ago(it, m, 2)] if b == 0 else []))
                            D = br["D"]
                            nk = (br["L"] + P - 1) // P
                            for kt in range(nk):
                                w = min(P, br["L"] - kt * P)
                                mm = nc.tensor.matmul(bank[4 + m % 2][:, b * D:(b + 1) * D],
                                                      self.pT[0:w, (t - 3) % 2, kt, :], br["v"](v, kt),
                                                      start=(kt == 0), stop=(kt == nk - 1))
                            mm.then_inc(self.sem("pv"), 1)

            def act(self, act):
                if self.first:
                    act.sem_inc(self.sem("pt"), 2)
                with self.loop(act) as (it, v):
                    for t in range(self.U + 2):
                        if t >= 2:
                            s, i, b, br = self.units[t - 2]
                            n = self.u0 + it * self.U + t - 2
                            act.wait_ge(self.sem("tr"), n + 5)
                            act.wait_ge(self.sem("pv"), n + 1)
                            w = min(P, br["L"])
                            nk = (br["L"] + P - 1) // P
                            nc.scalar.activation(self.pT[0:w, t % 2, 0:nk, :], split(bank[2 + t % 2][0:w, 0:nk * P], nk, P),
                                                 ACT.Copy).then_inc(self.sem("pt"), 1)
                        if t < self.U:
                            s, i, b, br = self.units[t]
                            m = NT * s + i
                            n = self.u0 + it * self.U + t
                            p = self.p[:, t % 4, 0:br["L"]]
                            if b == 0 and m in (0, NT // 2):
                                self.stage(act, it, 0 if m == 0 else 1)
                            act.wait_ge(self.sem("lg"), n + 5)
                            if b == 0:
                                act.wait_ge(*self.macros_ago(it, m, 4))
                            nc.scalar.activation(p, p, ACT.Exp, bias=self.negm[:, t % 4:t % 4 + 1], scale=-1.0,
                                                 accum_out=self.sums[:, m % 4, b:b + 1]).then_inc(self.sem("ex"), 1)

            def dve(self, dve, link):
                if self.first:
                    dve.sem_inc(self.sem("lg"), 4)
                    dve.sem_inc(self.sem("o"), O_FIRST)
                with self.loop(dve, link) as (it, v):
                    for t in range(self.U + 5):
                        if t < self.U:
                            s, i, b, br = self.units[t]
                            n = self.u0 + it * self.U + t
                            L = br["L"]
                            negm = self.negm[:, t % 4:t % 4 + 1]
                            first = i == 0 and b == 0
                            wait_apart(dve, (self.sem("qk"), n + 1), (self.sem("tr"), n + 1),
                                       *([(self.sem("biases"), self.staged(it, s))] if first else []))
                            ins_ = nc.vector.tensor_tensor_reduce(
                                out=self.p[:, t % 4, 0:L], in0=score_bank[t % 4][:, 0:L], in1=br["bias"](self.biases[s]),
                                scale=-1.0, scalar=3e38, op0=ALU.add, op1=ALU.min, accum_out=negm)
                            if br.get("clamp"):
                                link(ins_)
                                ins_ = nc.vector.tensor_scalar(negm, negm, CLAMP, None, ALU.min)
                            ins_.then_inc(self.sem("lg"), 1)
                        if t >= 5:
                            s, i, b, br = self.units[t - 5]
                            if b == self.NB - 1:
                                m = NT * s + i
                                dve.wait_ge(self.sem("coef"), self.m0 + it * M + m + 1)
                                dve.wait_ge(self.sem("pv"), self.u0 + it * self.U + t - 5 + 3)
                                self.finish(self, dve, link, v, s, m, i).then_inc(self.sem("o"), 1)

            def stage(self, act, it, s):
                wait_apart(act, (self.sem("o"), self.m0 + (it - 1) * M + (s + 1) * NT + O_FIRST))
                nc.scalar.activation(self.queries[s], self.q_of(it, s), ACT.Copy).then_inc(self.sem("queries"), 1)
                nc.scalar.activation(self.biases[s][..., ::-1], self.b_of(it, s), ACT.Copy).then_inc(self.sem("biases"), 1)

            def weights_of(self, pool, it, s, i):
                m = NT * s + i
                wait_apart(pool, (self.sem("ex"), self.u0 + it * self.U + (m + 1) * self.NB),
                           self.macros_ago(it, m, 4))
                self.weigh(self, pool, it, s, m, i).then_inc(self.sem("coef"), 1)

            def pool(self, pool):
                with pool.Fori(0, self.trips) as it:
                    for s in range(STAGES):
                        for i in range(NT):
                            self.weights_of(pool, it, s, i)

            def done(self, eng):
                eng.wait_ge(self.sem("o"), self.after[2] + O_FIRST)

        def outproj_pe(pe, tag, mixT, wo):
            turned(pe, tag)
            for half in range(2):
                pe.wait_ge(S(f"{tag}_w{half}"), past(f"{tag}_w{half}") + 16)
                for i in range(NT):
                    n = half * NT + i
                    if n >= 4:
                        pe.wait_ge(S(f"{tag}_add"), past(f"{tag}_add") + n - 3)
                    for k in range(KD):
                        mm = nc.tensor.matmul(bank[4 + n % 4][:, :], mixT[:, k, i * P:(i + 1) * P], wo[half][:, k, :],
                                              start=(k == 0), stop=(k == KD - 1))
                    mm.then_inc(S(f"{tag}_mm"), 1)

        def outproj_dve(dve, tag, next_tag):
            for half in range(2):
                for i in range(NT):
                    n = half * NT + i
                    dve.wait_ge(S(f"{tag}_mm"), past(f"{tag}_mm") + n + 1)
                    xs = xt[:, i, half * 512:(half + 1) * 512]
                    nc.vector.tensor_tensor(xs, xs, bank[4 + n % 4][:, :], ALU.add).then_inc(S(f"{tag}_add"), 1)
                    if half == 1 and i >= 1:
                        norm_row(dve, next_tag, i - 1)
            norm_row(dve, next_tag, NT - 1)

        e0 = O_RING
        T = at(e0, HEADS, TW); e0 += HEADS * TW
        xbcT = at(e0, CT, SEQ + TAPS - 1)
        xtok = at(e0, NT, DI)
        btok = at(e0 + NT * DI, NT, SG * SN)
        state = at(e0 + NT * (DI + SG * SN), DI)
        y_t = at(e0 + NT * (DI + SG * SN) + DI, DI)
        e0 += CT * (SEQ + TAPS - 1)
        O_XBCS = e0
        xbcS = at(e0, CT, SEQ); e0 += CT * SEQ
        z = at(e0, NT, DI); e0 += NT * DI
        O_QROWS = e0
        qrows = at(e0, NT, HEADS * HD); e0 += NT * HEADS * HD
        eqT = at(e0, 4, SEQ); e0 += 4 * SEQ
        kA = at(e0, SEQ); kB = at(e0 + SEQ, SEQ); e0 += 2 * SEQ
        kvd = at(e0, NT, 2 * HD + SH); e0 += NT * (2 * HD + SH)
        selm = split(arena[:, e0:e0 + NT * SEQ // 2].bitcast(BF16), NT, SEQ); e0 += NT * SEQ // 2
        O_SCORE = e0
        score = at(e0, NT - 1, SEQ); e0 += (NT - 1) * SEQ
        iqT = at(e0, 2, SEQ); ikA = at(e0 + 2 * SEQ, SEQ); ikB = at(e0 + 3 * SEQ, SEQ); e0 += 4 * SEQ
        O_EW = e0
        ew = [at(e0, KD, 512), at(e0 + KD * 512, KD, 512)]
        assert e0 + 2 * KD * 512 + SEQ <= RING * EW and O_SCORE + STAGES * 2 * TW <= e0, e0
        seg = at(O_EW, SG, 4, P)
        cbm = at(O_EW + 1024, SG, P)
        xdt = at(O_EW + 1280, DI)
        xw = at(O_EW + 1792, DI)
        y2 = at(O_EW + 2304, DI)
        ssm_gain = at(O_EW + 2816, DI)
        krn = at(O_EW + 3328, NT, P)
        junk = at(O_ROWS + NT * DI, NT, DI)
        kjunk = at(O_EW + 3328, NT, HD)
        tap = [at(O_ROWS + NT * DI, TAPS - 1, SEQ), at(O_QROWS, TAPS - 1, SEQ)]
        yjunk = at(O_EW + 3584, DI)
        e_wo = [hT, at(O_EW + KD * 512, KD, 512)]
        relu = at(O_ROWS, 2, SEQ)
        rows_m = at(O_ROWS, 2, NT, DI)
        mixT = at(O_EW, KD, SEQ)
        table = at(O_QROWS, BIAS_W)
        brow = at(O_QROWS + BIAS_W, BIAS_W)

        relb = sb("relb", [NB + 1, HEADS])
        conv_w = sb("conv_w", [P, TAPS, CT])
        conv_b = sb("conv_b", [P, CT])
        dt_bias = sb("dt_bias", [P, SH]); a_log = sb("a_log", [P, SH]); d_skip = sb("d_skip", [P, SH])
        head_gain = sb("head_gain", [P, 2])
        iw = sb("iw", [P, NT, IH])
        m8 = sb("m8", [P, 8])
        dt = sb("dt", [P, NT, SH]); dt_e = sb("dt_e", [P, NT, SH]); dA = sb("dA", [P, NT, SH])
        acum = sb("acum", [P, NT, SH]); eac = sb("eac", [P, NT, SH])
        alast = sb("alast", [P, SH]); cdecay = sb("cdecay", [P, SH]); to_end = sb("to_end", [P, SH])
        ssq = sb("ssq", [P, NT, HEADS + 1])
        ssg = sb("ssg", [P, 2])

        w_in = ins["even_w_in"][0]
        EV_CHUNKS = [[(C_IQ, EVEN_COLS - C_IQ)], [(C_XBC, 512)], [(C_XBC + 512, 512)],
                     [(C_K, 2 * HD), (C_DT, SH)], [(C_Z, DI)], [(C_Q, HEADS * HD)]]
        J_IQ, J_IK, J_IW, J_XBC, J_KV, J_Z, J_Q, J_END = 0, 2, 3, 4, 12, 14, 18, 22
        CHUNK_JOBS = [J_XBC, J_XBC + 4, J_KV, J_Z, J_Q, J_END]
        SC = [(i, h) for i in range(1, NT) for h in range(IH)]

        def load_chunk(sp, c, chunks, src, bufs, tag, done_jobs):
            nbuf = len(bufs)
            if c >= nbuf:
                sp.wait_ge(S(f"{tag}_mm"), past(f"{tag}_mm") + done_jobs[c - nbuf])
            off = 0
            for c0, n in chunks[c]:
                sp.dma_start(bufs[c % nbuf][:, :, off:off + n],
                             src[:, c0:c0 + n].rearrange("(k p) c -> p k c", p=P)).then_inc(S(f"{tag}_w{c}"), 16)
                off += n

        def even_sp(sp):
            for i in range(NT):
                sp.dma_start(xt[:, i, :], ins["x"][0, i * P:(i + 1) * P, :]).then_inc(S("x_in"), 16)
            sp.dma_start(gain[:], bcast_rows(ins["attn_norm"][0, :], DM)).then_inc(S("gain_in"), 16)
            load_chunk(sp, 0, EV_CHUNKS, w_in, ew, "ep", CHUNK_JOBS)
            sp.wait_ge(S("relb_ones"), 1)
            sp.dma_start(relb[0:NB, :], ins["rel_bias"]).then_inc(S("table_in"), 16)
            sp.dma_start(table[0:NB + 1, :], ins["bucket_table"]).then_inc(S("table_in"), 16)
            load_chunk(sp, 1, EV_CHUNKS, w_in, ew, "ep", CHUNK_JOBS)
            sp.dma_start(conv_b[:], ins["even_conv_b"][0].rearrange("(c p) -> p c", p=P)).then_inc(S("par_in"), 16)
            for k in range(TAPS):
                sp.dma_start(conv_w[:, k, :],
                             ins["even_conv_w"][0, k].rearrange("(c p) -> p c", p=P)).then_inc(S("par_in"), 16)
            for t_, name in ((dt_bias, "even_dt_bias"), (a_log, "even_a_log"), (d_skip, "even_d_skip")):
                sp.dma_start(t_[:], bcast_rows(ins[name][0], SH)).then_inc(S("par_in"), 16)
            for n, name in enumerate(("even_q_norm", "even_k_norm")):
                for half in range(2):
                    sp.dma_start(head_gain[half * HD:(half + 1) * HD, n:n + 1],
                                 ins[name][0].rearrange("(p c) -> p c", c=1)).then_inc(S("par_in"), 16)
            sp.wait_ge(S("brow"), 2)
            sp.dma_start(bias_row_d, brow[0:HEADS, :]).then_inc(S("bias_out"), 16)
            sp.wait_ge(S("bias_out"), 16)
            load_bias(sp, "T_in0")
            for c in range(2, 6):
                load_chunk(sp, c, EV_CHUNKS, w_in, ew, "ep", CHUNK_JOBS)
            sp.wait_ge(S("ep_mm"), J_Q)
            sp.dma_start(ssm_gain, bcast_rows(ins["even_ssm_norm"][0], DI)).then_inc(S("ssm_gain_in"), 16)
            sp.wait_ge(S("ep_mm"), J_END)
            sp.dma_start(e_wo[0], ins["even_w_out"][0, :, 0:512].rearrange("(k p) c -> p k c", p=P)).then_inc(S("eo_w0"), 16)
            sp.dma_start(e_wo[1], ins["even_w_out"][0, :, 512:1024].rearrange("(k p) c -> p k c", p=P)).then_inc(S("eo_w1"), 16)

        def load_bias(sp, done):
            src = bass.AP(bias_row_d.tensor, 0, [[1, P], [BIAS_W, HEADS], [1, TW]])
            sp.dma_start(T, src).then_inc(S(done), 16)

        def even_pe(pe):
            pe.wait_ge(S("consts"), 1)
            turn_pe(pe, "n0", lambda i, k: rows[:, i, k * P:(k + 1) * P], lambda e, i: rows_ready(e, "n0", i + 1))
            turned(pe, "n0")

            def job(n, mms):
                if n >= 4:
                    pe.wait_ge(S("ep_ev"), n - 3)
                for mm_args in mms:
                    for k in range(KD):
                        o, l, r = mm_args(k)
                        mm = nc.tensor.matmul(o, l, r, start=(k == 0), stop=(k == KD - 1))
                mm.then_inc(S("ep_mm"), 1)

            def channels(n, w, c0, hTk=hT):
                b = bank[n % 4]
                job(n, [lambda k: (b[:, :], w[:, k, c0:c0 + P], hT[:, k, :])])

            def tokens(n, w, tiles, cols):
                b = bank[n % 4]
                job(n, [lambda k, i=i, s=s: (b[:, s * cols:(s + 1) * cols], hT[:, k, i * P:(i + 1) * P], w[:, k, 0:cols])
                        for s, i in enumerate(tiles)])

            pe.wait_ge(S("table_in"), 32)
            for half in range(2):
                nc.tensor.matmul(bank[4 + half][0:HEADS, :], relb[:], table[0:NB + 1, half * 512:(half + 1) * 512],
                                 start=True, stop=True).then_inc(S("bias_mm"), 1)
            pe.wait_ge(S("ep_w0"), 16)
            for j in range(2):
                channels(J_IQ + j, ew[0], j * P)
            b = bank[J_IK % 4]
            c0 = IH * ID
            job(J_IK, [lambda k, q=q: (b[q * HD:(q + 1) * HD, :], ew[0][:, k, c0:c0 + ID], hT[:, k, :]) for q in range(2)])
            b2 = bank[J_IW % 4]
            c1 = c0 + ID
            job(J_IW, [lambda k, i=i: (b2[:, i * IH:(i + 1) * IH], hT[:, k, i * P:(i + 1) * P], ew[0][:, k, c1:c1 + IH])
                       for i in range(NT)])
            pe.wait_ge(S("ep_ev"), J_IK + 1)
            pe.wait_ge(S("brow"), 2)
            for u, (i, h) in enumerate(SC):
                if u >= 2:
                    pe.wait_ge(S("ix_relu"), u - 1)
                L = (i + 1) * P
                nc.tensor.matmul(bank[4 + u % 2][:, 0:L], iqT[:, h // 2, i * P:(i + 1) * P], (ikA, ikB)[h % 2][:, 0:L],
                                 start=True, stop=True).then_inc(S("ix_mm"), 1)
            for c in range(2):
                pe.wait_ge(S(f"ep_w{1 + c}"), 16)
                for j in range(4):
                    channels(J_XBC + 4 * c + j, ew[(1 + c) % 2], j * P)
            pe.wait_ge(S("ep_w3"), 32)
            for j in range(2):
                tokens(J_KV + j, ew[1], (2 * j, 2 * j + 1), 2 * HD + SH)
            pe.wait_ge(S("ep_w4"), 16)
            for i in range(NT):
                tokens(J_Z + i, ew[0], (i,), DI)
            pe.wait_ge(S("ep_ev"), J_Q)
            pe.wait_ge(S("dA"), 1)
            for i in range(NT):
                mm = nc.tensor.matmul(bank[3][:, i * SH:(i + 1) * SH], tri[:], dA[:, i, :], start=True, stop=True)
            mm.then_inc(S("acum_mm"), 1)
            pe.wait_ge(S("silu"), CT)

            def ssm_first(i):
                sl = slice(i * P, (i + 1) * P)
                if i >= 1:
                    pe.wait_ge(S("seg"), 2 * i)
                    pe.wait_ge(S("cbm"), i)
                for g in range(SG):
                    for h in range(4):
                        mm = nc.tensor.matmul(bank[6 + g][:, h * P:(h + 1) * P],
                                              dA[:, i, 4 * g + h:4 * g + h + 1].broadcast_to((P, P)), tri[:],
                                              start=True, stop=True)
                    mm.then_inc(S("abc_mm"), 1)
                if i == 0:
                    pe.wait_ge(S("acum"), 1)
                for g in range(SG):
                    mm = nc.tensor.matmul(bank[3][:, g * P:(g + 1) * P], xbcS[:, 4 + g, sl], xbcS[:, 6 + g, sl],
                                          start=True, stop=True)
                mm.then_inc(S("cb_mm"), 1)
                if i >= 1:
                    pe.wait_ge(S("state"), i)
                    for g in range(SG):
                        mm = nc.tensor.matmul(bank[1][:, g * 256:(g + 1) * 256], xbcS[:, 6 + g, sl],
                                              state[:, g * 256:(g + 1) * 256], start=True, stop=True)
                    mm.then_inc(S("yoff_mm"), 1)

            def ssm_second(i):
                if i < NT - 1:
                    pe.wait_ge(S("xw"), i + 1)
                    for g in range(SG):
                        mm = nc.tensor.matmul(bank[2][:, g * 256:(g + 1) * 256], btok[:, i, g * P:(g + 1) * P],
                                              xw[:, g * 256:(g + 1) * 256], start=True, stop=True)
                    mm.then_inc(S("st_mm"), 1)
                for g in range(SG):
                    pe.wait_ge(S("mt"), 2 * i + g + 1)
                    for h in range(4):
                        hh = 4 * g + h
                        mm = nc.tensor.matmul(bank[0][:, hh * SD:(hh + 1) * SD], seg[:, g, h, :],
                                              xdt[:, hh * SD:(hh + 1) * SD], start=True, stop=True)
                mm.then_inc(S("yd_mm"), 1)

            ssm_first(0)
            for i in range(NT):
                if i >= 1:
                    pe.wait_ge(S("tok_out"), 2 * i)
                for j in range(4):
                    mm = nc.tensor.transpose(bank[4][:, j * P:(j + 1) * P], xbcS[:, j, i * P:(i + 1) * P], ident[:])
                mm.then_inc(S("tok_turned"), 1)
                for g in range(SG):
                    mm = nc.tensor.transpose(bank[5][:, g * P:(g + 1) * P], xbcS[:, 4 + g, i * P:(i + 1) * P], ident[:])
                mm.then_inc(S("tok_turned"), 1)
            pe.wait_ge(S("ep_w5"), 16)
            for i in range(NT):
                if i >= 1:
                    ssm_first(i)
                if i == 0:
                    pe.wait_ge(S("tok_out"), 2 * NT)
                if i >= 2:
                    pe.wait_ge(S("sq"), i)
                for k in range(KD):
                    mm = nc.tensor.matmul(bank[4 + i % 2][:, :], hT[:, k, i * P:(i + 1) * P], ew[1][:, k, :],
                                          start=(k == 0), stop=(k == KD - 1))
                mm.then_inc(S("ep_mm"), 1)
                ssm_second(i)

            pe.wait_ge(S("y_gated"), NT)
            pe.wait_ge(S("kn"), 2)
            for i in range(NT):
                mm = nc.tensor.transpose(bank[0][:, i * P:(i + 1) * P], krn[:, i, :], ident[:])
            mm.then_inc(S("qk_turned"), 1)
            for i in range(NT):
                pe.wait_ge(S("qn"), i + 1)
                if i >= 2:
                    pe.wait_ge(S("qk_out"), i + 1)
                for j in range(4):
                    mm = nc.tensor.transpose(bank[1 + i % 2][:, j * P:(j + 1) * P], qrows[:, i, j * P:(j + 1) * P], ident[:])
                mm.then_inc(S("qk_turned"), 1)
            pe.wait_ge(S("qk_out"), NT + 2)

            pe.wait_ge(S("T_in0"), 16)
            pe.wait_ge(S("selm"), NT - 1)
            pe.wait_ge(S("y_gated"), NT)
            even_att.pe(pe)
            even_att.done(pe)
            pe.wait_ge(S("ssm_row"), NT)
            turn_pe(pe, "eo", lambda i, k: rows_m[:, k // 4, i, (k % 4) * P:(k % 4 + 1) * P], lambda e, i: None)
            outproj_pe(pe, "eo", mixT, e_wo)

        def even_act(act):
            norm_act(act, "n0", lambda e, i: e.wait_ge(S("x_in"), 16 * NT))
            for i in range(NT):
                turn_evac(act, "n0", hT, i, 0)
            for half in range(2):
                act.wait_ge(S("bias_mm"), half + 1)
                nc.scalar.activation(brow[0:HEADS, half * 512:(half + 1) * 512], bank[4 + half][0:HEADS, :],
                                     ACT.Copy).then_inc(S("brow"), 1)

            def ev(n, dst, src, scale=1.0):
                act.wait_ge(S("ep_mm"), n + 1)
                return nc.scalar.activation(dst, src, ACT.Copy)
            for j in range(2):
                ev(J_IQ + j, iqT[:, j, :], bank[J_IQ + j][:, :]).then_inc(S("ep_ev"), 1)
            act.wait_ge(S("pads"), 2)
            ev(J_IK, ikA[0:HD, :], bank[J_IK][0:HD, :])
            nc.scalar.activation(ikB[HD:P, :], bank[J_IK][HD:P, :], ACT.Copy).then_inc(S("ep_ev"), 1)
            ev(J_IW, iw[:], split(bank[J_IW][:, 0:NT * IH], NT, IH)).then_inc(S("ep_ev"), 1)
            turned(act, "n0")
            for u, (i, h) in enumerate(SC):
                L = (i + 1) * P
                act.wait_ge(S("ix_mm"), u + 1)
                if u >= 2:
                    act.wait_ge(S("ix_acc"), u - 1)
                nc.scalar.activation(relu[:, u % 2, 0:L], bank[4 + u % 2][:, 0:L], ACT.Relu,
                                     scale=float(ID * IH) ** -0.5).then_inc(S("ix_relu"), 1)
            act.wait_ge(S("pads"), 3)
            for c in range(CT):
                n = J_XBC + c
                ev(n, xbcT[:, c, TAPS - 1:], bank[n % 4][:, :]).then_inc(S("ep_ev"), 1)
                if c == 0:
                    act.wait_ge(S("par_in"), 16 * 12)
                    act.wait_ge(S("bias_out"), 16)
                if c >= 2:
                    act.wait_ge(S("conv"), c - 1)
                act.wait_ge(S("ep_ev"), n + 1)
                for k in range(TAPS):
                    nc.scalar.activation(tap[c % 2][:, k - 1, :] if k else xbcS[:, c, :], xbcT[:, c, k:k + SEQ], ACT.Copy,
                                         scale=conv_w[:, k, c:c + 1]).then_inc(S("taps"), 1)
            for j in range(2):
                n = J_KV + j
                w = 2 * HD + SH
                ev(n, kvd[:, 2 * j:2 * j + 2, :], split(bank[n % 4][:, 0:2 * w], 2, w)).then_inc(S("ep_ev"), 1)
            def softplus():
                act.wait_ge(S("dt_abs"), 1)
                nc.scalar.activation(dt_e[:], dt_e[:], ACT.Exp, scale=-1.0).then_inc(S("dt_exp"), 1)
                nc.scalar.activation(a_log[:], a_log[:], ACT.Exp).then_inc(S("a_exp"), 1)
                act.wait_ge(S("dt_exp"), 1)
                nc.scalar.activation(dt_e[:], dt_e[:], ACT.Ln, bias=1.0).then_inc(S("dt_ln"), 1)

            for i in range(NT):
                n = J_Z + i
                ev(n, z[:, i, :], bank[n % 4][:, :]).then_inc(S("ep_ev"), 1)
                for c in range(2 * i, 2 * i + 2):
                    act.wait_ge(S("conv"), c + 1)
                    nc.scalar.activation(xbcS[:, c, :], xbcS[:, c, :], ACT.Silu, bias=conv_b[:, c:c + 1]).then_inc(S("silu"), 1)
                act.wait_ge(S("ep_ev"), n + 1)
                nc.scalar.activation(z[:, i, :], z[:, i, :], ACT.Silu).then_inc(S("z_silu"), 1)
                if i == 1:
                    softplus()
            for i in range(NT):
                act.wait_ge(S("tok_turned"), 2 * i + 1)
                nc.scalar.activation(xtok[:, i, :], bank[4][:, :], ACT.Copy).then_inc(S("tok_out"), 1)
                act.wait_ge(S("tok_turned"), 2 * i + 2)
                nc.scalar.activation(btok[:, i, :], bank[5][:, 0:SG * SN], ACT.Copy).then_inc(S("tok_out"), 1)
            act.wait_ge(S("ep_ev"), J_Q)
            nc.scalar.activation(kjunk, kvd[:, :, 0:HD], ACT.Square).then_inc(S("sq"), 1)
            act.wait_ge(S("acum"), 1)
            nc.scalar.activation(eac[:], acum[:], ACT.Exp).then_inc(S("eac"), 1)
            for i in range(NT):
                act.wait_ge(S("alast"), i + 1)
                nc.scalar.activation(to_end[:], to_end[:], ACT.Exp).then_inc(S("ends"), 1)
                nc.scalar.activation(cdecay[:], alast[:], ACT.Exp).then_inc(S("ends"), 1)
                for g in range(SG):
                    act.wait_ge(S("seg"), 2 * i + g + 1)
                    nc.scalar.activation(seg[:, g], seg[:, g], ACT.Exp).then_inc(S("decay"), 1)
                act.wait_ge(S("ep_mm"), J_Q + i + 1)
                nc.scalar.activation(qrows[:, i, :], bank[4 + i % 2][:, :], ACT.Copy).then_inc(S("ep_ev"), 1)
                nc.scalar.activation(junk[:, i, :], bank[4 + i % 2][:, :], ACT.Square).then_inc(S("sq"), 1)
                act.wait_ge(S("y_gated"), i + 1)
                for g in range(SG):
                    nc.scalar.activation(yjunk[:, g * 256:(g + 1) * 256], y_t[:, g * 256:(g + 1) * 256], ACT.Square,
                                         accum_out=ssg[:, g:g + 1]).then_inc(S("y_sq"), 1)
            act.wait_ge(S("qk_turned"), 1)
            act.wait_ge(S("pads"), 5)
            act.wait_ge(S("hgain"), 1)
            nc.scalar.activation(kA[0:HD, :], bank[0][0:HD, :], ACT.Copy, scale=head_gain[0:HD, 1:2]).then_inc(S("qk_out"), 1)
            nc.scalar.activation(kB[HD:P, :], bank[0][HD:P, :], ACT.Copy, scale=head_gain[HD:P, 1:2]).then_inc(S("qk_out"), 1)
            for i in range(NT):
                act.wait_ge(S("qk_turned"), i + 2)
                nc.scalar.activation(eqT[:, :, i * P:(i + 1) * P], split(bank[1 + i % 2][:, :], 4, P), ACT.Copy,
                                     scale=head_gain[:, 0:1]).then_inc(S("qk_out"), 1)
            act.wait_ge(S("qk_out"), NT + 2)
            act.wait_ge(S("T_in0"), 16)
            act.wait_ge(S("selm"), NT - 1)
            act.wait_ge(S("ix_mm"), len(SC))
            act.wait_ge(S("yd_mm"), NT)
            even_att.act(act)
            for i in range(NT):
                turn_evac(act, "eo", mixT, i, 0)

        def even_pool(pool):
            steps = 0

            def c(ins_):
                nonlocal steps
                steps += 1
                ins_.then_inc(S("pool_const"), 1)
            g_ = nc.gpsimd
            c(g_.memset(ident[:], 0.0)); c(g_.memset(ones[:], 1.0)); c(g_.memset(onesb[:], 1.0)); c(g_.memset(tri[:], 1.0))
            c(g_.memset(tri_strict[:], 1.0)); c(g_.memset(score_base[:], 0.0)); c(g_.memset(nhalf[:], -0.5))
            c(g_.memset(minus1[:], -1.0))
            c(g_.iota(iota32[:], [[1, NE]], base=0, channel_multiplier=0, allow_small_or_imprecise_dtypes=True))
            c(g_.iota(row_off[:], [[CAP, NE]], base=0, channel_multiplier=0, allow_small_or_imprecise_dtypes=True))
            c(g_.iota(more_at[:], [[CAP, MORE]], base=CAP, channel_multiplier=0, allow_small_or_imprecise_dtypes=True))
            c(g_.iota(first_rows[:], [[1, CAP]], base=0, channel_multiplier=0, allow_small_or_imprecise_dtypes=True))
            pool.wait_ge(S("pool_const"), steps)
            c(g_.affine_select(out=ident[:], in_=ident[:], compare_op=ALU.not_equal, fill=1.0, base=0,
                               pattern=[[-1, P]], channel_multiplier=1))
            c(g_.affine_select(out=tri[:], in_=tri[:], compare_op=ALU.is_ge, fill=0.0, base=0,
                               pattern=[[1, P]], channel_multiplier=-1))
            c(g_.affine_select(out=tri_strict[:], in_=tri_strict[:], compare_op=ALU.is_gt, fill=0.0, base=0,
                               pattern=[[1, P]], channel_multiplier=-1))
            c(g_.affine_select(out=score_base[:, SEQ - P:], in_=score_base[:, SEQ - P:], compare_op=ALU.is_ge, fill=NEG,
                               base=0, pattern=[[-1, P]], channel_multiplier=1))
            c(g_.memset(relb[:], 1.0))
            pool.wait_ge(S("pool_const"), steps)
            g_.tensor_copy(identb[:], ident[:]).then_inc(S("consts"), 1)
            g_.sem_inc(S("relb_ones"), 1)
            g_.memset(ikA, 0.0).then_inc(S("pads"), 1)
            g_.memset(ikB, 0.0).then_inc(S("pads"), 1)
            g_.memset(xbcT[:, :, 0:TAPS - 1], 0.0).then_inc(S("pads"), 1)
            g_.memset(kA, 0.0).then_inc(S("pads"), 1)
            g_.memset(kB, 0.0).then_inc(S("pads"), 1)
            norm_pool(pool, "n0")
            pool.wait_ge(S("par_in"), 16 * 12)
            g_.tensor_scalar(head_gain[:, 0:1], head_gain[:, 0:1], HD ** -0.5, None, ALU.mult).then_inc(S("hgain"), 1)
            sums = 0
            for c in range(CT):
                pool.wait_ge(S("taps"), TAPS * (c + 1))
                for k in range(1, TAPS):
                    ins_ = g_.tensor_tensor(xbcS[:, c, :], xbcS[:, c, :], tap[c % 2][:, k - 1, :], ALU.add)
                    if k < TAPS - 1:
                        sums += 1
                        ins_.then_inc(S("tap_sum"), 1)
                        pool.wait_ge(S("tap_sum"), sums)
                ins_.then_inc(S("conv"), 1)

            def head_norm(n, sums):
                pool.wait_ge(S("ssq"), n + 1)
                g_.tensor_scalar(sums, sums, 1.0 / HD, EPS, ALU.mult, ALU.add).then_inc(S("ssq_ms"), 1)
                pool.wait_ge(S("ssq_ms"), n + 1)
                half = split(nhalf[:, 0:sums.shape[1] * sums.shape[2]], sums.shape[1], sums.shape[2])
                g_.tensor_tensor(sums, sums, half, ALU.pow).then_inc(S("ssq_rstd"), 1)

            for i in range(NT):
                pool.wait_ge(S("y_sq"), 2 * i + 2)
                g_.tensor_scalar(ssg[:], ssg[:], 1.0 / (DI // SG), EPS, ALU.mult, ALU.add).then_inc(S("y_ms"), 1)
                pool.wait_ge(S("y_ms"), i + 1)
                g_.tensor_tensor(ssg[:], ssg[:], nhalf[:, 0:2], ALU.pow).then_inc(S("y_rstd"), 1)
                head_norm(i, ssq[:, i - 1:i, 0:HEADS] if i else ssq[:, :, HEADS:])
            head_norm(NT, ssq[:, NT - 1:NT, 0:HEADS])

            even_att.pool(pool)

        def heads_bc(ap, w):
            return ap.unsqueeze(2).broadcast_to((P, ap.shape[1], w))

        def even_dve(dve, link):
            v_ = nc.vector
            for i in range(NT):
                norm_row(dve, "n0", i)
            norm_turns(dve, "n0")
            dve.wait_ge(S("ep_ev"), J_IW + 1)
            for u, (i, h) in enumerate(SC):
                L = (i + 1) * P
                dve.wait_ge(S("ix_relu"), u + 1)
                sc = score[:, i - 1, 0:L]
                v_.scalar_tensor_tensor(sc, relu[:, u % 2, 0:L], iw[:, i, h:h + 1],
                                        score_base[:, SEQ - L:] if h == 0 else sc, ALU.mult, ALU.add).then_inc(S("ix_acc"), 1)
                dve.wait_ge(S("ix_acc"), u + 1)
            def take(sc, n):
                with dve.Fori(0, n // 16) as r:
                    link.enter(r, 4)
                    for _ in range(2):
                        link(v_.max(m8[:], sc))
                        link(v_.match_replace(sc, m8[:], sc, TAKEN))
                    link.leave(n // 16)

            def raw_dt():
                dve.wait_ge(S("ep_ev"), J_Z)
                dve.wait_ge(S("par_in"), 16 * 12)
                link(v_.tensor_tensor(dt[:], kvd[:, :, 2 * HD:], dt_bias[:].unsqueeze(1).broadcast_to((P, NT, SH)), ALU.add))
                link(v_.tensor_scalar(dt_e[:], dt[:], -1.0, None, ALU.mult))
                v_.tensor_tensor(dt_e[:], dt_e[:], dt[:], ALU.max).then_inc(S("dt_abs"), 1)

            for i in range(1, NT):
                L = (i + 1) * P
                sc = score[:, i - 1, 0:L]
                take(sc, TOPK // 2)
                if i == NT - 1:
                    raw_dt()
                take(sc, TOPK - TOPK // 2)
                v_.tensor_scalar(selm[:, i, 0:L], sc, TAKEN / 2, NEG, ALU.is_gt, ALU.mult).then_inc(S("selm"), 1)
            def key_sums():
                dve.wait_ge(S("sq"), 1)
                v_.tensor_reduce(ssq[:, :, HEADS:HEADS + 1], kjunk, AX.X, ALU.add).then_inc(S("ssq"), 1)

            def query_sums(i):
                dve.wait_ge(S("sq"), i + 2)
                v_.tensor_reduce(ssq[:, i, 0:HEADS], split(junk[:, i, :], HEADS, HD), AX.X, ALU.add).then_inc(S("ssq"), 1)
            dve.wait_ge(S("dt_ln"), 1)
            link(v_.scalar_tensor_tensor(dt[:], dt[:], 0.0, dt_e[:], ALU.max, ALU.add))
            dve.wait_ge(S("a_exp"), 1)
            v_.scalar_tensor_tensor(dA[:], dt[:], -1.0, a_log[:].unsqueeze(1).broadcast_to((P, NT, SH)),
                                    ALU.mult, ALU.mult).then_inc(S("dA"), 1)
            dve.wait_ge(S("acum_mm"), 1)
            v_.tensor_copy(acum[:], split(bank[3][:, 0:NT * SH], NT, SH)).then_inc(S("acum"), 1)
            dve.wait_ge(S("acum"), 1)
            dve.wait_ge(S("ssm_gain_in"), 16)
            dve.wait_ge(S("ep_mm"), J_Q)
            for i in range(NT):
                for g in range(SG):
                    dve.wait_ge(S("abc_mm"), 2 * i + g + 1)
                    link(v_.tensor_copy(alast[:, 4 * g:4 * g + 4], split(bank[6 + g][:, :], 4, P)[:, :, P - 1]))
                v_.tensor_tensor(to_end[:], alast[:], acum[:, i, :], ALU.subtract).then_inc(S("alast"), 1)
                if i >= 1:
                    dve.wait_ge(S("yd_mm"), i)
                for g in range(SG):
                    for h in range(4):
                        hh = 4 * g + h
                        ins_ = v_.tensor_scalar(seg[:, g, h, :], bank[6 + g][:, h * P:(h + 1) * P],
                                                acum[:, i, hh:hh + 1], 0.0, ALU.subtract, ALU.min)
                    ins_.then_inc(S("seg"), 1)
                dve.wait_ge(S("cb_mm"), i + 1)
                v_.tensor_tensor(cbm, split(bank[3][:, 0:SG * P], SG, P), tri[:].unsqueeze(1).broadcast_to((P, SG, P)),
                                 ALU.mult).then_inc(S("cbm"), 1)
                dve.wait_ge(S("tok_out"), 2 * i + 1)
                link(v_.tensor_tensor(split(xdt, SH, SD), split(xtok[:, i, :], SH, SD), heads_bc(dt[:, i, :], SD), ALU.mult))
                dve.wait_ge(S("ends"), 2 * i + 2)
                if i < NT - 1:
                    if i >= 1:
                        dve.wait_ge(S("st_mm"), i)
                    v_.tensor_tensor(split(xw, SH, SD), split(xdt, SH, SD), heads_bc(to_end[:], SD), ALU.mult).then_inc(S("xw"), 1)
                for g in range(SG):
                    dve.wait_ge(S("decay"), 2 * i + g + 1)
                    dve.wait_ge(S("cbm"), i + 1)
                    v_.tensor_tensor(seg[:, g], seg[:, g], cbm[:, g:g + 1, :].broadcast_to((P, 4, P)), ALU.mult).then_inc(S("mt"), 1)
                link(v_.tensor_tensor(split(y2, SH, SD), split(xtok[:, i, :], SH, SD), heads_bc(d_skip[:], SD), ALU.mult))
                if i >= 1:
                    dve.wait_ge(S("eac"), 1)
                    dve.wait_ge(S("yoff_mm"), i)
                    dve.wait_ge(S("ssm_row"), i)
                    link(v_.tensor_tensor(split(y_t, SH, SD), split(bank[1][:, :], SH, SD), heads_bc(eac[:, i, :], SD), ALU.mult))
                    link(v_.tensor_tensor(y2, y2, y_t, ALU.add))
                if i < NT - 1:
                    dve.wait_ge(S("st_mm"), i + 1)
                    if i == 0:
                        v_.tensor_copy(state, bank[2][:, :]).then_inc(S("state"), 1)
                    else:
                        link(v_.tensor_tensor(split(state, SH, SD), split(state, SH, SD), heads_bc(cdecay[:], SD), ALU.mult))
                        v_.tensor_tensor(state, state, bank[2][:, :], ALU.add).then_inc(S("state"), 1)
                if i == 0:
                    key_sums()
                else:
                    query_sums(i - 1)
                dve.wait_ge(S("z_silu"), i + 1)
                dve.wait_ge(S("eac"), 1)
                dve.wait_ge(S("yd_mm"), i + 1)
                link(v_.tensor_tensor(y2, y2, bank[0][:, :], ALU.add))
                v_.tensor_tensor(y_t, y2, z[:, i, :], ALU.mult).then_inc(S("y_gated"), 1)
                dve.wait_ge(S("y_rstd"), i + 1)
                for g in range(SG):
                    cs = slice(g * 256, (g + 1) * 256)
                    ins_ = v_.scalar_tensor_tensor(rows_m[:, 0, i, cs], y_t[:, cs], ssg[:, g:g + 1], ssm_gain[:, cs],
                                                   ALU.mult, ALU.mult)
                ins_.then_inc(S("ssm_row"), 1)
            query_sums(NT - 1)
            dve.wait_ge(S("ssq_rstd"), 1)
            for q in range(2):
                v_.tensor_tensor(krn[:, :, q * HD:(q + 1) * HD], kvd[:, :, 0:HD],
                                 ssq[:, :, HEADS:HEADS + 1].broadcast_to((P, NT, HD)), ALU.mult).then_inc(S("kn"), 1)
            for i in range(NT):
                dve.wait_ge(S("ssq_rstd"), i + 2)
                q_ = split(qrows[:, i, :], HEADS, HD)
                v_.tensor_tensor(q_, q_, heads_bc(ssq[:, i, 0:HEADS], HD), ALU.mult).then_inc(S("qn"), 1)
            dve.wait_ge(S("T_in0"), 16)
            even_att.dve(dve, link)
            for i in range(NT):
                turn_evac(dve, "eo", mixT, i, 1)
            outproj_dve(dve, "eo", "m0n")

        @contextmanager
        def loop_pairs(eng, link=None):
            with eng.Fori(0, HEADS // 4) as it:
                if link:
                    link.enter(it, 0)
                yield it, it
                if link:
                    link.leave(HEADS // 4)

        def flat(ap):
            return ap.rearrange("p a b -> p (a b)")

        def even_weigh(a, pool, it, s, m, i):
            return nc.gpsimd.tensor_tensor(a.coef[:, m % 4, :], a.sums[:, m % 4, :], minus1[:, 0:2], ALU.pow)

        def even_finish(a, dve, link, it, s, m, i):
            o = rows_m[:, 1, i, :].rearrange("p (j q d) -> p j q d", q=2, d=HD)[:, bass.ds(2 * it + s, 1), :, :]
            return nc.vector.tensor_tensor(o, split(bank[4 + m % 2][:, 0:2 * HD], 1, 2, HD),
                                           a.coef[:, m % 4, :].unsqueeze(1).unsqueeze(3).broadcast_to((P, 1, 2, HD)), ALU.mult)

        def tile_bias(i):
            return slice(SEQ - P - i * P, SEQ - P - i * P + (i + 1) * P)

        even_branches = [[dict(L=(i + 1) * P, D=HD, bias=lambda b, i=i, q=q: b[:, q, tile_bias(i)],
                               k=lambda it, i=i, q=q: (kA, kB)[q][:, 0:(i + 1) * P],
                               mask=selm[:, i, 0:(i + 1) * P] if i else None,
                               v=lambda it, kt: kvd[:, kt, HD:2 * HD]) for q in range(2)] for i in range(NT)]
        even_att = Attention("ea", even_branches, loop_pairs, HEADS // 4,
                             [at(RING * EW - SEQ, SEQ), at(O_XBCS, SEQ)],
                             [at(O_SCORE + n * 2 * TW, 2, TW) for n in range(STAGES)],
                             lambda it, s: flat(eqT[:, bass.ds(2 * it + s, 1), :]),
                             lambda it, s: split(arena[:, 0:HEADS * TW], HEADS // 2, 2, TW)[:, bass.ds(2 * it + s, 1), :, :],
                             O_EW, even_weigh, even_finish)

        o0 = HEADS * TW
        oqT = at(o0, HEADS, SEQ); o0 += HEADS * SEQ
        O_KROWS = o0
        krows = at(o0, 2, NT, OKV); o0 += 2 * NT * OKV
        ojunk = at(o0, OKV)
        kT = at(o0, 2, OG, SEQ); o0 += 2 * OG * SEQ
        vv = at(o0, 2, NT, OKV); o0 += 2 * NT * OKV
        O_CT = o0
        qjunk = at(O_CT, 512)
        cT = at(o0, 2, OG, SEQ); o0 += 2 * OG * SEQ
        blk = [at(o0 + q * OG * CB * NC, CB, OG * NC) for q in range(2)]
        o_work = o0
        o0 += 2 * OG * CB * NC
        O_OW = 2 * EW
        cw2 = at(o0, 2, OD); o0 += 2 * OD
        kcT = at(o0, OG, NC); o0 += OG * NC
        kc_rows, kc_sq, vc = (split(arena[0:NC, o0 + n * OG * OD:o0 + (n + 1) * OG * OD], OG, OD) for n in range(3))
        o0 += 3 * OG * OD
        assert o0 <= O_OW and 6 * SEQ <= 2 * OG * CB * NC and STAGES * TW <= 2 * NT * OKV and STAGES * SEQ <= 2 * OG * SEQ
        ow = [at(O_OW + n * KD * 512, KD, 512) for n in range(3)]
        cw1 = [at(0, CB, OD), at(HEADS * TW, CB, OD)]
        o_wo = [hT, ow[0]]
        o_mixT = at(O_OW + KD * 512, KD, SEQ)
        gl = sb("gl", [P, NT, 3, HEADS])
        gates = sb("gates", [P, NT, HEADS, 3])
        oss = sb("oss", [P, NT, HEADS + 4])
        qk_gain = sb("qk_gain", [P, 4])
        posT = sb("posT", [P, 2, CB])
        hidT_c = sb("hidT_c", [P, 2, OG * NC])
        kc_ss = sb("kc_ss", [NC, OG])

        w_odd = ins["odd_w_in"][0]
        OD_CHUNKS = [[(C_OK, 512)], [(C_OK + 512, 256), (C_OK + 1024, 256)], [(C_OK + 768, 256), (C_OK + 1280, 256)],
                     [(C_GL, 3 * HEADS)], [(0, 512)], [(512, 512)]]
        K_C, K_K, K_V, K_G, K_Q, K_END = 0, 4, 8, 12, 13, 21
        OD_JOBS = [K_K, K_V, K_G, K_Q, K_Q + 4, K_END]

        def odd_sp(sp):
            sp.wait_ge(S("m_x"), 2 * NT)
            for n, name in enumerate(("odd_cmp_k_w1", "odd_cmp_v_w1")):
                sp.dma_start(cw1[n], ins[name][0].rearrange("(r d) h -> d r h", d=OD)).then_inc(S(f"cw1_in{n}"), 16)
            for n, name in enumerate(("odd_q_norm", "odd_ks_norm", "odd_kw_norm", "odd_kc_norm")):
                sp.dma_start(qk_gain[:, n:n + 1], ins[name][0].rearrange("(p c) -> p c", c=1)).then_inc(S("opar_in"), 16)
            for n, name in enumerate(("odd_cmp_pos_k", "odd_cmp_pos_v")):
                sp.dma_start(posT[:, n, :], ins[name][0].rearrange("r d -> d r")).then_inc(S("opar_in"), 16)
            for n, name in enumerate(("odd_cmp_k_w2", "odd_cmp_v_w2")):
                sp.dma_start(cw2[:, n, :], ins[name][0]).then_inc(S("opar_in"), 16)
            for c in range(3, 6):
                load_chunk(sp, c, OD_CHUNKS, w_odd, ow, "op", OD_JOBS)
            sp.wait_ge(S("c_hid"), past("c_hid") + 1)
            load_bias(sp, "T_in1")
            sp.wait_ge(S("op_mm"), past("op_mm") + K_Q)
            sp.dma_start(o_wo[1], ins["odd_w_out"][0, :, 512:1024].rearrange("(k p) c -> p k c", p=P)).then_inc(S("oo_w1"), 16)
            sp.wait_ge(S("op_mm"), past("op_mm") + K_END)
            sp.dma_start(o_wo[0], ins["odd_w_out"][0, :, 0:512].rearrange("(k p) c -> p k c", p=P)).then_inc(S("oo_w0"), 16)

        def odd_early(sp):
            sp.wait_ge(S("m_dn"), RING * TRIPS + 1)
            sp.dma_start(gain[:], bcast_rows(ins["attn_norm"][1, :], DM)).then_inc(S("gain_in"), 16)
            for c in range(3):
                load_chunk(sp, c, OD_CHUNKS, w_odd, ow, "op", OD_JOBS)

        def odd_pe(pe):
            turn_pe(pe, "n2", lambda i, k: rows[:, i, k * P:(k + 1) * P], lambda e, i: rows_ready(e, "n2", i + 1))
            turned(pe, "n2")

            def job(n, runs):
                if n >= 4:
                    pe.wait_ge(S("op_ev"), past("op_ev") + n - 3)
                for o, lhs, rhs in runs:
                    for k in range(KD):
                        mm = nc.tensor.matmul(o, lhs(k), rhs(k), start=(k == 0), stop=(k == KD - 1))
                mm.then_inc(S("op_mm"), 1)

            def tokens(n, w, i, cols):
                job(n, [(bank[n % 4][:, 0:cols], lambda k: hT[:, k, i * P:(i + 1) * P], lambda k: w[:, k, 0:cols])])

            pe.wait_ge(S("op_w0"), past("op_w0") + 16)
            for j in range(4):
                job(K_C + j, [(bank[j][:, :], lambda k: ow[0][:, k, j * P:(j + 1) * P], lambda k: hT[:, k, :])])
            for c, first in ((1, K_K), (2, K_V)):
                pe.wait_ge(S(f"op_w{c}"), past(f"op_w{c}") + 32)
                for i in range(NT):
                    tokens(first + i, ow[c], i, 512)
            for q in range(2):
                pe.wait_ge(S(f"cw1_in{q}"), past(f"cw1_in{q}") + 16)
                pe.wait_ge(S("blk"), past("blk") + 2 * q + 2)
                for r in range(CB):
                    mm = nc.tensor.matmul(bank[6 + q][:, 0:OG * NC], cw1[q][:, r, :], blk[q][:, r, :],
                                          start=(r == 0), stop=(r == CB - 1))
                mm.then_inc(S("c_hid"), 1)
            pe.wait_ge(S("op_w3"), past("op_w3") + 16)
            job(K_G, [(bank[K_G % 4][:, i * 3 * HEADS:(i + 1) * 3 * HEADS], lambda k, i=i: hT[:, k, i * P:(i + 1) * P],
                       lambda k: ow[0][:, k, 0:3 * HEADS]) for i in range(NT)])
            pe.wait_ge(S("op_w4"), past("op_w4") + 16)
            for i in range(NT):
                tokens(K_Q + i, ow[1], i, 512)
            for i in range(NT):
                pe.wait_ge(S("ok_n"), past("ok_n") + 2 * i + 2)
                for q in range(2):
                    n = 2 * i + q
                    if n >= 2:
                        pe.wait_ge(S("ok_out"), past("ok_out") + n - 1)
                    for g in range(OG):
                        mm = nc.tensor.transpose(bank[4 + q][:, g * P:(g + 1) * P], krows[:, q, i, g * OD:(g + 1) * OD], ident[:])
                    mm.then_inc(S("ok_turned"), 1)
            pe.wait_ge(S("ok_out"), past("ok_out") + 2 * NT)
            for q in range(2):
                pe.wait_ge(S("hid_c"), past("hid_c") + q + 1)
                for g in range(OG):
                    mm = nc.tensor.matmul(bank[4 + q][0:NC, g * P:(g + 1) * P], hidT_c[:, q, g * NC:(g + 1) * NC],
                                          cw2[:, q, :], start=True, stop=True)
                mm.then_inc(S("c_rows"), 1)
            pe.wait_ge(S("op_w5"), past("op_w5") + 16)
            for i in range(NT):
                tokens(K_Q + 4 + i, ow[2], i, 512)
            pe.wait_ge(S("op_ev"), past("op_ev") + K_END)
            pe.wait_ge(S("kc_n"), past("kc_n") + 1)
            for g in range(OG):
                mm = nc.tensor.transpose(bank[7][:, g * NC:(g + 1) * NC], kc_rows[:, g, :], ident[0:NC, 0:NC])
            mm.then_inc(S("kc_turned"), 1)
            for half in range(2):
                for i in range(NT):
                    n = NT * half + i
                    pe.wait_ge(S("oq_n"), past("oq_n") + n + 1)
                    if n >= 2:
                        pe.wait_ge(S("oq_out"), past("oq_out") + n - 1)
                    for j in range(4):
                        c = (4 * half + j) * P
                        mm = nc.tensor.transpose(bank[2 + n % 2][:, j * P:(j + 1) * P], rows[:, i, c:c + P], ident[:])
                    mm.then_inc(S("oq_turned"), 1)
            pe.wait_ge(S("kcT"), past("kcT") + 1)
            pe.wait_ge(S("oq_out"), past("oq_out") + 2 * NT)
            odd_att.pe(pe)
            odd_att.done(pe)
            turn_pe(pe, "oo", lambda i, k: rows[:, i, k * P:(k + 1) * P], lambda e, i: None)
            outproj_pe(pe, "oo", o_mixT, o_wo)

        def odd_act(act):
            norm_act(act, "n2", lambda e, i: e.wait_ge(S("m_x"), 2 * i + 2))
            for i in range(NT):
                turn_evac(act, "n2", hT, i, 0)

            def ev(n, dst, src):
                act.wait_ge(S("op_mm"), past("op_mm") + n + 1)
                nc.scalar.activation(dst, src, ACT.Copy).then_inc(S("op_ev"), 1)
            for j in range(4):
                ev(K_C + j, cT[:, j // 2, j % 2, :], bank[j][:, :])
            for dst, first in ((krows, K_K), (vv, K_V)):
                for i in range(NT):
                    ev(first + i, dst[:, :, i, :], split(bank[(first + i) % 4][:, :], 2, OKV))
            for q in range(2):
                act.wait_ge(S("c_hid"), past("c_hid") + q + 1)
                nc.scalar.activation(hidT_c[:, q, :], bank[6 + q][:, 0:OG * NC], ACT.Silu).then_inc(S("hid_c"), 1)
            ev(K_G, gl[:], bank[K_G % 4][:, 0:NT * 3 * HEADS].rearrange("p (i b h) -> p i b h", i=NT, b=3))
            act.wait_ge(S("op_ev"), past("op_ev") + K_G + 1)
            nc.scalar.activation(gl[:], gl[:], ACT.Exp, scale=-1.0).then_inc(S("gl_exp"), 1)
            turned(act, "n2")

            def ev_queries(half):
                for i in range(NT):
                    n = K_Q + 4 * half + i
                    ev(n, rows[:, i, half * 512:(half + 1) * 512], bank[n % 4][:, :])
            ev_queries(0)
            act.wait_ge(S("opar_in"), past("opar_in") + 16 * 8)
            for i in range(NT):
                for q in range(2):
                    act.wait_ge(S("ok_turned"), past("ok_turned") + 2 * i + q + 1)
                    nc.scalar.activation(kT[:, q, :, i * P:(i + 1) * P], split(bank[4 + q][:, 0:2 * P], OG, P), ACT.Copy,
                                         scale=qk_gain[:, 1 + q:2 + q]).then_inc(S("ok_out"), 1)
            act.wait_ge(S("c_rows"), past("c_rows") + 1)
            nc.scalar.activation(kc_rows, split(bank[4][0:NC, 0:OG * OD], OG, OD), ACT.Copy).then_inc(S("kc_raw"), 1)
            act.wait_ge(S("c_rows"), past("c_rows") + 2)
            nc.scalar.activation(vc, split(bank[5][0:NC, 0:OG * OD], OG, OD), ACT.Copy).then_inc(S("kc_raw"), 1)
            ev_queries(1)
            act.wait_ge(S("kc_turned"), past("kc_turned") + 1)
            nc.scalar.activation(kcT, split(bank[7][:, 0:OG * NC], OG, NC), ACT.Copy, scale=qk_gain[:, 3:4]).then_inc(S("kcT"), 1)
            act.wait_ge(S("qscale"), past("qscale") + 1)
            for half in range(2):
                for i in range(NT):
                    n = NT * half + i
                    act.wait_ge(S("oq_turned"), past("oq_turned") + n + 1)
                    nc.scalar.activation(oqT[:, 4 * half:4 * half + 4, i * P:(i + 1) * P], split(bank[2 + n % 2][:, :], 4, P),
                                         ACT.Copy, scale=qk_gain[:, 0:1]).then_inc(S("oq_out"), 1)
            act.wait_ge(S("oq_out"), past("oq_out") + 2 * NT)
            act.wait_ge(S("T_in1"), past("T_in1") + 16)
            act.wait_ge(S("ok_turned"), past("ok_turned") + 2 * NT)
            act.wait_ge(S("oss"), past("oss") + 3 * NT)
            odd_att.act(act)
            for i in range(NT):
                turn_evac(act, "oo", o_mixT, i, 0)

        def odd_pool(pool):
            g_ = nc.gpsimd
            norm_pool(pool, "n2")
            pool.wait_ge(S("opar_in"), past("opar_in") + 16 * 8)
            g_.tensor_scalar(qk_gain[:, 0:1], qk_gain[:, 0:1], OD ** -0.5, None, ALU.mult).then_inc(S("qscale"), 1)

            def head_rstd(n, done, cols):
                pool.wait_ge(S("oss"), past("oss") + done)
                o = oss[:, :, cols]
                g_.tensor_scalar(o, o, 1.0 / OD, EPS, ALU.mult, ALU.add).then_inc(S("oss_ms"), 1)
                pool.wait_ge(S("oss_ms"), past("oss_ms") + n)
                g_.tensor_tensor(o, o, split(nhalf[:, 0:4 * NT], NT, 4), ALU.pow).then_inc(S("oss_rstd"), 1)
            head_rstd(1, NT, slice(HEADS, HEADS + 4))
            head_rstd(2, 2 * NT, slice(0, 4))
            pool.wait_ge(S("kc_ss"), past("kc_ss") + 1)
            g_.tensor_scalar(kc_ss[:], kc_ss[:], 1.0 / OD, EPS, ALU.mult, ALU.add).then_inc(S("kc_ms"), 1)
            pool.wait_ge(S("kc_ms"), past("kc_ms") + 1)
            g_.tensor_tensor(kc_ss[:], kc_ss[:], nhalf[0:NC, 0:OG], ALU.pow).then_inc(S("kc_rstd"), 1)
            head_rstd(3, 3 * NT, slice(4, 8))
            pool.wait_ge(S("gates"), 1)
            odd_att.pool(pool)

        def odd_dve(dve, link):
            v_ = nc.vector
            norm_turns(dve, "n2")
            for i in range(NT):
                dve.wait_ge(S("op_ev"), past("op_ev") + K_K + i + 1)
                for q in range(2):
                    k_ = krows[:, q, i, :]
                    link(v_.tensor_tensor(ojunk, k_, k_, ALU.mult))
                    ins_ = v_.tensor_reduce(oss[:, i, HEADS + 2 * q:HEADS + 2 * q + 2], split(ojunk, OG, OD), AX.X, ALU.add)
                    if q == 0:
                        link(ins_)
                    else:
                        ins_.then_inc(S("oss"), 1)
                        dve.wait_ge(S("oss"), past("oss") + i + 1)
            dve.wait_ge(S("opar_in"), past("opar_in") + 16 * 8)
            for q in range(2):
                for g in range(OG):
                    src = cT[:, q, g, :]
                    win = bass.AP(src.tensor, src.offset, [list(src.ap[0]), [1, CB], [CS, NC]])
                    v_.tensor_tensor(blk[q][:, :, g * NC:(g + 1) * NC], win,
                                     posT[:, q, :].unsqueeze(2).broadcast_to((P, CB, NC)), ALU.add).then_inc(S("blk"), 1)
            dve.wait_ge(S("oss_rstd"), past("oss_rstd") + 1)
            for i in range(NT):
                for q in range(2):
                    k_ = split(krows[:, q, i, :], OG, OD)
                    v_.tensor_tensor(k_, k_, heads_bc(oss[:, i, HEADS + 2 * q:HEADS + 2 * q + 2], OD), ALU.mult).then_inc(S("ok_n"), 1)

            def query_squares(half):
                for i in range(NT):
                    dve.wait_ge(S("op_ev"), past("op_ev") + K_Q + 4 * half + i + 1)
                    q_ = rows[:, i, half * 512:(half + 1) * 512]
                    link(v_.tensor_tensor(qjunk, q_, q_, ALU.mult))
                    v_.tensor_reduce(oss[:, i, 4 * half:4 * half + 4], split(qjunk, 4, OD), AX.X, ALU.add).then_inc(S("oss"), 1)
                    dve.wait_ge(S("oss"), past("oss") + NT * (1 + half) + i + 1)

            def scale_queries(half):
                dve.wait_ge(S("oss_rstd"), past("oss_rstd") + 2 + half)
                for i in range(NT):
                    q_ = split(rows[:, i, half * 512:(half + 1) * 512], 4, OD)
                    v_.tensor_tensor(q_, q_, heads_bc(oss[:, i, 4 * half:4 * half + 4], OD), ALU.mult).then_inc(S("oq_n"), 1)
            dve.wait_ge(S("gl_exp"), past("gl_exp") + 1)
            link(v_.tensor_scalar(gl[:], gl[:], 1.0, None, ALU.add))
            v_.reciprocal(gates[:].rearrange("p i h b -> p i b h"), gl[:]).then_inc(S("gates"), 1)
            query_squares(0)
            scale_queries(0)
            dve.wait_ge(S("kc_raw"), past("kc_raw") + 1)
            link(v_.tensor_tensor(kc_sq, kc_rows, kc_rows, ALU.mult))
            v_.tensor_reduce(kc_ss[:].unsqueeze(2), kc_sq, AX.X, ALU.add).then_inc(S("kc_ss"), 1)
            dve.wait_ge(S("kc_rstd"), past("kc_rstd") + 1)
            v_.tensor_tensor(kc_rows, kc_rows, kc_ss[:].unsqueeze(2).broadcast_to((NC, OG, OD)), ALU.mult).then_inc(S("kc_n"), 1)
            query_squares(1)
            scale_queries(1)
            dve.wait_ge(S("T_in1"), past("T_in1") + 16)
            odd_att.dve(dve, link)
            for i in range(NT):
                turn_evac(dve, "oo", o_mixT, i, 1)
            outproj_dve(dve, "oo", "m1n")

        @contextmanager
        def loop_heads(eng, link=None):
            links = 2 * M + STAGES
            per = HPG // STAGES
            with eng.Fori(0, OG) as g:
                with eng.Fori(0, per) as n:
                    it = g * per + n
                    if link:
                        link.enter(it, links)
                    yield it, (g, it)
                    if link:
                        link.leave(1)
                        link.n -= links
            if link:
                link.n += OG * per * links

        def odd_weigh(a, pool, it, s, m, i):
            c_ = a.coef[:, m % 4, :]
            nc.gpsimd.tensor_scalar(c_, a.sums[:, m % 4, :], 1e-30, None, ALU.max).then_inc(S("recip"), 1)
            wait_apart(pool, (S("recip"), 2 * (it * M + m) + 1))
            nc.gpsimd.tensor_tensor(c_, c_, minus1[:], ALU.pow).then_inc(S("recip"), 1)
            wait_apart(pool, (S("recip"), 2 * (it * M + m) + 2))
            return nc.gpsimd.tensor_tensor(c_, c_, flat(gates[:, i, bass.ds(2 * it + s, 1), :]), ALU.mult)

        def odd_finish(a, dve, link, v, s, m, i):
            h = bass.ds(2 * v[1] + s, 1)
            c_ = a.coef[:, m % 4, :]
            y = flat(split(rows[:, i, :], HEADS, OD)[:, h, :])
            b_ = bank[4 + m % 2]
            link(nc.vector.tensor_scalar(y, b_[:, 0:OD], c_[:, 0:1], None, ALU.mult))
            link(nc.vector.scalar_tensor_tensor(y, b_[:, OD:2 * OD], c_[:, 1:2], y, ALU.mult, ALU.add))
            return nc.vector.scalar_tensor_tensor(y, b_[:, 2 * OD:3 * OD], c_[:, 2:3], y, ALU.mult, ALU.add)

        def o_compressed(i):
            u0 = tile_bias(i).start + CB - 1
            return dict(L=NC, D=OD, clamp=i == 0, bias=lambda b: b[:, u0:u0 + CS * (NC - 1) + 1:CS],
                        k=lambda v: flat(kcT[:, bass.ds(v[0], 1), :]),
                        v=lambda v, kt: flat(vc[:, bass.ds(v[0], 1), :]))

        def o_branch(i, q):
            return dict(L=(i + 1) * P, D=OD, bias=lambda b: b[:, tile_bias(i)],
                        k=lambda v: flat(kT[:, q, bass.ds(v[0], 1), 0:(i + 1) * P]),
                        v=lambda v, kt: flat(split(vv[:, q, kt, :], OG, OD)[:, bass.ds(v[0], 1), :]))

        odd_att = Attention("oa", [[o_compressed(i), o_branch(i, 0), o_branch(i, 1)] for i in range(NT)],
                            loop_heads, HEADS // STAGES,
                            [at(O_CT + n * SEQ, SEQ) for n in range(STAGES)],
                            [at(O_KROWS + n * TW, TW) for n in range(STAGES)],
                            lambda it, s: flat(oqT[:, bass.ds(2 * it + s, 1), :]),
                            lambda it, s: flat(T[:, bass.ds(2 * it + s, 1), :]),
                            o_work, odd_weigh, odd_finish, before=even_att)

        router_w = [sb(f"router_w{n}", [P, KD, NR]) for n in range(2)]
        dest = sb("dest", [P, 2, NT], I32)
        weight = sb("weight", [P, 2, NT])
        more_i = sb("more_i", [P, 1 + NX], I32)
        dest_f = sb("dest_f", [P, 2 * NT])
        blk_rows = sb("blk_rows", [P, CAP])
        xe = at(O_HT, 512)
        xeT = at(O_HT + 512, 4, P)
        hidT = at(O_HT + 1024, 2, P)
        act_g = at(O_HT + 1280, FH)
        hid = at(O_HT + 1536, FH)
        yb = at(O_HT + 1792, RING, 512)
        same = at(O_HT + 3328, 2, NT, CAP)
        pick = at(O_HT + 3328 + 2 * NT * CAP, NT, CAP)
        y_rows = at(O_HT, 2, NT, DM)
        wgu = [at(u * EW, 2, KD, FF) for u in range(RING)]
        wd = [at(u * EW + 2 * KD * FF, FF // P, DM) for u in range(RING)]
        r0 = 2 * EW + 2 * KD * FF
        lgt = at(r0, NT, NR); r0 += NT * NR
        cand = at(r0, NT, EPG); r0 += NT * EPG
        eqs = at(r0, NT, EPG); r0 += NT * EPG
        oh_g = at(r0, NT, MG); r0 += NT * MG
        es = at(r0, NT, EPG); r0 += NT * EPG
        oh_e = at(r0, 2, NT, EPG); r0 += 2 * NT * EPG
        prod = at(r0, 2 * NT, NE); r0 += 2 * NT * NE
        oh = at(r0, 2, NT, NE); r0 += 2 * NT * NE
        oh_sum = split(arena[:, r0:r0 + NT * NE // 2].bitcast(BF16), NT, NE); r0 += NT * NE // 2
        before = at(r0, NT, NE); r0 += NT * NE
        load = at(r0, NE); r0 += NE
        xn = at(r0, NE); r0 += NE
        xend = at(r0, NE); r0 += NE
        xrow = at(r0, NE); r0 += NE
        cmp_ = at(r0, NE, MORE); r0 += NE * MORE
        cmpx = at(r0, NX, NE); r0 += NX * NE
        more_f = at(r0, 1 + NX); r0 += 1 + NX
        small = at(r0, 12, NT); r0 += 12 * NT
        pos = at(r0, 2 * NT); r0 += 2 * NT
        base = at(r0, 2 * NT); r0 += 2 * NT
        xbase = at(r0, 2 * NT); r0 += 2 * NT
        over = at(r0, 2 * NT); r0 += 2 * NT
        onesr = at(r0, NE); r0 += NE
        assert r0 <= RING * EW and 3328 + 3 * NT * CAP <= KD * SEQ

        def gate_up_weights(sp, t, layer, e, u):
            for n, name in enumerate(("moe_w_gate", "moe_w_up")):
                src = ins[name][layer, bass.ds(e, 1)].rearrange("e (h p j) f -> p (e h) (j f)", h=2, j=4)
                sp.dma_start(wgu[u][:, n].rearrange("p (h j) f -> p h (j f)", h=2), src).then_inc(S(f"{t}_wgu{u}"), 16)

        def down_weights(sp, t, layer, e, u):
            src = ins["moe_w_down"][layer, bass.ds(e, 1)].rearrange("e (h p j) d -> p (e h) (j d)", h=2, j=2)
            sp.dma_start(wd[u].rearrange("p (h j) d -> p h (j d)", h=2), src).then_inc(S(f"{t}_wd{u}"), 16)

        def weights(sp, t, layer, e, u):
            gate_up_weights(sp, t, layer, e, u)
            down_weights(sp, t, layer, e, u)

        def pick_ones(link):
            link(nc.vector.tensor_tensor(
                same.rearrange("p a b c -> p (a b) c"), dest_f[:].unsqueeze(2).broadcast_to((P, 2 * NT, CAP)),
                blk_rows[:].unsqueeze(1).broadcast_to((P, 2 * NT, CAP)), ALU.is_equal))
            link(nc.vector.tensor_scalar(blk_rows[:], blk_rows[:], float(CAP), None, ALU.add))
            return nc.vector.tensor_tensor(pick, same[:, 0], same[:, 1], ALU.add)

        def pick_rows():
            for i in range(NT):
                for h in range(2):
                    mm = nc.tensor.matmul(bank[4][h * CAP:(h + 1) * CAP, :], pick[:, i, :], rows[:, i, h * 512:(h + 1) * 512],
                                          start=(i == 0), stop=(i == NT - 1))
            return mm

        def copy_picked():
            return nc.scalar.activation(xe, bank[4][:, :], ACT.Copy)

        def turn_rows():
            for j in range(4):
                mm = nc.tensor.transpose(bank[0][:, j * P:(j + 1) * P], xe[:, j::4], ident[:])
            return mm

        def copy_x():
            return nc.scalar.activation(xeT, split(bank[0][:, :], 4, P), ACT.Copy)

        def gate_up_mms(u):
            for n in range(KD):
                half, j = n // 4, n % 4
                for fh in range(2):
                    mm = nc.tensor.matmul(bank[1][fh * CAP:(fh + 1) * CAP, :], xeT[:, j, half * CAP:(half + 1) * CAP],
                                          wgu[u][:, :, n, fh * FH:(fh + 1) * FH], start=(n == 0), stop=(n == KD - 1))
            return mm

        def turn_hidden():
            for j in range(2):
                mm = nc.tensor.transpose(bank[2][:, j * P:(j + 1) * P], hid[:, j::2], ident[:])
            return mm

        def down_mms(u):
            for n in range(FF // P):
                fh, j = n // 2, n % 2
                for dh in range(2):
                    mm = nc.tensor.matmul(bank[3][dh * CAP:(dh + 1) * CAP, :], hidT[:, j, fh * CAP:(fh + 1) * CAP],
                                          wd[u][:, n, dh * 512:(dh + 1) * 512], start=(n == 0), stop=(n == FF // P - 1))
            return mm

        def store_y(act, t, layer, u, blk_n):
            d = y_d[layer].rearrange("(b s) (h c) -> b h s c", s=CAP, h=2)[bass.ds(blk_n, 1)]
            for h in range(2):
                act.dma_start(d[:, h].rearrange("b s c -> (b s) c"), yb[h * CAP:(h + 1) * CAP, u, :]).then_inc(S(f"{t}_yout{u}"), 16)

        (X_ONES, X_PICKED, X_ROWS, X_TURN, X_XT, X_GU, X_G, X_HID, X_HTURN, X_HT, X_DN, X_Y) = range(1, 13)
        X_STEPS = 12

        def x_step(eng, x, j, step):
            eng.wait_ge(S(f"{x}_step"), j * X_STEPS + 1 + step)

        def ones_for(dve, t, c, link):
            wait_apart(dve, (S(f"{t}_picked"), c + 1))
            pick_ones(link).then_inc(S(f"{t}_ones"), 1)

        def picked(pe, t, c):
            pe.wait_ge(S(f"{t}_ones"), c + 1)
            pe.wait_ge(S(f"{t}_rows"), c + 1)
            pick_rows().then_inc(S(f"{t}_picked"), 1)

        def rows_out(act, t, c):
            act.wait_ge(S(f"{t}_picked"), c + 2)
            act.wait_ge(S(f"{t}_xturn"), c + 1)
            copy_picked().then_inc(S(f"{t}_rows"), 1)

        def x_turn(pe, t, c):
            pe.wait_ge(S(f"{t}_rows"), c + 2)
            pe.wait_ge(S(f"{t}_xT"), c + 1)
            turn_rows().then_inc(S(f"{t}_xturn"), 1)

        def gate_up(pe, t, c, cu, u):
            pe.wait_ge(S(f"{t}_xT"), c + 2)
            pe.wait_ge(S(f"{t}_hid"), c + 1)
            pe.wait_ge(S(f"{t}_wgu{u}"), 32 * (cu + 1))
            gate_up_mms(u).then_inc(S(f"{t}_gu"), 1)

        def hid_turn(pe, t, c):
            pe.wait_ge(S(f"{t}_hid"), c + 2)
            turn_hidden().then_inc(S(f"{t}_hturn"), 1)

        def down(pe, t, c, cu, u):
            pe.wait_ge(S(f"{t}_hT"), c + 2)
            pe.wait_ge(S(f"{t}_y"), c + 1)
            pe.wait_ge(S(f"{t}_wd{u}"), 16 * (cu + 1))
            down_mms(u).then_inc(S(f"{t}_dn"), 1)

        def x_out(act, t, c):
            act.wait_ge(S(f"{t}_xturn"), c + 2)
            copy_x().then_inc(S(f"{t}_xT"), 1)

        def silu(act, t, c):
            act.wait_ge(S(f"{t}_gu"), c + 1)
            act.wait_ge(S(f"{t}_hid"), c + 1)
            nc.scalar.activation(act_g, bank[1][:, 0:FH], ACT.Silu).then_inc(S(f"{t}_g"), 1)

        def y_out(act, t, layer, c, cu, u, blk_n):
            act.wait_ge(S(f"{t}_dn"), c + 2)
            act.wait_ge(S(f"{t}_yout{u}"), 16 * (cu + 1))
            nc.scalar.activation(yb[:, u, :], bank[3][:, :], ACT.Copy).then_inc(S(f"{t}_y"), 1)
            act.wait_ge(S(f"{t}_y"), c + 2)
            store_y(act, t, layer, u, blk_n)

        def hidden(dve, t, c):
            dve.wait_ge(S(f"{t}_g"), c + 1)
            dve.wait_ge(S(f"{t}_hturn"), c + 1)
            nc.vector.tensor_tensor(hid, act_g, bank[1][:, FH:2 * FH], ALU.mult).then_inc(S(f"{t}_hid"), 1)

        def hid_out(dve, t, c):
            dve.wait_ge(S(f"{t}_hturn"), c + 2)
            nc.vector.tensor_copy(hidT, split(bank[2][:, 0:2 * P], 2, P)).then_inc(S(f"{t}_hT"), 1)

        def per_expert(eng, L, body, link=None):
            with eng.Fori(0, TRIPS) as it:
                if link:
                    link.enter(it, 2 * RING)
                for u in range(RING):
                    body(it * RING + u, it * RING + u + L * NE, it + L * uses(u), u, 2)
                if link:
                    link.leave(TRIPS)
            for u in range(NE - RING * TRIPS):
                e = RING * TRIPS + u
                body(e, e + L * NE, TRIPS + L * uses(u), u, NE - 1 - e)

        def uses(u):
            return TRIPS + (1 if u < NE - RING * TRIPS else 0)

        def fence(eng, t, L):
            for u in range(RING):
                eng.wait_ge(S(f"{t}_yout{u}"), 32 * uses(u) * (L + 1) + 16)

        def further(eng, t, layer, body, first=None, last=None, none=None):
            eng.wait_ge(S("m_routed"), past("m_routed") + layer + 1)
            n = eng.value_load(more_i[0:1, 0:1], min_val=0, max_val=NX)
            with eng.If(n > 0):
                fence(eng, t, layer)
                if first:
                    first()
                if body:
                    with eng.Fori(0, NX) as j:
                        with eng.If(n > j):
                            body(j)
                        with eng.Else():
                            eng.nop()
                        eng.nop()
                if last:
                    last(n)
            with eng.Else():
                if none:
                    none()
                else:
                    eng.nop()
            eng.nop()

        def moe_sp(sp, L, mixed, prev_norm, att):
            t, x = "m", f"mx{L}"
            rows_ready(sp, prev_norm, NT)
            sp.dma_start(gain[:], bcast_rows(ins["ffn_norm"][L, :], DM)).then_inc(S("gain_in"), 16)
            sp.dma_start(router_w[L][:, :, 0:MG], ins["moe_router_group"][L].rearrange("(k p) g -> p k g", p=P)).then_inc(S(f"{t}_rw"), 16)
            for g in range(MG):
                sp.dma_start(router_w[L][:, :, MG + g * EPG:MG + (g + 1) * EPG],
                             ins["moe_router_expert"][L, g].rearrange("(k p) e -> p k e", p=P)).then_inc(S(f"{t}_rw"), 16)
            att.done(sp)
            for u in range(2):
                weights(sp, t, L, u, u)
            sp.wait_ge(S(f"{mixed}_add"), past(f"{mixed}_add") + 2 * NT)
            gate_up_weights(sp, t, L, 2, 2)
            sp.wait_ge(S(f"{t}_routed"), past("m_routed") + L + 1)
            down_weights(sp, t, L, 2, 2)
            def next_weights(c, u):
                sp.wait_ge(S(f"{t}_gu"), c + 1 + L * NE)
                gate_up_weights(sp, t, L, c + RING, u)
                sp.wait_ge(S(f"{t}_dn"), c + 2 + L * NE)
                down_weights(sp, t, L, c + RING, u)
            with sp.Fori(0, TRIPS - 1) as it:
                for u in range(RING):
                    next_weights(it * RING + u, u)
            for u in range(NE - RING * TRIPS):
                next_weights(RING * (TRIPS - 1) + u, u)

            if L == 0:
                odd_early(sp)

            def body(j):
                sp.wait_ge(S(f"{x}_step"), j * X_STEPS + 1)
                e = sp.value_load(more_i[0:1, bass.ds(j + 1, 1)], min_val=0, max_val=NE - 1)
                weights(sp, x, L, e, 0)
            further(sp, t, L, body)

        def moe_pe(pe, L):
            t, x = "m", f"mx{L}"
            pe.sem_inc(S(f"{x}_step"), 1)
            if L == 0:
                pe.sem_inc(S(f"{t}_dn"), 1)
                pe.sem_inc(S(f"{t}_hturn"), 1)
                pe.sem_inc(S(f"{t}_xturn"), 1)
                pe.sem_inc(S(f"{t}_picked"), 1)

            def route(i):
                if i == 0:
                    pe.wait_ge(S(f"{t}_rw"), past("m_rw") + 16 * 5 * (L + 1))
                for half in range(2):
                    pe.wait_ge(S(f"turn_out{half}"), NT * TURN[f"m{L}n"] + i + 1)
                for k in range(KD):
                    mm = nc.tensor.matmul(bank[4][:, i * NR:(i + 1) * NR], hT[:, k, i * P:(i + 1) * P], router_w[L][:, k, :],
                                          start=(k == 0), stop=(k == KD - 1))
                if i == NT - 1:
                    mm.then_inc(S(f"{t}_rmm"), 1)
            turn_pe(pe, f"m{L}n", lambda i, k: rows[:, i, k * P:(k + 1) * P], lambda e, i: rows_ready(e, f"m{L}n", i + 1), route)
            pe.wait_ge(S(f"{t}_oh"), past("m_oh") + L + 1)
            for i in range(NT):
                for j in range(i + 1):
                    mm = nc.tensor.matmul(bank[5][:, i * NE:(i + 1) * NE], (tri_strict if j == i else onesb)[:], oh_sum[:, j, :],
                                          start=(j == 0), stop=(j == i))
            for j in range(NT):
                mm = nc.tensor.matmul(bank[6][:, 0:NE], onesb[:], oh_sum[:, j, :], start=(j == 0), stop=(j == NT - 1))
            mm.then_inc(S(f"{t}_cnt"), 1)
            picked(pe, t, L * NE)
            x_turn(pe, t, L * NE)
            picked(pe, t, L * NE + 1)

            def body(e, c, cu, u, after):
                gate_up(pe, t, c, cu, u)
                if after >= 1:
                    x_turn(pe, t, c + 1)
                if after >= 2:
                    picked(pe, t, c + 2)
                hid_turn(pe, t, c)
                down(pe, t, c, cu, u)
            per_expert(pe, L, body)

            def more(j):
                x_step(pe, x, j, X_ONES)
                pick_rows().then_inc(S(f"{x}_step"), 1)
                x_step(pe, x, j, X_ROWS)
                turn_rows().then_inc(S(f"{x}_step"), 1)
                x_step(pe, x, j, X_XT)
                pe.wait_ge(S(f"{x}_wgu0"), 32 * (j + 1))
                gate_up_mms(0).then_inc(S(f"{x}_step"), 1)
                x_step(pe, x, j, X_HID)
                turn_hidden().then_inc(S(f"{x}_step"), 1)
                x_step(pe, x, j, X_HT)
                pe.wait_ge(S(f"{x}_wd0"), 16 * (j + 1))
                down_mms(0).then_inc(S(f"{x}_step"), 1)
            further(pe, t, L, more)

        def moe_act(act, L, x_ready):
            t, x = "m", f"mx{L}"
            if L == 0:
                act.sem_inc(S(f"{t}_xT"), 1)
                act.sem_inc(S(f"{t}_y"), 1)
                act.sem_inc(S(f"{t}_rows"), 1)
                for u in range(RING):
                    act.sem_inc(S(f"{t}_yout{u}"), 16)
            norm_act(act, f"m{L}n", x_ready)
            for i in range(NT):
                turn_evac(act, f"m{L}n", hT, i, 0)
            act.wait_ge(S(f"{t}_d"), 2 * L + 1)
            nc.scalar.activation(small[:, 0:4, :], small[:, 0:4, :], ACT.Exp).then_inc(S(f"{t}_exp"), 1)
            act.wait_ge(S(f"{t}_d"), 2 * L + 2)
            nc.scalar.activation(small[:, 8, :], small[:, 8, :], ACT.Exp).then_inc(S(f"{t}_exp"), 1)
            rows_out(act, t, L * NE)
            x_out(act, t, L * NE)
            rows_out(act, t, L * NE + 1)

            def body(e, c, cu, u, after):
                silu(act, t, c)
                if after >= 1:
                    x_out(act, t, c + 1)
                if after >= 2:
                    rows_out(act, t, c + 2)
                y_out(act, t, L, c, cu * 2, u, e)
            per_expert(act, L, body)

            def more(j):
                x_step(act, x, j, X_PICKED)
                copy_picked().then_inc(S(f"{x}_step"), 1)
                x_step(act, x, j, X_TURN)
                copy_x().then_inc(S(f"{x}_step"), 1)
                x_step(act, x, j, X_GU)
                nc.scalar.activation(act_g, bank[1][:, 0:FH], ACT.Silu).then_inc(S(f"{x}_step"), 1)
                x_step(act, x, j, X_DN)
                nc.scalar.activation(yb[:, 0, :], bank[3][:, :], ACT.Copy).then_inc(S(f"{x}_y"), 1)
                act.wait_ge(S(f"{x}_y"), j + 1)
                store_y(act, x, L, 0, NE + j)
                act.wait_ge(S(f"{x}_yout0"), 32 * (j + 1))
                act.sem_inc(S(f"{x}_step"), 1)
            further(act, t, L, more, first=lambda: act.wait_ge(S(f"{x}_zero"), 16))

        def moe_pool(pool, L):
            t, x = "m", f"mx{L}"
            norm_pool(pool, f"m{L}n")
            pool.wait_ge(S(f"{t}_dest"), past("m_dest") + L + 1)
            def zero_rows():
                nc.gpsimd.memset(y_rows[:, 0, 0, :], 0.0).then_inc(S(f"{x}_zeroed"), 1)
                pool.wait_ge(S(f"{x}_zeroed"), 1)
                pool.dma_start(y_d[L][NE * CAP:, :].rearrange("(a p) c -> p a c", p=4 * NX),
                               y_rows[0:4 * NX, 0, 0:1, :].broadcast_to((4 * NX, CAP // 4, DM))).then_inc(S(f"{x}_zero"), 16)
                pool.wait_ge(S(f"{x}_zero"), 16)

            def fetch(n_rows):
                for i in range(NT):
                    for k in range(2):
                        nc.gpsimd.indirect_dma_start(
                            out=y_rows[:, k, i, :], out_offset=None, in_=y_d[L][0:n_rows, :],
                            in_offset=bass.IndirectOffsetOnAxis(ap=dest[:, k, i:i + 1], axis=0)).then_inc(S(f"{t}_yin{i}"), 16)

            def all_made(n):
                wait_apart(pool, (S(f"{x}_step"), n * X_STEPS + 1))
                fetch(ROWS)

            def none():
                fence(pool, t, L)
                fetch(NE * CAP)
            further(pool, t, L, None, zero_rows, all_made, none)

        def moe_dve(dve, L, link):
            t, x = "m", f"mx{L}"
            v_ = nc.vector
            if L == 0:
                dve.sem_inc(S(f"{t}_hid"), 1)
                dve.sem_inc(S(f"{t}_hT"), 1)
            norm_turns(dve, f"m{L}n")
            dve.wait_ge(S(f"{t}_rmm"), past("m_rmm") + L + 1)
            link(v_.tensor_copy(lgt, split(bank[4][:, 0:NT * NR], NT, NR)))
            gl_, el_ = lgt[:, :, 0:MG], lgt[:, :, MG:].rearrange("p i (g e) -> p i g e", g=MG)

            def bc(ap, n):
                return ap.unsqueeze(2).broadcast_to((P, NT, n))

            def first_max(vals, n, mx, onehot):
                link(v_.tensor_reduce(mx.unsqueeze(2), vals, AX.X, ALU.max))
                link(v_.tensor_tensor(eqs[:, :, 0:n], vals, bc(mx, n), ALU.is_equal))
                link(v_.scalar_tensor_tensor(cand[:, :, 0:n], eqs[:, :, 0:n], -100.0,
                                             iota32[:, 0:n].unsqueeze(1).broadcast_to((P, NT, n)), ALU.mult, ALU.add))
                link(v_.tensor_reduce(small[:, 11, :].unsqueeze(2), cand[:, :, 0:n], AX.X, ALU.min))
                link(v_.tensor_tensor(onehot, cand[:, :, 0:n], bc(small[:, 11, :], n), ALU.is_equal))

            first_max(gl_, MG, small[:, 4, :], oh_g)
            v_.tensor_tensor(small[:, 0:4, :].rearrange("p g i -> p i g"), gl_, bc(small[:, 4, :], MG), ALU.subtract).then_inc(S(f"{t}_d"), 1)
            pg = prod[:, 0:NT, :].rearrange("p i (e g) -> p i e g", g=MG)
            link(v_.tensor_tensor(pg, el_.rearrange("p i g e -> p i e g"), oh_g.unsqueeze(2).broadcast_to((P, NT, EPG, MG)), ALU.mult))
            link(v_.tensor_reduce(es.unsqueeze(3), pg, AX.X, ALU.add))
            first_max(es, EPG, small[:, 5, :], oh_e[:, 0])
            link(v_.scalar_tensor_tensor(es, oh_e[:, 0], NEG, es, ALU.mult, ALU.add))
            first_max(es, EPG, small[:, 6, :], oh_e[:, 1])
            v_.tensor_tensor(small[:, 8, :], small[:, 6, :], small[:, 5, :], ALU.subtract).then_inc(S(f"{t}_d"), 1)
            for k in range(2):
                ins_ = v_.tensor_tensor(oh[:, k].rearrange("p i (g e) -> p i g e", g=MG), oh_g.unsqueeze(3).broadcast_to((P, NT, MG, EPG)),
                                        oh_e[:, k].unsqueeze(2).broadcast_to((P, NT, MG, EPG)), ALU.mult)
                link(ins_)
            v_.tensor_tensor(oh_sum, oh[:, 0], oh[:, 1], ALU.add).then_inc(S(f"{t}_oh"), 1)
            dve.wait_ge(S(f"{t}_exp"), 2 * L + 1)
            link(v_.tensor_reduce(small[:, 7, :].unsqueeze(2), small[:, 0:4, :].rearrange("p g i -> p i g"), AX.X, ALU.add))
            dve.wait_ge(S(f"{t}_exp"), 2 * L + 2)
            link(v_.tensor_scalar(small[:, 9, :], small[:, 8, :], 1.0, None, ALU.add))
            link(v_.tensor_tensor(small[:, 9, :], small[:, 9, :], small[:, 7, :], ALU.mult))
            link(v_.reciprocal(weight[:, 0, :], small[:, 9, :]))
            link(v_.tensor_tensor(weight[:, 1, :], weight[:, 0, :], small[:, 8, :], ALU.mult))
            dve.wait_ge(S(f"{t}_cnt"), past("m_cnt") + L + 1)
            link.loose(v_.tensor_copy(before, split(bank[5][:, 0:NT * NE], NT, NE)))
            link.loose(v_.memset(onesr, 1.0))
            link(v_.tensor_copy(load, bank[6][:, 0:NE]))
            link(v_.tensor_tensor(cmp_, load.unsqueeze(2).broadcast_to((P, NE, MORE)), more_at[:].unsqueeze(1).broadcast_to((P, NE, MORE)), ALU.is_gt))
            link(v_.tensor_reduce(xn.unsqueeze(2), cmp_, AX.X, ALU.add))
            link(v_.tensor_tensor_scan(xend, onesr, xn, 0.0, ALU.mult, ALU.add))
            link(v_.tensor_tensor(xrow, xend, xn, ALU.subtract))
            link(v_.tensor_scalar(xrow, xrow, float(CAP), float(CAP * NE - CAP), ALU.mult, ALU.add))
            ohf = oh.rearrange("p k i e -> p (k i) e")
            for k in range(2):
                (link if k else link.loose)(v_.tensor_tensor(
                    split(prod.rearrange("p a b -> p (a b)"), 2, NT, NE)[:, k], oh[:, k], before, ALU.mult))
            link(v_.tensor_reduce(pos.unsqueeze(2), prod, AX.X, ALU.add))
            for tab, o in ((row_off[:], base), (xrow, xbase)):
                link(v_.tensor_tensor(prod, ohf, tab.unsqueeze(1).broadcast_to((P, 2 * NT, NE)), ALU.mult))
                link(v_.tensor_reduce(o.unsqueeze(2), prod, AX.X, ALU.add))
            link(v_.tensor_scalar(over, pos, float(CAP), None, ALU.is_ge))
            link(v_.tensor_tensor(xbase, xbase, base, ALU.subtract))
            link(v_.tensor_tensor(xbase, xbase, over, ALU.mult))
            link(v_.tensor_tensor(pos, pos, base, ALU.add))
            link(v_.tensor_tensor(dest_f[:], pos, xbase, ALU.add))
            link(v_.tensor_copy(blk_rows[:], first_rows[:]))
            v_.tensor_copy(dest[:].rearrange("p k i -> p (k i)"), dest_f[:]).then_inc(S(f"{t}_dest"), 1)
            dve.wait_ge(S(f"{t}_dest"), past("m_dest") + L + 1)
            for c in range(2):
                ones_for(dve, t, L * NE + c, link)
            link(v_.tensor_tensor(cmpx, xend.unsqueeze(1).broadcast_to((P, NX, NE)), iota32[:, 0:NX].unsqueeze(2).broadcast_to((P, NX, NE)), ALU.is_le))
            link(v_.tensor_reduce(more_f[:, 1:].unsqueeze(2), cmpx, AX.X, ALU.add))
            link(v_.tensor_copy(more_f[:, 0:1], xend[:, NE - 1:NE]))
            link(v_.tensor_scalar(more_i[:], more_f, float(NE - 1), None, ALU.min))
            dve.sem_inc(S(f"{t}_routed"), 1)

            def body(e, c, cu, u, after):
                if after >= 2:
                    ones_for(dve, t, c + 2, link)
                hidden(dve, t, c)
                hid_out(dve, t, c)
            per_expert(dve, L, body, link)
            more_link = Chain(dve, S(f"{x}_chain"))

            def more(j):
                dve.wait_ge(S(f"{x}_step"), j * X_STEPS + 1)
                more_link.enter(j, 2)
                pick_ones(more_link).then_inc(S(f"{x}_step"), 1)
                more_link.leave(NX)
                x_step(dve, x, j, X_G)
                nc.vector.tensor_tensor(hid, act_g, bank[1][:, FH:2 * FH], ALU.mult).then_inc(S(f"{x}_step"), 1)
                x_step(dve, x, j, X_HTURN)
                nc.vector.tensor_copy(hidT, split(bank[2][:, 0:2 * P], 2, P)).then_inc(S(f"{x}_step"), 1)
            further(dve, t, L, more)
            for i in range(NT):
                dve.wait_ge(S(f"{t}_yin{i}"), 32 * (L + 1))
                for k in range(2):
                    v_.scalar_tensor_tensor(xt[:, i, :], y_rows[:, k, i, :], weight[:, k, i:i + 1], xt[:, i, :],
                                            ALU.mult, ALU.add).then_inc(S(f"{t}_x"), 1)
                    dve.wait_ge(S(f"{t}_x"), 2 * NT * L + 2 * i + k + 1)
                if L == 0 and i >= 1:
                    norm_row(dve, "n2", i - 1)
            if L == 0:
                norm_row(dve, "n2", NT - 1)

        block = ctx.enter_context(nc.Block())

        @block.sync
        def _(sp):
            even_sp(sp)
            moe_sp(sp, 0, "eo", "n0", even_att)
            odd_sp(sp)
            moe_sp(sp, 1, "oo", "n2", odd_att)
            for i in range(NT):
                sp.wait_ge(S("m_x"), 2 * NT + 2 * i + 2)
                sp.dma_start(out[0, i * P:(i + 1) * P, :], xt[:, i, :]).then_inc(S("out"), 16)
            sp.wait_ge(S("out"), 16 * NT)

        @block.tensor
        def _(pe):
            even_pe(pe)
            moe_pe(pe, 0)
            odd_pe(pe)
            moe_pe(pe, 1)

        @block.scalar
        def _(act):
            even_act(act)
            moe_act(act, 0, lambda e, i: e.wait_ge(S("eo_add"), NT + i + 1))
            odd_act(act)
            moe_act(act, 1, lambda e, i: e.wait_ge(S("oo_add"), past("oo_add") + NT + i + 1))

        @block.gpsimd
        def _(pool):
            even_pool(pool)
            moe_pool(pool, 0)
            odd_pool(pool)
            moe_pool(pool, 1)

        @block.vector
        def _(dve):
            link = Chain(dve, S("dve_chain"))
            even_dve(dve, link)
            moe_dve(dve, 0, link)
            odd_dve(dve, link)
            moe_dve(dve, 1, link)


_INS = ['x', 'rel_bias', 'attn_norm', 'ffn_norm', 'even_w_in', 'even_conv_w', 'even_conv_b', 'even_dt_bias',
        'even_a_log', 'even_d_skip', 'even_ssm_norm', 'even_q_norm', 'even_k_norm', 'even_w_out', 'odd_w_in',
        'odd_q_norm', 'odd_kc_norm', 'odd_ks_norm', 'odd_kw_norm', 'odd_cmp_pos_k', 'odd_cmp_pos_v',
        'odd_cmp_k_w1', 'odd_cmp_k_w2', 'odd_cmp_v_w1', 'odd_cmp_v_w2', 'odd_w_out', 'moe_router_group',
        'moe_router_expert', 'moe_w_gate', 'moe_w_up', 'moe_w_down']


def kernel(**inputs):
    import concourse.bacc as bacc
    from concourse.bass_utils import run_bass_kernel_spmd

    nc = bacc.Bacc("TRN2", target_bir_lowering=False, num_devices=1)
    arrays, aps = {}, {}
    for name in _INS:
        arrays[f"in_{name}"] = np.ascontiguousarray(inputs[name])
    arrays["in_bucket_table"] = bucket_table()
    for name, a in arrays.items():
        aps[name[3:]] = nc.dram_tensor(name, a.shape, mybir.dt.from_np(a.dtype), kind="ExternalInput").ap()
    out = nc.dram_tensor("out_x", (1, SEQ, DM), F32, kind="ExternalOutput").ap()
    build(nc, aps, out)
    r = run_bass_kernel_spmd(nc, [arrays], core_ids=[0])
    return r.results[0]["out_x"]
```
